# Optimizing a Trainium2 kernel written in Bass

```python
import jax, jax.numpy as jnp
from jax import lax
import numpy as np

D_MODEL = 1024
BATCH = 1
SEQ = 1024
DEPTH = 2

CTX_LEN = 256
GRID_W = 64
D_MIX = D_MODEL
N_GROUPS = 4
GROUP_W = D_MIX // N_GROUPS
HEAD_DIM = 64
GROUP_HEADS = GROUP_W // HEAD_DIM
NORM_EPS = 1e-6

CONV_W = GROUP_W
MLA_HEADS = GROUP_HEADS
MLA_NOPE = HEAD_DIM
MLA_ROPE = HEAD_DIM // 2
MLA_QK = MLA_NOPE + MLA_ROPE
MLA_V = HEAD_DIM
MLA_W = MLA_HEADS * MLA_V
KV_RANK = D_MODEL // 8
ROPE_BASE = 10000.0
Q_BLOCK = 128
RWKV_HEADS = GROUP_HEADS
RWKV_N = HEAD_DIM
RWKV_W = GROUP_W
DECAY_LORA = 64
ICLR_LORA = 64
GATE_LORA = 128
RWKV_GN_EPS = 64e-5
RET_HEADS = GROUP_HEADS
RET_DK = HEAD_DIM
RET_DV = HEAD_DIM
RET_W = GROUP_W
RET_CHUNK = 128
RET_THETA_BASE = 10000.0
N_EXP = 16
CAP_FACTOR = 2
EXP_FF = D_MODEL

COLS_CONV = 3 * CONV_W
COLS_MLA = MLA_HEADS * MLA_QK + KV_RANK + MLA_ROPE
COLS_RWKV = 3 * RWKV_W + DECAY_LORA + ICLR_LORA + GATE_LORA
COLS_RET = 4 * RET_W
IN_COLS = COLS_CONV + COLS_MLA + COLS_RWKV + COLS_RET
MIX_SPLITS = (COLS_CONV, COLS_CONV + COLS_MLA, COLS_CONV + COLS_MLA + COLS_RWKV)
MLA_SPLITS = (MLA_HEADS * MLA_NOPE, MLA_HEADS * MLA_QK, MLA_HEADS * MLA_QK + KV_RANK)
RWKV_SPLITS = (RWKV_W, 2 * RWKV_W, 3 * RWKV_W, 3 * RWKV_W + DECAY_LORA, 3 * RWKV_W + DECAY_LORA + ICLR_LORA)

kernel_name = 'hybrid_diffusion_parallel_groups_ec_moe'

def rms_norm(t, g):
    tf = t.astype(jnp.float32)
    y = tf * lax.rsqrt(jnp.mean(tf * tf, axis=-1, keepdims=True) + NORM_EPS)
    return y.astype(t.dtype) * g

def modulate(h, shift, scale):
    return h * (1.0 + scale) + shift

def split_heads(t, n):
    return t.reshape(t.shape[:-1] + (n, t.shape[-1] // n))

def merge_heads(t):
    return t.reshape(t.shape[:-2] + (-1,))

def shift_prev(t):
    return jnp.pad(t, ((0, 0), (1, 0), (0, 0)))[:, :-1]

def shift_next(t):
    return jnp.pad(t, ((0, 0), (0, 1), (0, 0)))[:, 1:]

def cos_sin(ang):
    return jnp.cos(ang)[:, None, :], jnp.sin(ang)[:, None, :]

def rotate(t, cos, sin):
    t1, t2 = jnp.split(t, 2, axis=-1)
    return jnp.concatenate([t1 * cos - t2 * sin, t1 * sin + t2 * cos], axis=-1)

def short_conv_mixer(z, conv_w, g_out):
    b, cg, h = jnp.split(z, 3, axis=-1)
    u = cg * h
    y = conv_w[0] * shift_prev(u) + conv_w[1] * u + conv_w[2] * shift_next(u)
    return rms_norm(b * y, g_out)

def rope_2d_tail(t, rot_row, rot_col):
    nope, rr, rc = jnp.split(t, [MLA_NOPE, MLA_NOPE + MLA_ROPE // 2], axis=-1)
    return jnp.concatenate([nope, rotate(rr, *rot_row), rotate(rc, *rot_col)], axis=-1)

def mla_queries(z, g_q):
    q_nope, q_rope, _, _ = jnp.split(z, MLA_SPLITS, axis=-1)
    q = jnp.concatenate([split_heads(q_nope, MLA_HEADS), split_heads(q_rope, MLA_HEADS)], axis=-1)
    return rms_norm(q, g_q)

def mla_keys_values(z, g_kv, w_uk, w_uv, g_k):
    _, _, ckv, k_rope = jnp.split(z, MLA_SPLITS, axis=-1)
    ckv = rms_norm(ckv, g_kv)
    k_nope = split_heads(ckv @ w_uk, MLA_HEADS)
    v = split_heads(ckv @ w_uv, MLA_HEADS)
    k_rope = jnp.broadcast_to(k_rope[:, :, None, :], k_nope.shape[:-1] + (MLA_ROPE,))
    k = rms_norm(jnp.concatenate([k_nope, k_rope], axis=-1), g_k)
    return k, v

def softmax_attend(q, k, v):
    s = jnp.einsum('bqhd,bkhd->bhqk', q, k).astype(jnp.float32) * (MLA_QK ** -0.5)
    p = jax.nn.softmax(s, axis=-1).astype(v.dtype)
    return jnp.einsum('bhqk,bkhd->bqhd', p, v)

def blocked_attend(q, k, v):
    B, L, H, dq = q.shape
    qb = q.reshape(B, L // Q_BLOCK, Q_BLOCK, H, dq).swapaxes(0, 1)
    out = lax.map(lambda blk: softmax_attend(blk, k, v), qb)
    return out.swapaxes(0, 1).reshape(B, L, H, -1)

def mla_mixer(z_x, z_c, g_kv, w_uk, w_uv, g_q, g_k, g_out, rot_row, rot_col, need_ctx):
    k_c, v_c = mla_keys_values(z_c, g_kv, w_uk, w_uv, g_k)
    k_x, v_x = mla_keys_values(z_x, g_kv, w_uk, w_uv, g_k)
    k_x = rope_2d_tail(k_x, rot_row, rot_col)
    q_x = rope_2d_tail(mla_queries(z_x, g_q), rot_row, rot_col)
    k_all = jnp.concatenate([k_c, k_x], axis=1)
    v_all = jnp.concatenate([v_c, v_x], axis=1)
    y_x = rms_norm(merge_heads(blocked_attend(q_x, k_all, v_all)), g_out)
    y_c = rms_norm(merge_heads(softmax_attend(mla_queries(z_c, g_q), k_c, v_c)), g_out) if need_ctx else None
    return y_x, y_c

def rwkv_project(z, mu, w0, w2, a0, a2, k_k, k_a):
    z = z.astype(jnp.float32)
    z = z + mu * (0.5 * (shift_prev(z) + shift_next(z)) - z)
    r, k, v, wl, al, gl = jnp.split(z, RWKV_SPLITS, axis=-1)
    kk = split_heads(k * k_k, RWKV_HEADS)
    kk = kk * lax.rsqrt(jnp.sum(kk * kk, axis=-1, keepdims=True) + 1e-12)
    dirs = []
    for d in range(2):
        log_w = -jax.nn.softplus(-(w0[d] + jnp.tanh(wl) @ w2[d])) - 0.5
        w = jnp.exp(-jnp.exp(log_w))
        a = jax.nn.sigmoid(a0[d] + al @ a2[d])
        kt = k * (1.0 + (a - 1.0) * k_a)
        dirs.append((split_heads(w, RWKV_HEADS), split_heads(a, RWKV_HEADS), split_heads(kt, RWKV_HEADS)))
    return split_heads(r, RWKV_HEADS), split_heads(v, RWKV_HEADS), kk, gl, dirs

def wkv_scan(state, w, a, k, v, kk, r, reverse, emit):
    xs = (w, a, k, v, kk) + ((r,) if emit else ())
    xs = tuple(jnp.moveaxis(t, 1, 0) for t in xs)

    def step(s, inp):
        w_t, a_t, k_t, v_t, kk_t = inp[:5]
        s = (s * w_t[:, :, None, :]
             - jnp.einsum('bhvk,bhk->bhv', s, kk_t)[..., None] * (kk_t * a_t)[:, :, None, :]
             + v_t[..., None] * k_t[:, :, None, :])
        y = jnp.einsum('bhvk,bhk->bhv', s, inp[5]) if emit else None
        return s, y

    state, ys = lax.scan(step, state, xs, reverse=reverse)
    return state, (jnp.moveaxis(ys, 0, 1) if emit else None)

def rwkv_out(y, r, v, k_sum, gl, g2, r_k, g_ln):
    mean = jnp.mean(y, axis=-1, keepdims=True)
    var = jnp.mean(jnp.square(y - mean), axis=-1, keepdims=True)
    y = (y - mean) * lax.rsqrt(var + RWKV_GN_EPS) * g_ln.reshape(RWKV_HEADS, RWKV_N)
    y = y + jnp.sum(r * k_sum * r_k.reshape(RWKV_HEADS, RWKV_N), axis=-1, keepdims=True) * v
    return merge_heads(y) * (jax.nn.sigmoid(gl) @ g2)

def rwkv_mixer(z_x, z_c, mu, w0, w2, a0, a2, g2, k_k, k_a, r_k, g_ln, need_ctx):
    s0 = jnp.zeros((z_x.shape[0], RWKV_HEADS, RWKV_N, RWKV_N), jnp.float32)
    rx, vx, kkx, glx, dx = rwkv_project(z_x, mu, w0, w2, a0, a2, k_k, k_a)
    rc, vc, kkc, glc, dc = rwkv_project(z_c, mu, w0, w2, a0, a2, k_k, k_a)
    s_fw, yc_fw = wkv_scan(s0, *dc[0], vc, kkc, rc, False, need_ctx)
    s_bw, yc_bw = wkv_scan(s0, *dc[1], vc, kkc, rc, True, need_ctx)
    _, yx_fw = wkv_scan(s_fw, *dx[0], vx, kkx, rx, False, True)
    _, yx_bw = wkv_scan(s_bw, *dx[1], vx, kkx, rx, True, True)
    y_x = rwkv_out(yx_fw + yx_bw, rx, vx, dx[0][2] + dx[1][2], glx, g2, r_k, g_ln)
    y_c = rwkv_out(yc_fw + yc_bw, rc, vc, dc[0][2] + dc[1][2], glc, g2, r_k, g_ln) if need_ctx else None
    return y_x, y_c

def ret_project(z, rot):
    q, k, v, g = jnp.split(z.astype(jnp.float32), 4, axis=-1)
    q = split_heads(q, RET_HEADS) * (RET_DK ** -0.5)
    k = split_heads(k, RET_HEADS)
    if rot is not None:
        q = rotate(q, *rot)
        k = rotate(k, *rot)
    return q, k, split_heads(v, RET_HEADS), g

def ret_chunkwise(q, k, v, r0, log_gamma, strict, emit):
    B, L, H, dk = k.shape
    nc = L // RET_CHUNK
    kc = k.reshape(B, nc, RET_CHUNK, H, dk)
    vc = v.reshape(B, nc, RET_CHUNK, H, -1)
    j = jnp.arange(RET_CHUNK, dtype=jnp.float32)
    zeta = jnp.exp((RET_CHUNK - 1 - j)[:, None] * log_gamma[None, :])
    d_r = jnp.einsum('bnchk,bnchv->bnhkv', kc * zeta[None, None, :, :, None], vc)
    dec_c = jnp.exp(RET_CHUNK * log_gamma)[None, :, None, None]

    def step(r_state, dr_i):
        return r_state * dec_c + dr_i, (r_state if emit else None)

    r_fin, r_prev = lax.scan(step, r0, d_r.swapaxes(0, 1))
    if not emit:
        return None, r_fin
    qc = q.reshape(B, nc, RET_CHUNK, H, dk)
    xi = jnp.exp((j + 1.0)[:, None] * log_gamma[None, :])
    cross = jnp.einsum('bnchk,nbhkv->bnchv', qc * xi[None, None, :, :, None], r_prev)
    diff = j[:, None] - j[None, :]
    mask = diff > 0 if strict else diff >= 0
    dmat = jnp.where(mask[None], jnp.exp(jnp.where(mask, diff, 0.0)[None] * log_gamma[:, None, None]), 0.0)
    s = jnp.einsum('bnqhd,bnkhd->bnhqk', qc, kc) * dmat[None, None]
    inner = jnp.einsum('bnhqk,bnkhv->bnqhv', s, vc)
    return (inner + cross).reshape(B, L, H, -1), r_fin

def ret_out(y, g, g_norm):
    y = rms_norm(y, g_norm.reshape(RET_HEADS, RET_DV))
    return jax.nn.silu(g) * merge_heads(y)

def retention_mixer(z_x, z_c, g_norm, rot, log_gamma, need_ctx):
    r0 = jnp.zeros((z_x.shape[0], RET_HEADS, RET_DK, RET_DV), jnp.float32)
    flip = lambda t: jnp.flip(t, axis=1)
    qx, kx, vx, gx = ret_project(z_x, rot)
    qc, kc, vc, gc = ret_project(z_c, None)
    yc_fw, r_fw = ret_chunkwise(qc, kc, vc, r0, log_gamma, False, need_ctx)
    yc_bw, r_bw = ret_chunkwise(flip(qc), flip(kc), flip(vc), r0, log_gamma, True, need_ctx)
    yx_fw, _ = ret_chunkwise(qx, kx, vx, r_fw, log_gamma, False, True)
    yx_bw, _ = ret_chunkwise(flip(qx), flip(kx), flip(vx), r_bw, log_gamma, True, True)
    y_x = ret_out(yx_fw + flip(yx_bw), gx, g_norm)
    y_c = ret_out(yc_fw + flip(yc_bw), gc, g_norm) if need_ctx else None
    return y_x, y_c

def ec_ffn(h, w_router, b_router, w_gate, w_up, w_down):
    n_tok = h.shape[1]
    cap = CAP_FACTOR * n_tok // N_EXP

    def route_set(hs):
        aff = jax.nn.softmax((hs @ w_router + b_router).astype(jnp.float32), axis=-1)
        gate, idx = lax.top_k(aff.T, cap)
        xe = hs[idx]
        hid = jax.nn.silu(jnp.einsum('ecd,edf->ecf', xe, w_gate)) * jnp.einsum('ecd,edf->ecf', xe, w_up)
        ye = jnp.einsum('ecf,efd->ecd', hid, w_down) * gate[..., None].astype(hid.dtype)
        return jnp.zeros(hs.shape, ye.dtype).at[idx.reshape(-1)].add(ye.reshape(-1, hs.shape[-1]))

    return jax.vmap(route_set)(h)

def setup_inputs(seed: int = 0) -> dict:
    key = jax.random.key(seed)
    ks = iter(jax.random.split(key, 40))
    f32 = jnp.float32
    D = D_MODEL

    def nrm(shape, scale):
        return scale * jax.random.normal(next(ks), shape, f32)

    def gain(shape):
        return 1.0 + nrm(shape, 0.02)

    return {
        'x': nrm((BATCH, SEQ, D), 1.0),
        'c': nrm((BATCH, D), 1.0),
        'ctx': nrm((BATCH, CTX_LEN, D), 1.0),
        'c_ctx': nrm((D,), 1.0),
        'w_ada': nrm((DEPTH, D, 6 * D), 0.5 * D ** -0.5),
        'b_ada': nrm((DEPTH, 6 * D), 0.02),
        'g_norm1': gain((DEPTH, D)),
        'g_norm2': gain((DEPTH, D)),
        'w_in': nrm((DEPTH, D, IN_COLS), D ** -0.5),
        'w_out': nrm((DEPTH, D_MIX, D), D_MIX ** -0.5),
        'conv_w': nrm((DEPTH, 3, CONV_W), 0.5),
        'g_out_conv': gain((DEPTH, CONV_W)),
        'g_kv_norm': gain((DEPTH, KV_RANK)),
        'w_uk': nrm((DEPTH, KV_RANK, MLA_HEADS * MLA_NOPE), KV_RANK ** -0.5),
        'w_uv': nrm((DEPTH, KV_RANK, MLA_HEADS * MLA_V), KV_RANK ** -0.5),
        'g_q_norm': gain((DEPTH, MLA_QK)),
        'g_k_norm': gain((DEPTH, MLA_QK)),
        'g_out_mla': gain((DEPTH, MLA_W)),
        'rwkv_mu': 0.5 + nrm((DEPTH, COLS_RWKV), 0.1),
        'rwkv_w0': jax.random.uniform(next(ks), (DEPTH, 2, RWKV_W), f32, -6.0, -1.0),
        'rwkv_w2': nrm((DEPTH, 2, DECAY_LORA, RWKV_W), 0.1),
        'rwkv_a0': nrm((DEPTH, 2, RWKV_W), 0.1),
        'rwkv_a2': nrm((DEPTH, 2, ICLR_LORA, RWKV_W), 0.1),
        'rwkv_g2': nrm((DEPTH, GATE_LORA, RWKV_W), GATE_LORA ** -0.5),
        'rwkv_k_k': 0.85 + nrm((DEPTH, RWKV_W), 0.05),
        'rwkv_k_a': 1.0 + nrm((DEPTH, RWKV_W), 0.05),
        'rwkv_r_k': nrm((DEPTH, RWKV_W), 0.1),
        'g_ln_x': gain((DEPTH, RWKV_W)),
        'g_ret_norm': gain((DEPTH, RET_W)),
        'w_router': nrm((DEPTH, D, N_EXP), D ** -0.5),
        'b_router': nrm((DEPTH, N_EXP), 0.01),
        'w_gate': nrm((DEPTH, N_EXP, D, EXP_FF), D ** -0.5),
        'w_up': nrm((DEPTH, N_EXP, D, EXP_FF), D ** -0.5),
        'w_down': nrm((DEPTH, N_EXP, EXP_FF, D), EXP_FF ** -0.5),
    }

def reference(x, c, ctx, c_ctx, w_ada, b_ada, g_norm1, g_norm2, w_in, w_out, conv_w, g_out_conv,
              g_kv_norm, w_uk, w_uv, g_q_norm, g_k_norm, g_out_mla, rwkv_mu, rwkv_w0, rwkv_w2,
              rwkv_a0, rwkv_a2, rwkv_g2, rwkv_k_k, rwkv_k_a, rwkv_r_k, g_ln_x, g_ret_norm,
              w_router, b_router, w_gate, w_up, w_down):
    f32 = jnp.float32
    L = x.shape[1]
    ROWS = L // GRID_W
    row = jnp.repeat(jnp.arange(ROWS, dtype=f32), GRID_W)
    col = jnp.tile(jnp.arange(GRID_W, dtype=f32), ROWS)
    axis_dim = MLA_ROPE // 2
    inv_axis = ROPE_BASE ** (-jnp.arange(0, axis_dim, 2, dtype=f32) / axis_dim)
    rot_row = cos_sin(row[:, None] * inv_axis[None, :])
    rot_col = cos_sin(col[:, None] * inv_axis[None, :])
    theta = 1.0 / (RET_THETA_BASE ** jnp.linspace(0.0, 1.0, RET_DK // 2, dtype=f32))
    rot_ret = cos_sin(jnp.arange(L, dtype=f32)[:, None] * theta[None, :])
    log_gamma = jnp.log1p(-jnp.exp2(-5.0 - jnp.arange(RET_HEADS, dtype=f32)))

    xc = ctx
    for l in range(DEPTH):
        need_ctx = l < DEPTH - 1
        mod_x = (jax.nn.silu(c) @ w_ada[l] + b_ada[l])[:, None, :]
        mod_c = jax.nn.silu(c_ctx) @ w_ada[l] + b_ada[l]
        sh1, sc1, ga1, sh2, sc2, ga2 = jnp.split(mod_x, 6, axis=-1)
        csh1, csc1, cga1, csh2, csc2, cga2 = jnp.split(mod_c, 6, axis=-1)

        z_x = modulate(rms_norm(x, g_norm1[l]), sh1, sc1) @ w_in[l]
        z_c = modulate(rms_norm(xc, g_norm1[l]), csh1, csc1) @ w_in[l]
        zx_conv, zx_mla, zx_rwkv, zx_ret = jnp.split(z_x, MIX_SPLITS, axis=-1)
        zc_conv, zc_mla, zc_rwkv, zc_ret = jnp.split(z_c, MIX_SPLITS, axis=-1)
        y_mla_x, y_mla_c = mla_mixer(zx_mla, zc_mla, g_kv_norm[l], w_uk[l], w_uv[l], g_q_norm[l],
                                     g_k_norm[l], g_out_mla[l], rot_row, rot_col, need_ctx)
        y_rwkv_x, y_rwkv_c = rwkv_mixer(zx_rwkv, zc_rwkv, rwkv_mu[l], rwkv_w0[l], rwkv_w2[l], rwkv_a0[l],
                                        rwkv_a2[l], rwkv_g2[l], rwkv_k_k[l], rwkv_k_a[l], rwkv_r_k[l],
                                        g_ln_x[l], need_ctx)
        y_ret_x, y_ret_c = retention_mixer(zx_ret, zc_ret, g_ret_norm[l], rot_ret, log_gamma, need_ctx)
        y_x = jnp.concatenate([short_conv_mixer(zx_conv, conv_w[l], g_out_conv[l]),
                               y_mla_x, y_rwkv_x, y_ret_x], axis=-1).astype(x.dtype)
        x = x + ga1 * (y_x @ w_out[l])
        if need_ctx:
            y_c = jnp.concatenate([short_conv_mixer(zc_conv, conv_w[l], g_out_conv[l]),
                                   y_mla_c, y_rwkv_c, y_ret_c], axis=-1).astype(xc.dtype)
            xc = xc + cga1 * (y_c @ w_out[l])

        h_x = modulate(rms_norm(x, g_norm2[l]), sh2, sc2)
        x = x + ga2 * ec_ffn(h_x, w_router[l], b_router[l], w_gate[l], w_up[l], w_down[l])
        if need_ctx:
            h_c = modulate(rms_norm(xc, g_norm2[l]), csh2, csc2)
            xc = xc + cga2 * ec_ffn(h_c, w_router[l], b_router[l], w_gate[l], w_up[l], w_down[l])
    return x


_drawn_inputs = setup_inputs


def setup_inputs(seed=0):
    import zlib

    import numpy as np

    out = dict(_drawn_inputs(seed))
    spreads = {}
    factors = {'g_norm1': 4.981,
     'g_norm2': 6.345,
     'g_out_conv': 8.0,
     'g_kv_norm': 8.0,
     'g_q_norm': 8.0,
     'g_k_norm': 8.0,
     'g_out_mla': 8.0,
     'rwkv_w2': 4.907,
     'rwkv_a0': 8.0,
     'g_ln_x': 8.0,
     'g_ret_norm': 8.0,
     'b_router': 8.0}
    for name, (base, spread) in spreads.items():
        noise = np.random.default_rng([zlib.crc32(name.encode()), seed]).standard_normal(out[name].shape)
        drawn = base * np.exp(spread * noise) if base else spread * noise
        out[name] = __import__('jax').numpy.asarray(drawn.astype(out[name].dtype))
    for name, factor in factors.items():
        out[name] = (out[name] * factor).astype(out[name].dtype)
    return out
```

```python
from contextlib import ExitStack

import numpy as np

import concourse.bass as bass
from concourse import mybir

ALU = mybir.AluOpType
ACT = mybir.ActivationFunctionType
F32 = mybir.dt.float32
I32 = mybir.dt.int32
U32 = mybir.dt.uint32
AX_X = mybir.AxisListType.X

P = 128
D = 1024
KT = D // P
CTX, SEQ = 256, 1024
T = CTX + SEQ
NT = T // P
NCT = CTX // P
DEPTH = 2
GRID_W = 64
EPS = 1e-6
GW = 256
HD = 64
H = 4
QK = 96
C_MLA, C_RWKV, C_RET = 768, 1312, 2336
W_MLA, W_RET = 544, 1024
NE, FF = 16, 1024
CAPX, CAPC = 2 * SEQ // NE, 2 * CTX // NE
CH = 64
LEVELS = 6
LWC = -float(np.exp(-0.5))
GN_EPS = 64e-5
SPANS = [(0, 256), (256, 512), (768, 512)]


class Signal:

    def __init__(self, ctx, nc, name):
        self.sem = ctx.enter_context(nc.semaphore(name))
        self.base = 0
        self.made = 0

    def up(self, n=1):
        self.made += n
        return self.sem, n

    def at(self, k):
        return self.sem, self.base + k


class Signals:

    def __init__(self, ctx, nc):
        self.ctx, self.nc, self.by = ctx, nc, {}

    def __call__(self, name):
        if name not in self.by:
            self.by[name] = Signal(self.ctx, self.nc, name)
        return self.by[name]

    def settle(self):
        for s in self.by.values():
            s.base = s.made


def linker(eng, sig):
    def link(ins):
        ins.then_inc(*sig.up())
        eng.wait_ge(sig.sem, sig.made)
    return link


CONSTS = ["ident", "ones", "blk", "masks", "nlev", "reset", "dmat", "xi", "zeta", "gdec", "rope_m", "rope_r"]


def constants():
    f = np.float32
    i = np.arange(P)
    same = (i[:, None] // CH) == (i[None, :] // CH)
    strict = same & (i[:, None] < i[None, :])
    incl = same & (i[:, None] <= i[None, :])
    masks = np.zeros((P, 2, 4, P), f)
    masks[:, 0] = np.stack([strict, incl, strict, incl], 1)
    masks[:, 1] = np.stack([strict.T, incl.T, strict.T, incl.T], 1)
    nlev = np.zeros((P, 2, LEVELS, P), f)
    for s in range(LEVELS):
        w = 1 << s
        m = ((i[None, :] // w) % 2 == 1) & ((i[:, None] // w) == (i[None, :] // w) - 1)
        nlev[:, 0, s] = -m.astype(f)
        nlev[:, 1, s] = -m.T.astype(f)
    blk = np.zeros((P, P), f)
    blk[:HD, :HD] = 1
    blk[HD:, HD:] = 1
    lg = np.log1p(-np.exp2(-5.0 - np.arange(H)))
    dist = np.abs(i[:, None] - i[None, :])
    sc = HD ** -0.5
    dmat = (np.exp(dist[:, None, :] * lg[None, :, None]) * sc).astype(f)
    head = np.arange(GW) // HD
    xi = np.zeros((P, 2, 2, P), f)
    gdec = np.zeros((P, 2), f)
    for p in range(2):
        g = lg[head[p * P:(p + 1) * P]]
        xi[:, p, 0] = np.exp(g[:, None] * (i[None, :] + 1)) * sc
        xi[:, p, 1] = np.exp(g[:, None] * (P - i[None, :])) * sc
        gdec[:, p] = np.exp(g * P)
    zeta = np.zeros((P, 2, GW), f)
    zeta[:, 0] = np.exp((P - 1 - i)[:, None] * lg[head][None, :])
    zeta[:, 1] = np.exp(i[:, None] * lg[head][None, :])
    reset = np.ones((P, T), f)
    reset[:, ::CH] = 0
    tok = np.arange(SEQ, dtype=f)
    ax = 10000.0 ** (-np.arange(0, 16, 2, dtype=f) / f(16))
    pos = [np.floor(tok / GRID_W), tok % GRID_W]
    rm = np.zeros((SEQ, 2, 2, 2, 8), f)
    for a in range(2):
        ang = (pos[a].astype(f)[:, None] * ax.astype(f)[None, :]).astype(f)
        rm[:, 0, a, :] = np.cos(ang)[:, None]
        rm[:, 1, a, 0] = -np.sin(ang)
        rm[:, 1, a, 1] = np.sin(ang)
    th = (1.0 / (10000.0 ** np.linspace(0.0, 1.0, HD // 2, dtype=f))).astype(f)
    ang = (tok[:, None] * th[None, :]).astype(f)
    rr = np.zeros((SEQ, 2, 2, HD // 2), f)
    rr[:, 0] = np.cos(ang)[:, None]
    rr[:, 1, 0] = -np.sin(ang)
    rr[:, 1, 1] = np.sin(ang)
    out = dict(ident=np.eye(P, dtype=f), ones=np.ones((P, P), f), blk=blk, masks=masks.reshape(P, -1),
               nlev=nlev.reshape(P, -1), reset=reset, dmat=dmat.reshape(P, -1), xi=xi.reshape(P, -1),
               zeta=zeta.reshape(P, -1), gdec=gdec, rope_m=rm.reshape(SEQ, -1), rope_r=rr.reshape(SEQ, -1))
    return {k: np.ascontiguousarray(v.astype(f)) for k, v in out.items()}


class Bufs:

    def __init__(self, nc, ctx, stage):
        self.nc, self.ctx, self.stage = nc, ctx, stage

    def __call__(self, name, shape, dt=F32):
        return self.ctx.enter_context(self.nc.sbuf_tensor(f"{self.stage}_{name}", shape, dt))


def col(v, n):
    return v.rearrange("(k p) -> p k", k=n)


def row(v):
    return v.partition_broadcast(P)


def stage_modulation(nc, g, I):
    sg, ps = g.sg, g.ps
    NCH = 6 * D // 512
    RW = 4
    with ExitStack() as cx:
        sb = Bufs(nc, cx, "mod")
        cc = sb("cc", [P, KT, 2])
        sc = sb("sc", [P, KT, 2])
        wa = sb("wa", [P, RW, KT, 512])
        ba = sb("ba", [2, DEPTH, 6 * D])
        mo = sb("mo", [2, 6 * D])
        w_in, c_in = [sg(f"w_slot{i}") for i in range(RW)], sg("small_in")
        silu_done, mm, used, stored = sg("silu_done"), sg("mod_mm"), sg("mod_used"), sg("stored")
        jobs = [(l, n) for l in range(DEPTH) for n in range(NCH)]
        with nc.Block() as block:
            @block.sync
            def _(sp):
                with nc.allow_non_contiguous_dma(reason="vectors into columns"):
                    sp.dma_start(cc[:, :, 0], col(I["c"][0], KT)).then_inc(*c_in.up(16))
                    sp.dma_start(cc[:, :, 1], col(I["c_ctx"], KT)).then_inc(*c_in.up(16))
                for l in range(DEPTH):
                    sp.dma_start(ba[:, l, :], I["b_ada"][l].partition_broadcast(2)).then_inc(*c_in.up(16))
                for j, (l, n) in enumerate(jobs):
                    if j >= RW:
                        sp.wait_ge(*mm.at(j - RW + 1))
                    sp.dma_start(wa[:, j % RW], I["w_ada"][l].rearrange("(k p) f -> p k f", p=P)
                                 [:, :, n * 512:(n + 1) * 512]).then_inc(*w_in[j % RW].up(16))

            @block.scalar
            def _(act):
                act.wait_ge(*c_in.at(16 * (2 + DEPTH)))
                nc.scalar.activation(sc[:], cc[:], ACT.Silu).then_inc(*silu_done.up())
                for l in range(DEPTH):
                    act.wait_ge(*used.at((l + 1) * NCH))
                    act.dma_start(g.mod[l], mo[:]).then_inc(*stored.up(16))
                act.wait_ge(*stored.at(16 * DEPTH))

            @block.tensor
            def _(pe):
                pe.wait_ge(*silu_done.at(1))
                for j, (l, n) in enumerate(jobs):
                    pe.wait_ge(*w_in[j % RW].at(16 * (j // RW + 1)))
                    if j >= 4:
                        pe.wait_ge(*used.at(j - 3))
                    for k in range(KT):
                        ins = nc.tensor.matmul(ps[0:2, j % 4, :], sc[:, k, :], wa[:, j % RW, k, :],
                                               start=(k == 0), stop=(k == KT - 1))
                    ins.then_inc(*mm.up())

            @block.vector
            def _(dve):
                dve.wait_ge(*c_in.at(16 * (2 + DEPTH)))
                for j, (l, n) in enumerate(jobs):
                    dve.wait_ge(*mm.at(j + 1))
                    if j == NCH:
                        dve.wait_ge(*stored.at(16))
                    s = slice(n * 512, (n + 1) * 512)
                    nc.vector.tensor_tensor(mo[:, s], ps[0:2, j % 4, :], ba[:, l, s], ALU.add).then_inc(*used.up())
        sg.settle()


def stage_norm1(nc, g, I, l):
    sg, ps, hT = g.sg, g.ps, g.hT
    with ExitStack() as cx:
        sb = Bufs(nc, cx, f"n{l}")
        xb = sb("xb", [P, 3, D])
        xn = sb("xn", [P, 2, D])
        junk = sb("junk", [P, D])
        ss = sb("ss", [P, NT])
        rs = sb("rs", [P, NT])
        mc = sb("mc", [P, 2, 2, KT])
        gn = sb("gn", [P, KT])
        G = sb("G", [P, 2, KT])
        x_in, small, sq, normed = [sg(f"w_slot{i}") for i in range(3)], sg("small_in"), sg("sq_done"), sg("normed")
        tr, ev_a, ev_d, coef, chain = sg("transposed"), sg("evac_a"), sg("evac_d"), sg("coef"), sg("dve_chain")
        with nc.Block() as block:
            @block.sync
            def _(sp):
                with nc.allow_non_contiguous_dma(reason="vectors into columns"):
                    for s in range(2):
                        for w in range(2):
                            sp.dma_start(mc[:, s, w], col(g.mod[l, s, w * D:(w + 1) * D], KT)).then_inc(*small.up(16))
                    sp.dma_start(gn[:], col(I["g_norm1"][l], KT)).then_inc(*small.up(16))
                for t in range(NT):
                    if t >= 3:
                        sp.wait_ge(*normed.at(t - 2))
                    sp.dma_start(xb[:, t % 3], g.x_rows(I, l, t)).then_inc(*x_in[t % 3].up(16))

            def evac_act(act, t):
                act.wait_ge(*tr.at(2 * t + 1))
                s = 1 if t < NCT else 0
                for k in range(4):
                    ins = nc.scalar.activation(hT[:, k, t * P:(t + 1) * P], ps[:, 2 * (t % 2), k * P:(k + 1) * P],
                                               ACT.Identity, bias=mc[:, s, 0, k:k + 1], scale=G[:, s, k:k + 1])
                ins.then_inc(*ev_a.up())

            @block.scalar
            def _(act):
                act.wait_ge(*coef.at(2))
                for t in range(NT):
                    act.wait_ge(*x_in[t % 3].at(16 * (t // 3 + 1)))
                    if t >= 1:
                        act.wait_ge(*sq.at(t))
                    nc.scalar.activation(junk[:], xb[:, t % 3], ACT.Square, accum_out=ss[:, t:t + 1]).then_inc(*sq.up())
                    if t >= 1:
                        evac_act(act, t - 1)
                evac_act(act, NT - 1)

            def evac_dve(dve, t):
                dve.wait_ge(*tr.at(2 * t + 2))
                s = 1 if t < NCT else 0
                for k in range(4, 8):
                    ins = nc.vector.tensor_scalar(hT[:, k, t * P:(t + 1) * P], ps[:, 2 * (t % 2) + 1, (k - 4) * P:(k - 3) * P],
                                                  G[:, s, k:k + 1], mc[:, s, 0, k:k + 1], ALU.mult, ALU.add)
                ins.then_inc(*ev_d.up())

            @block.vector
            def _(dve):
                link = linker(dve, chain)
                dve.wait_ge(*small.at(16 * 5))
                for s in range(2):
                    nc.vector.scalar_tensor_tensor(G[:, s], mc[:, s, 1], 1.0, gn[:], ALU.add, ALU.mult).then_inc(*coef.up())
                dve.wait_ge(*coef.at(2))
                for t in range(NT):
                    dve.wait_ge(*sq.at(t + 1))
                    nc.vector.tensor_scalar(rs[:, t:t + 1], ss[:, t:t + 1], 1.0 / D, EPS, ALU.mult, ALU.add).then_inc(*g.vr.up())
                    dve.wait_ge(*g.rq.at(t + 1))
                    if t >= 2:
                        dve.wait_ge(*tr.at(2 * (t - 1)))
                    nc.vector.tensor_scalar(xn[:, t % 2], xb[:, t % 3], rs[:, t:t + 1], None, ALU.mult).then_inc(*normed.up())
                    if t >= 1:
                        evac_dve(dve, t - 1)
                evac_dve(dve, NT - 1)

            @block.gpsimd
            def _(pool):
                for t in range(NT):
                    pool.wait_ge(*g.vr.at(t + 1))
                    nc.gpsimd.tensor_tensor(rs[:, t:t + 1], rs[:, t:t + 1], g.mhalf[:, 0:1], ALU.pow).then_inc(*g.rq.up())

            @block.tensor
            def _(pe):
                for t in range(NT):
                    pe.wait_ge(*normed.at(t + 1))
                    for half in range(2):
                        if t >= 2:
                            pe.wait_ge(*(ev_d if half else ev_a).at(t - 1))
                        for k in range(4):
                            ins = nc.tensor.transpose(ps[:, 2 * (t % 2) + half, k * P:(k + 1) * P],
                                                      xn[:, t % 2, (4 * half + k) * P:(4 * half + k + 1) * P], g.ident)
                        ins.then_inc(*tr.up())
        sg.settle()


def stage_project(nc, g, I, l):
    sg, ps, hT = g.sg, g.ps, g.hT
    groups = [(0, 512, "c", 0), (512, 256, "c", 512), (C_RWKV, 512, "c", 768), (C_RWKV + 512, 512, "c", 1280),
              (C_MLA, 272, "t", 0), (C_MLA + 272, 272, "t", 272), (C_RET, 512, "t", W_MLA), (C_RET + 512, 512, "t", W_MLA + 512)]
    jobs = []
    for n, (c0, w, kind, o) in enumerate(groups):
        if kind == "c":
            jobs += [(n, m, s) for m in range(w // P) for s in range(3)]
        else:
            jobs += [(n, t, None) for t in range(NT)]
    lastjob = [max(j for j, x in enumerate(jobs) if x[0] == n) for n in range(len(groups))]
    RW, RO = 3, 6
    with ExitStack() as cx:
        sb = Bufs(nc, cx, f"p{l}")
        w = sb("w", [P, RW, KT, 512])
        zo = sb("zo", [P, RO, 512])
        w_in = [sg(f"w_slot{i}") for i in range(RW)]
        st = [sg(f"out_slot{i}") for i in range(RO)]
        mm, ev = sg("mm_done"), [sg("evac_a"), sg("evac_d")]
        with nc.Block() as block:
            @block.sync
            def _(sp):
                for n, (c0, wd, kind, o) in enumerate(groups):
                    if n >= RW:
                        sp.wait_ge(*mm.at(lastjob[n - RW] + 1))
                    sp.dma_start(w[:, n % RW, :, 0:wd], I["w_in"][l].rearrange("(k p) f -> p k f", p=P)[:, :, c0:c0 + wd]) \
                        .then_inc(*w_in[n % RW].up(16))

            @block.tensor
            def _(pe):
                for j, (n, m, s) in enumerate(jobs):
                    if j == 0 or jobs[j - 1][0] != n:
                        pe.wait_ge(*w_in[n % RW].at(16 * (n // RW + 1)))
                    if j >= 8:
                        pe.wait_ge(*ev[j % 2].at((j - 8) // 2 + 1))
                    wd = groups[n][1]
                    for k in range(KT):
                        if s is not None:
                            t0, tw = SPANS[s]
                            ins = nc.tensor.matmul(ps[:, j % 8, 0:tw], w[:, n % RW, k, m * P:(m + 1) * P], hT[:, k, t0:t0 + tw],
                                                   start=(k == 0), stop=(k == KT - 1))
                        else:
                            ins = nc.tensor.matmul(ps[:, j % 8, 0:wd], hT[:, k, m * P:(m + 1) * P], w[:, n % RW, k, 0:wd],
                                                   start=(k == 0), stop=(k == KT - 1))
                    ins.then_inc(*mm.up())

            def width(j):
                n, m, s = jobs[j]
                return groups[n][1] if s is None else SPANS[s][1]

            @block.scalar
            def _(act):
                for j in range(0, len(jobs), 2):
                    act.wait_ge(*mm.at(j + 1))
                    if j >= RO:
                        act.wait_ge(*st[j % RO].at(16 * (j // RO)))
                    nc.scalar.copy(zo[:, j % RO, 0:width(j)], ps[:, j % 8, 0:width(j)]).then_inc(*ev[0].up())

            @block.vector
            def _(dve):
                for j in range(1, len(jobs), 2):
                    dve.wait_ge(*mm.at(j + 1))
                    if j >= RO:
                        dve.wait_ge(*st[j % RO].at(16 * (j // RO)))
                    nc.vector.tensor_copy(zo[:, j % RO, 0:width(j)], ps[:, j % 8, 0:width(j)]).then_inc(*ev[1].up())

            @block.gpsimd
            def _(pool):
                for j, (n, m, s) in enumerate(jobs):
                    pool.wait_ge(*ev[j % 2].at(j // 2 + 1))
                    o = groups[n][3]
                    if s is not None:
                        t0, tw = SPANS[s]
                        dst = g.zc[o + m * P:o + (m + 1) * P, t0:t0 + tw]
                    else:
                        dst = g.zt[m * P:(m + 1) * P, o:o + groups[n][1]]
                    pool.dma_start(dst, zo[:, j % RO, 0:width(j)]).then_inc(*st[j % RO].up(16))
                for s in st:
                    pool.wait_ge(s.sem, s.made)
        sg.settle()


def stage_conv(nc, g, I, l):
    sg, ps, yT = g.sg, g.ps, g.yT
    with ExitStack() as cx:
        sb = Bufs(nc, cx, f"c{l}")
        z = sb("z", [P, 6, T])
        u = sb("u", [P, 2, T + 4])
        y = sb("y", [P, 2, T])
        sq = sb("sq", [P, 2, T])
        rs = sb("rs", [P, T])
        cw = sb("cw", [P, 3, 2])
        go = sb("go", [P, 2])
        z_in, small, chain = sg("z_in"), sg("small_in"), sg("dve_chain")
        prod, sqd, mm, lnd = sg("normed"), sg("sq_done"), sg("mm_done"), sg("ln_done")
        with nc.Block() as block:
            @block.sync
            def _(sp):
                sp.dma_start(z[:], g.zc[0:768].rearrange("(m p) t -> p m t", p=P)).then_inc(*z_in.up(16))
                with nc.allow_non_contiguous_dma(reason="vectors into columns"):
                    for n in range(3):
                        sp.dma_start(cw[:, n], col(I["conv_w"][l, n], 2)).then_inc(*small.up(16))
                    sp.dma_start(go[:], col(I["g_out_conv"][l], 2)).then_inc(*small.up(16))

            @block.vector
            def _(dve):
                link = linker(dve, chain)
                link(nc.vector.memset(u[:], 0.0))
                dve.wait_ge(*z_in.at(16))
                dve.wait_ge(*small.at(64))
                for i in range(2):
                    link(nc.vector.tensor_tensor(u[:, i, 1:CTX + 1], z[:, 2 + i, 0:CTX], z[:, 4 + i, 0:CTX], ALU.mult))
                    link(nc.vector.tensor_tensor(u[:, i, CTX + 3:T + 3], z[:, 2 + i, CTX:T], z[:, 4 + i, CTX:T], ALU.mult))
                    for a, b, o in ((0, CTX, 0), (CTX, T, 2)):
                        link(nc.vector.tensor_scalar(y[:, i, a:b], u[:, i, a + o:b + o], cw[:, 0, i:i + 1], None, ALU.mult))
                        link(nc.vector.scalar_tensor_tensor(y[:, i, a:b], u[:, i, a + o + 1:b + o + 1], cw[:, 1, i:i + 1],
                                                            y[:, i, a:b], ALU.mult, ALU.add))
                        link(nc.vector.scalar_tensor_tensor(y[:, i, a:b], u[:, i, a + o + 2:b + o + 2], cw[:, 2, i:i + 1],
                                                            y[:, i, a:b], ALU.mult, ALU.add))
                    nc.vector.tensor_tensor(y[:, i], y[:, i], z[:, i], ALU.mult).then_inc(*prod.up())
                for s, (t0, tw) in enumerate(SPANS):
                    dve.wait_ge(*mm.at(s + 1))
                    r = rs[:, t0:t0 + tw]
                    nc.vector.tensor_scalar(r, ps[:, s, 0:tw], 1.0 / GW, EPS, ALU.mult, ALU.add).then_inc(*g.vr.up())
                for s, (t0, tw) in enumerate(SPANS):
                    dve.wait_ge(*g.rq.at(s + 1))
                    r = rs[:, t0:t0 + tw]
                    for i in range(2):
                        nc.vector.scalar_tensor_tensor(yT[:, i, t0:t0 + tw], y[:, i, t0:t0 + tw], go[:, i:i + 1], r,
                                                       ALU.mult, ALU.mult)

            @block.scalar
            def _(act):
                for i in range(2):
                    act.wait_ge(*prod.at(i + 1))
                    nc.scalar.activation(sq[:, i], y[:, i], ACT.Square).then_inc(*sqd.up())
                for s, (t0, tw) in enumerate(SPANS):
                    act.wait_ge(*g.vr.at(s + 1))
                    r = rs[:, t0:t0 + tw]
                    nc.scalar.activation(r, r, ACT.Ln).then_inc(*lnd.up())
                    act.wait_ge(*lnd.at(s + 1))
                    nc.scalar.activation(r, r, ACT.Exp, scale=-0.5).then_inc(*g.rq.up())

            @block.tensor
            def _(pe):
                pe.wait_ge(*sqd.at(2))
                for s, (t0, tw) in enumerate(SPANS):
                    for i in range(2):
                        ins = nc.tensor.matmul(ps[:, s, 0:tw], g.ones, sq[:, i, t0:t0 + tw], start=(i == 0), stop=(i == 1))
                    ins.then_inc(*mm.up())
        sg.settle()


def stage_mla_prep(nc, g, I, l, S):
    sg, ps = g.sg, g.ps
    QT, KTr, V = S["QT"], S["KT"], S["V"]
    with ExitStack() as cx:
        sb = Bufs(nc, cx, f"m{l}")
        z = sb("z", [P, 3, W_MLA])
        rope = sb("rope", [P, SEQ // P, 2, 32])
        wkv = sb("wkv", [P, 512])
        gkv = sb("gkv", [P, 1])
        gqk = sb("gqk", [P, 2, QK])
        junk = sb("junk", [P, P])
        st = sb("st", [P, NT, 2])
        cn = sb("cn", [P, P])
        cT = sb("cT", [P, P])
        qk = sb("qk", [P, 2, 8, QK])
        sq = sb("sq", [P, 8, QK])
        s8 = sb("s8", [P, 8])
        ra = sb("ra", [P, 8, 32])
        rb = sb("rb", [P, 8, 32])
        z_in, small, chain = [sg(f"w_slot{i}") for i in range(3)], sg("small_in"), sg("dve_chain")
        sqd, cnd, ctd, cte, kvd, gath = sg("sq_done"), sg("normed"), sg("mla_ct"), sg("mla_cte"), sg("mm_done"), sg("mla_gath")
        kvr, qkd, tr, ev_a, ev_d = sg("mla_kvr"), sg("mla_qk"), sg("transposed"), sg("evac_a"), sg("evac_d")
        with nc.Block() as block:
            @block.sync
            def _(sp):
                sp.dma_start(wkv[:, 0:GW], I["w_uk"][l]).then_inc(*small.up(16))
                sp.dma_start(wkv[:, GW:2 * GW], I["w_uv"][l]).then_inc(*small.up(16))
                with nc.allow_non_contiguous_dma(reason="vectors into columns"):
                    sp.dma_start(gkv[:], col(I["g_kv_norm"][l], 1)).then_inc(*small.up(16))
                sp.dma_start(gqk[:, 0], row(I["g_q_norm"][l])).then_inc(*small.up(16))
                sp.dma_start(gqk[:, 1], row(I["g_k_norm"][l])).then_inc(*small.up(16))
                sp.dma_start(rope[:], g.C["rope_m"].rearrange("(t p) (c f) -> p t c f", p=P, c=2)).then_inc(*small.up(16))
                for t in range(NT):
                    if t >= 3:
                        sp.wait_ge(*gath.at(t - 2))
                    sp.dma_start(z[:, t % 3], g.zt[t * P:(t + 1) * P, 0:W_MLA]).then_inc(*z_in[t % 3].up(16))

            @block.scalar
            def _(act):
                act.wait_ge(*small.at(96))
                for t in range(NT):
                    zz = z[:, t % 3]
                    act.wait_ge(*z_in[t % 3].at(16 * (t // 3 + 1)))
                    if t >= 1:
                        act.wait_ge(*sqd.at(t))
                    nc.scalar.activation(junk[:], zz[:, 384:512], ACT.Square, accum_out=st[:, t, 0:1]).then_inc(*sqd.up())
                    if t >= 2:
                        act.wait_ge(*tr.at(2 * (t - 1)))
                    q = qk[:, t % 2]
                    nc.scalar.copy(q[:, 0:4, 0:64], zz[:, 0:256].rearrange("p (h d) -> p h d", h=4))
                    nc.scalar.copy(q[:, 0:4, 64:96], zz[:, 256:384].rearrange("p (h d) -> p h d", h=4))
                    act.wait_ge(*cnd.at(t + 1))
                    nc.scalar.copy(q[:, 4:8, 64:96], zz[:, 512:544].unsqueeze(1).broadcast_to([P, 4, 32])).then_inc(*gath.up())
                    act.wait_ge(*ctd.at(t + 1))
                    nc.scalar.activation(cT[:], ps[:, 0, 0:P], ACT.Copy, scale=gkv[:, 0:1]).then_inc(*cte.up())
                    act.wait_ge(*kvd.at(t + 1))
                    nc.scalar.copy(q[:, 4:8, 0:64], ps[:, 1, 0:256].rearrange("p (h d) -> p h d", h=4))
                    nc.scalar.copy(V[:, t, :, 0:64], ps[:, 1, 256:512].rearrange("p (h d) -> p h d", h=4)).then_inc(*kvr.up())
                    act.wait_ge(*tr.at(2 * t + 1))
                    nc.scalar.copy(QT[0:QK, :, t * P:(t + 1) * P], ps[0:QK, 2, :].rearrange("p (h d) -> p h d", h=4)).then_inc(*ev_a.up())

            @block.vector
            def _(dve):
                link = linker(dve, chain)
                link(nc.vector.memset(V[:, :, :, 64:65], 1.0))
                link(nc.vector.memset(KTr[QK:QK + 1], 1.0))
                dve.wait_ge(*small.at(96))
                for t in range(NT):
                    zz, q = z[:, t % 3], qk[:, t % 2]
                    dve.wait_ge(*sqd.at(t + 1))
                    nc.vector.tensor_scalar(st[:, t, 1:2], st[:, t, 0:1], 1.0 / P, EPS, ALU.mult, ALU.add).then_inc(*g.vr.up())
                    dve.wait_ge(*g.rq.at(2 * t + 1))
                    if t >= 1:
                        dve.wait_ge(*ctd.at(t))
                    nc.vector.tensor_scalar(cn[:], zz[:, 384:512], st[:, t, 1:2], None, ALU.mult).then_inc(*cnd.up())
                    dve.wait_ge(*kvr.at(t + 1))
                    link(nc.vector.tensor_tensor(sq[:], q, q, ALU.mult))
                    link(nc.vector.tensor_reduce(s8[:], sq[:], AX_X, ALU.add))
                    nc.vector.tensor_scalar(s8[:], s8[:], 1.0 / QK, EPS, ALU.mult, ALU.add).then_inc(*g.vr.up())
                    dve.wait_ge(*g.rq.at(2 * t + 2))
                    link(nc.vector.tensor_tensor(q, q, s8[:].unsqueeze(2).broadcast_to([P, 8, QK]), ALU.mult))
                    for i in range(2):
                        link(nc.vector.tensor_tensor(q[:, 4 * i:4 * i + 4], q[:, 4 * i:4 * i + 4],
                                                     gqk[:, i].unsqueeze(1).broadcast_to([P, 4, QK]), ALU.mult))
                    if t >= NCT:
                        r = rope[:, t - NCT]
                        link(nc.vector.tensor_tensor(ra[:], q[:, :, 64:96], r[:, 0].unsqueeze(1).broadcast_to([P, 8, 32]), ALU.mult))
                        q5 = q[:, :, 64:96].rearrange("p h (a s f) -> p h a s f", a=2, s=2)
                        b5 = rb[:].rearrange("p h (a s f) -> p h a s f", a=2, s=2)
                        r5 = r[:, 1].rearrange("p (a s f) -> p a s f", a=2, s=2)
                        for s in range(2):
                            link(nc.vector.tensor_tensor(b5[:, :, :, s], q5[:, :, :, 1 - s],
                                                         r5[:, :, s].unsqueeze(1).broadcast_to([P, 8, 2, 8]), ALU.mult))
                        link(nc.vector.tensor_tensor(q[:, :, 64:96], ra[:], rb[:], ALU.add))
                    nc.vector.tensor_copy(s8[0:1, 0:1], s8[0:1, 0:1]).then_inc(*qkd.up())
                    dve.wait_ge(*tr.at(2 * t + 2))
                    nc.vector.tensor_copy(KTr[0:QK, :, t * P:(t + 1) * P], ps[0:QK, 3, :].rearrange("p (h d) -> p h d", h=4)).then_inc(*ev_d.up())

            @block.gpsimd
            def _(pool):
                for t in range(NT):
                    pool.wait_ge(*g.vr.at(2 * t + 1))
                    nc.gpsimd.tensor_tensor(st[:, t, 1:2], st[:, t, 1:2], g.mhalf[:, 0:1], ALU.pow).then_inc(*g.rq.up())
                    pool.wait_ge(*g.vr.at(2 * t + 2))
                    nc.gpsimd.tensor_tensor(s8[:], s8[:], g.mhalf[:, 0:8], ALU.pow).then_inc(*g.rq.up())

            @block.tensor
            def _(pe):
                for t in range(NT):
                    pe.wait_ge(*cnd.at(t + 1))
                    if t >= 1:
                        pe.wait_ge(*cte.at(t))
                    nc.tensor.transpose(ps[:, 0, 0:P], cn[:], g.ident).then_inc(*ctd.up())
                    pe.wait_ge(*cte.at(t + 1))
                    if t >= 1:
                        pe.wait_ge(*kvr.at(t))
                    nc.tensor.matmul(ps[:, 1, :], cT[:], wkv[:], start=True, stop=True).then_inc(*kvd.up())
                    pe.wait_ge(*qkd.at(t + 1))
                    for i in range(2):
                        if t >= 1:
                            pe.wait_ge(*(ev_d if i else ev_a).at(t))
                        for h in range(4):
                            ins = nc.tensor.transpose(ps[0:QK, 2 + i, h * P:(h + 1) * P], qk[:, t % 2, 4 * i + h], g.ident)
                        ins.then_inc(*tr.up())
        sg.settle()


def stage_mla_attend(nc, g, I, l, S, need_ctx):
    sg, ps, yT = g.sg, g.ps, g.yT
    QT, KTr, V = S["QT"], S["KT"], S["V"]
    SCALE = QK ** -0.5
    groups = ([(0, CTX, NCT)] if need_ctx else []) + [(CTX, 512, NT), (CTX + 512, 512, NT)]
    NP = 3
    with ExitStack() as cx:
        sb = Bufs(nc, cx, f"a{l}")
        mx = sb("mx", [P, 2, H])
        pt = sb("pt", [P, NP, 512])
        ot = sb("ot", [65, H, 512])
        o = sb("o", [P, GW])
        on = sb("on", [P, 2, GW])
        junk = sb("junk", [P, GW])
        rc = sb("rc", [P, H])
        ss = sb("ss", [P, 2])
        go = sb("go", [P, 2])
        small, chain = sg("small_in"), sg("dve_chain")
        sc, mxd, mt, mrow = sg("at_sc"), sg("at_mx"), sg("at_mt"), sg("at_mrow")
        st, ex, pv, ote = sg("at_st"), sg("at_ex"), sg("at_pv"), sg("at_ote")
        otr, od, sqd, ond, ytr, ye = sg("at_otr"), sg("at_od"), sg("sq_done"), sg("normed"), sg("transposed"), sg("evac_a")
        with nc.Block() as block:
            @block.sync
            def _(sp):
                with nc.allow_non_contiguous_dma(reason="vectors into columns"):
                    sp.dma_start(go[:], col(I["g_out_mla"][l], 2)).then_inc(*small.up(16))

            @block.tensor
            def _(pe):
                nsc = nst = nq = nh = 0
                for q0, qw, nk in groups:
                    keys = nk * P
                    if nq:
                        pe.wait_ge(*ye.at(nq))
                    for qt in range(qw // P):
                        qs = slice(q0 + qt * P, q0 + (qt + 1) * P)
                        for h in range(H):
                            if nsc >= 2:
                                pe.wait_ge(*mxd.at(nsc - 1))
                            b = 3 * (nsc % 2)
                            for n in range(0, keys, 512):
                                kw = min(512, keys - n)
                                ins = nc.tensor.matmul(ps[:, b + n // 512, 0:kw], QT[0:QK, h, qs], KTr[0:QK, h, n:n + kw],
                                                       start=True, stop=True)
                            ins.then_inc(*sc.up())
                            nsc += 1
                        pe.wait_ge(*mxd.at(nsc))
                        if nq >= 1:
                            pe.wait_ge(*mrow.at(nq))
                        for h in range(H):
                            ins = nc.tensor.matmul(ps[96:97, 6, h * P:(h + 1) * P], mx[:, nq % 2, h:h + 1], g.ident,
                                                   start=True, stop=True)
                        ins.then_inc(*mt.up())
                        nq += 1
                    pe.wait_ge(*mrow.at(nq))
                    for h in range(H):
                        def scores_t(kt):
                            n = nst + kt
                            if n >= 4:
                                pe.wait_ge(*ex.at(n - 3))
                            nc.tensor.matmul(ps[:, n % 4, 0:qw], KTr[0:QK + 1, h, kt * P:(kt + 1) * P],
                                             QT[0:QK + 1, h, q0:q0 + qw], start=True, stop=True).then_inc(*st.up())
                        for kt in range(min(2, nk)):
                            scores_t(kt)
                        for kt in range(nk):
                            if kt + 2 < nk:
                                scores_t(kt + 2)
                            pe.wait_ge(*ex.at(nst + kt + 1))
                            if kt == 0 and nh >= 2:
                                pe.wait_ge(*ote.at(nh - 1))
                            nc.tensor.matmul(ps[0:65, 4 + nh % 2, 0:qw], V[:, kt, h], pt[:, (nst + kt) % NP, 0:qw],
                                             start=(kt == 0), stop=(kt == nk - 1)).then_inc(*pv.up())
                        nst += nk
                        nh += 1
                    pe.wait_ge(*ote.at(nh))
                    for qt in range(qw // P):
                        n = nq - qw // P + qt
                        if n >= 1:
                            pe.wait_ge(*od.at(n))
                        for h in range(H):
                            ins = nc.tensor.transpose(ps[:, 7, h * 65:(h + 1) * 65], ot[:, h, qt * P:(qt + 1) * P], g.ident[0:65, 0:65])
                        ins.then_inc(*otr.up())
                        pe.wait_ge(*ond.at(n + 1))
                        if n >= 1:
                            pe.wait_ge(*ye.at(n))
                        for i in range(2):
                            ins = nc.tensor.transpose(ps[:, 6, i * P:(i + 1) * P], on[:, n % 2, i * P:(i + 1) * P], g.ident)
                        ins.then_inc(*ytr.up())

            @block.gpsimd
            def _(pool):
                for n in range(sum(qw // P for _, qw, _ in groups)):
                    pool.wait_ge(*g.vr.at(n + 1))
                    nc.gpsimd.tensor_tensor(ss[:, 1:2], ss[:, 1:2], g.mhalf[:, 0:1], ALU.pow).then_inc(*g.rq.up())

            @block.vector
            def _(dve):
                link = linker(dve, chain)
                nsc = nq = 0
                for q0, qw, nk in groups:
                    keys = nk * P
                    for qt in range(qw // P):
                        for h in range(H):
                            dve.wait_ge(*sc.at(nsc + 1))
                            if h == 0 and nq >= 2:
                                dve.wait_ge(*mt.at(nq - 1))
                            b = 3 * (nsc % 2)
                            src = ps[:, b:b + 3, :].rearrange("p b n -> p (b n)")[:, 0:keys]
                            nc.vector.reduce_max(mx[:, nq % 2, h:h + 1], src, AX_X).then_inc(*mxd.up())
                            nsc += 1
                        nq += 1
                    for qt in range(qw // P):
                        n = nq - qw // P + qt
                        dve.wait_ge(*otr.at(n + 1))
                        pss = ps[:, 7, 0:260].rearrange("p (h d) -> p h d", h=H)
                        link(nc.vector.reciprocal(rc[:], pss[:, :, 64]))
                        nc.vector.tensor_tensor(o[:].rearrange("p (h d) -> p h d", h=H), pss[:, :, 0:64],
                                                rc[:].unsqueeze(2).broadcast_to([P, H, 64]), ALU.mult).then_inc(*od.up())
                        dve.wait_ge(*sqd.at(n + 1))
                        nc.vector.tensor_scalar(ss[:, 1:2], ss[:, 0:1], 1.0 / GW, EPS, ALU.mult, ALU.add).then_inc(*g.vr.up())
                        dve.wait_ge(*g.rq.at(n + 1))
                        if n >= 2:
                            dve.wait_ge(*ytr.at(n - 1))
                        nc.vector.tensor_scalar(on[:, n % 2], o[:], ss[:, 1:2], None, ALU.mult).then_inc(*ond.up())

            @block.scalar
            def _(act):
                act.wait_ge(*small.at(16))
                nq = nst = nh = 0
                for q0, qw, nk in groups:
                    for qt in range(qw // P):
                        act.wait_ge(*mt.at(nq + 1))
                        nc.scalar.activation(QT[96:97, :, q0 + qt * P:q0 + (qt + 1) * P],
                                             ps[96:97, 6, :].rearrange("p (h d) -> p h d", h=H), ACT.Copy, scale=-1.0).then_inc(*mrow.up())
                        nq += 1
                    for h in range(H):
                        for kt in range(nk):
                            act.wait_ge(*st.at(nst + 1))
                            if nst >= NP:
                                act.wait_ge(*pv.at(nst - NP + 1))
                            nc.scalar.activation(pt[:, nst % NP, 0:qw], ps[:, nst % 4, 0:qw], ACT.Exp, scale=SCALE).then_inc(*ex.up())
                            nst += 1
                        act.wait_ge(*pv.at(nst))
                        nc.scalar.copy(ot[:, h, 0:qw], ps[0:65, 4 + nh % 2, 0:qw]).then_inc(*ote.up())
                        nh += 1
                    for qt in range(qw // P):
                        n = nq - qw // P + qt
                        act.wait_ge(*od.at(n + 1))
                        if n >= 1:
                            act.wait_ge(*sqd.at(n))
                        nc.scalar.activation(junk[:], o[:], ACT.Square, accum_out=ss[:, 0:1]).then_inc(*sqd.up())
                        act.wait_ge(*ytr.at(n + 1))
                        for i in range(2):
                            ins = nc.scalar.activation(yT[:, 2 + i, q0 + qt * P:q0 + (qt + 1) * P], ps[:, 6, i * P:(i + 1) * P],
                                                       ACT.Copy, scale=go[:, i:i + 1])
                        ins.then_inc(*ye.up())
        sg.settle()


def stage_retention(nc, g, I, l, need_ctx):
    sg, ps, yT = g.sg, g.ps, g.yT
    t_first = 0 if need_ctx else NCT
    with ExitStack() as cx:
        sb = Bufs(nc, cx, f"r{l}")
        z = sb("z", [P, 2, W_RET])
        rope = sb("rope", [P, 2, 2, HD])
        ra = sb("ra", [P, 8, HD])
        rb = sb("rb", [P, 8, HD])
        qk = sb("qk", [P, 2, 8, HD])
        QT = sb("QT", [P, 4, T])
        QX = sb("QX", [P, 2, 2, T])
        kz = sb("kz", [P, 2, GW])
        V = sb("V", [P, NT, GW])
        G = sb("G", [P, NT, GW])
        R = sb("R", [P, NT, 4, P])
        dR = sb("dR", [P, NT, 4, P])
        dm = sb("dm", [P, H, P])
        xi = sb("xi", [P, 2, 2, P])
        ze = sb("ze", [P, 2, GW])
        gd = sb("gd", [P, 2])
        pt = sb("pt", [P, H, P])
        o = sb("o", [P, GW])
        sq = sb("sq", [P, GW])
        s4 = sb("s4", [P, H])
        on = sb("on", [P, GW])
        gr = sb("gr", [P, GW])
        z_in, small, chain = [sg(f"w_slot{i}") for i in range(2)], sg("small_in"), sg("dve_chain")
        qkd, tr, ev_a, ev_d, zd, gd_s = sg("normed"), sg("transposed"), sg("evac_a"), sg("evac_d"), sg("rt_zd"), sg("rt_g")
        kzd, rm, rev = sg("rt_kz"), sg("rt_rm"), sg("rt_rev")
        with nc.Block() as block:
            @block.sync
            def _(sp):
                for name, dst in (("dmat", dm), ("xi", xi), ("zeta", ze), ("gdec", gd)):
                    shape = list(dst.shape)
                    sp.dma_start(dst[:], g.C[name].rearrange("p (a b c) -> p a b c", a=2, b=2) if name == "xi" else
                                 g.C[name] if name == "gdec" else
                                 g.C[name].rearrange("p (a b) -> p a b", a=shape[1])).then_inc(*small.up(16))
                sp.dma_start(gr[:], row(I["g_ret_norm"][l])).then_inc(*small.up(16))
                for t in range(NT):
                    if t >= 2:
                        sp.wait_ge(*zd.at(t - 1))
                        sp.wait_ge(*gd_s.at(t - 1))
                    sp.dma_start(z[:, t % 2], g.zt[t * P:(t + 1) * P, W_MLA:W_MLA + W_RET]).then_inc(*z_in[t % 2].up(16))
                    if t >= NCT:
                        sp.dma_start(rope[:, t % 2], g.C["rope_r"].rearrange("(t p) (c f) -> p t c f", p=P, c=2)[:, t - NCT]) \
                            .then_inc(*z_in[t % 2].up(16))

            def z_at(t):
                n = 0
                for u in range(t % 2, t + 1, 2):
                    n += 16 if u < NCT else 32
                return n

            @block.vector
            def _(dve):
                link = linker(dve, chain)
                dve.wait_ge(*small.at(80))
                for t in range(NT):
                    zz, q = z[:, t % 2], qk[:, t % 2]
                    dve.wait_ge(*z_in[t % 2].at(z_at(t)))
                    z8 = zz[:, 0:512].rearrange("p (h d) -> p h d", h=8)
                    if t >= 2:
                        dve.wait_ge(*tr.at(t - 1))
                    if t < NCT:
                        link(nc.vector.tensor_copy(q, z8))
                    else:
                        r = rope[:, t % 2]
                        link(nc.vector.tensor_tensor(ra[:], z8, r[:, 0].unsqueeze(1).broadcast_to([P, 8, HD]), ALU.mult))
                        for s in range(2):
                            a, b = 32 * s, 32 * (1 - s)
                            link(nc.vector.tensor_tensor(rb[:, :, a:a + 32], z8[:, :, b:b + 32],
                                                         r[:, 1, a:a + 32].unsqueeze(1).broadcast_to([P, 8, 32]), ALU.mult))
                        link(nc.vector.tensor_tensor(q, ra[:], rb[:], ALU.add))
                    if t >= 1:
                        dve.wait_ge(*rm.at(t))
                    for d in range(2):
                        link(nc.vector.tensor_tensor(kz[:, d], q[:, 4:8].rearrange("p h d -> p (h d)"), ze[:, d], ALU.mult))
                    nc.vector.tensor_copy(V[:, t], zz[:, 512:768]).then_inc(*zd.up())
                    dve.wait_ge(*zd.at(t + 1))
                    nc.vector.tensor_copy(s4[0:1, 0:1], gr[0:1, 0:1]).then_inc(*qkd.up())
                    dve.wait_ge(*ev_a.at(t + 1))
                    for d in range(2):
                        link(nc.vector.tensor_tensor(QX[:, :, d, t * P:(t + 1) * P],
                                                     ps[:, t % 2, 0:2 * P].rearrange("p (a n) -> p a n", a=2), xi[:, :, d], ALU.mult))
                    nc.vector.tensor_copy(s4[0:1, 0:1], gr[0:1, 0:1]).then_inc(*ev_d.up())
                    dve.wait_ge(*rm.at(t + 1))
                    nc.vector.tensor_tensor(dR[:, t], ps[:, 2 + t % 2].rearrange("p (a n) -> p a n", a=4),
                                            g.blk.unsqueeze(1).broadcast_to([P, 4, P]), ALU.mult).then_inc(*rev.up())
                dve.wait_ge(*rev.at(NT))
                for d, order in ((0, list(range(NT))), (1, [1, 0] + list(range(NT - 1, NCT - 1, -1)))):
                    link(nc.vector.memset(R[:, order[0], 2 * d:2 * d + 2], 0.0))
                    for a, b in zip(order, order[1:]):
                        for p in range(2):
                            link(nc.vector.scalar_tensor_tensor(R[:, b, 2 * d + p], R[:, a, 2 * d + p], gd[:, p:p + 1],
                                                                dR[:, a, 2 * d + p], ALU.mult, ALU.add))

            @block.scalar
            def _(act):
                for t in range(NT):
                    act.wait_ge(*z_in[t % 2].at(z_at(t)))
                    nc.scalar.activation(G[:, t], z[:, t % 2, 768:1024], ACT.Silu).then_inc(*gd_s.up())
                    act.wait_ge(*tr.at(t + 1))
                    nc.scalar.copy(QT[:, :, t * P:(t + 1) * P], ps[:, t % 2].rearrange("p (a n) -> p a n", a=4)).then_inc(*ev_a.up())

            @block.tensor
            def _(pe):
                for t in range(NT):
                    pe.wait_ge(*qkd.at(t + 1))
                    if t >= 2:
                        pe.wait_ge(*ev_a.at(t - 1))
                        pe.wait_ge(*ev_d.at(t - 1))
                        pe.wait_ge(*rev.at(t - 1))
                    for a in range(4):
                        ins = nc.tensor.transpose(ps[:, t % 2, a * P:(a + 1) * P],
                                                  qk[:, t % 2, 2 * a:2 * a + 2].rearrange("p h d -> p (h d)"), g.ident)
                    ins.then_inc(*tr.up())
                    for d in range(2):
                        for p in range(2):
                            n = 2 * d + p
                            ins = nc.tensor.matmul(ps[:, 2 + t % 2, n * P:(n + 1) * P], kz[:, d, p * P:(p + 1) * P],
                                                   V[:, t, p * P:(p + 1) * P], start=True, stop=True)
                    ins.then_inc(*rm.up())
        sg.settle()
        sc, ptd, om, oe, od, ytr, ye = sg("at_sc"), sg("at_ex"), sg("at_pv"), sg("at_ote"), sg("normed"), sg("transposed"), sg("evac_a")
        tiles = list(range(t_first, NT))
        with nc.Block() as block:
            @block.tensor
            def _(pe):
                for n, t in enumerate(tiles):
                    ts = slice(t * P, (t + 1) * P)
                    if n >= 1:
                        pe.wait_ge(*ptd.at(n))
                    for h in range(H):
                        hp = slice(HD * (h % 2), HD * (h % 2) + HD)
                        b = 3 * (h % 2)
                        ins = nc.tensor.matmul(ps[:, b, (h // 2) * P:(h // 2 + 1) * P], QT[hp, 2 + h // 2, ts], QT[hp, h // 2, ts],
                                               start=True, stop=True)
                    ins.then_inc(*sc.up())
                    pe.wait_ge(*ptd.at(n + 1))
                    if n >= 1:
                        pe.wait_ge(*oe.at(n))
                    for p in range(2):
                        for d in range(2):
                            nc.tensor.matmul(ps[:, 1, p * P:(p + 1) * P], QX[:, p, d, ts], R[:, t, 2 * d + p], start=(d == 0), stop=False)
                        for h in (2 * p, 2 * p + 1):
                            ins = nc.tensor.matmul(ps[:, 1, h * HD:(h + 1) * HD], pt[:, h], V[:, t, h * HD:(h + 1) * HD],
                                                   start=False, stop=(h == 2 * p + 1))
                    ins.then_inc(*om.up())
                    pe.wait_ge(*od.at(n + 1))
                    if n >= 1:
                        pe.wait_ge(*ye.at(n))
                    for i in range(2):
                        ins = nc.tensor.transpose(ps[:, 2, i * P:(i + 1) * P], on[:, i * P:(i + 1) * P], g.ident)
                    ins.then_inc(*ytr.up())

            @block.vector
            def _(dve):
                link = linker(dve, chain)
                for n, t in enumerate(tiles):
                    dve.wait_ge(*sc.at(n + 1))
                    if n >= 1:
                        dve.wait_ge(*om.at(n))
                    for a in range(2):
                        ins = nc.vector.tensor_tensor(pt[:, a::2], ps[:, 3 * a, 0:2 * P].rearrange("p (h n) -> p h n", h=2), dm[:, a::2], ALU.mult)
                    ins.then_inc(*ptd.up())
                    dve.wait_ge(*oe.at(n + 1))
                    o4 = o[:].rearrange("p (h d) -> p h d", h=H)
                    link(nc.vector.tensor_tensor(sq[:], o[:], o[:], ALU.mult))
                    link(nc.vector.tensor_reduce(s4[:], sq[:].rearrange("p (h d) -> p h d", h=H), AX_X, ALU.add))
                    nc.vector.tensor_scalar(s4[:], s4[:], 1.0 / HD, EPS, ALU.mult, ALU.add).then_inc(*g.vr.up())
                    dve.wait_ge(*g.rq.at(n + 1))
                    link(nc.vector.tensor_tensor(o4, o4, s4[:].unsqueeze(2).broadcast_to([P, H, HD]), ALU.mult))
                    link(nc.vector.tensor_tensor(o[:], o[:], gr[:], ALU.mult))
                    if n >= 1:
                        dve.wait_ge(*ytr.at(n))
                    nc.vector.tensor_tensor(on[:], o[:], G[:, t], ALU.mult).then_inc(*od.up())

            @block.gpsimd
            def _(pool):
                for n in range(len(tiles)):
                    pool.wait_ge(*g.vr.at(n + 1))
                    nc.gpsimd.tensor_tensor(s4[:], s4[:], g.mhalf[:, 0:H], ALU.pow).then_inc(*g.rq.up())

            @block.scalar
            def _(act):
                for n, t in enumerate(tiles):
                    act.wait_ge(*om.at(n + 1))
                    if n >= 1:
                        act.wait_ge(*od.at(n))
                    nc.scalar.copy(o[:], ps[:, 1, 0:GW]).then_inc(*oe.up())
                    act.wait_ge(*ytr.at(n + 1))
                    nc.scalar.copy(yT[:, 6:8, t * P:(t + 1) * P], ps[:, 2, 0:2 * P].rearrange("p (a n) -> p a n", a=2)).then_inc(*ye.up())
        sg.settle()


def views(need_ctx):
    return ([(0, CTX, 0)] if need_ctx else []) + [(CTX, SEQ, 1)]


def bank(ps, b, w):
    return ps[:, b:b + (w + 511) // 512, :].rearrange("p b n -> p (b n)")[:, 0:w]


def stage_rwkv_mix(nc, g, I, l, R):
    sg, M = g.sg, R["M"]
    with ExitStack() as cx:
        sb = Bufs(nc, cx, f"x{l}")
        z = sb("z", [P, 2, T + 4])
        tmp = sb("tmp", [P, T + 2])
        mu = sb("mu", [P, 8])
        hmu = sb("hmu", [P, 8])
        omu = sb("omu", [P, 8])
        z_in, small, chain, mixed, pad = [sg(f"w_slot{i}") for i in range(2)], sg("small_in"), sg("dve_chain"), sg("normed"), sg("coef")
        acted = sg("evac_a")
        with nc.Block() as block:
            @block.sync
            def _(sp):
                with nc.allow_non_contiguous_dma(reason="vectors into columns"):
                    sp.dma_start(mu[:], col(I["rwkv_mu"][l], 8)).then_inc(*small.up(16))
                    for d in range(2):
                        sp.dma_start(R["w0"][:, d], col(I["rwkv_w0"][l, d], 2)).then_inc(*small.up(16))
                        sp.dma_start(R["a0"][:, d], col(I["rwkv_a0"][l, d], 2)).then_inc(*small.up(16))
                        sp.dma_start(R["wa2"][0:64, d], I["rwkv_w2"][l, d]).then_inc(*small.up(16))
                        sp.dma_start(R["wa2"][64:128, d], I["rwkv_a2"][l, d]).then_inc(*small.up(16))
                    for name, n in (("rwkv_k_k", "kk"), ("rwkv_k_a", "ka"), ("rwkv_r_k", "rk"), ("g_ln_x", "gln")):
                        sp.dma_start(R[n][:], col(I[name][l], 2)).then_inc(*small.up(16))
                sp.dma_start(R["g2"][:], I["rwkv_g2"][l]).then_inc(*small.up(16))
                sp.dma_start(R["masks"][:], g.C["masks"].rearrange("p (d a n) -> p d a n", d=2, a=4)).then_inc(*small.up(16))
                sp.dma_start(R["nlev"][:], g.C["nlev"].rearrange("p (d a n) -> p d a n", d=2, a=LEVELS)).then_inc(*small.up(16))
                sp.wait_ge(*pad.at(1))
                for i in range(8):
                    if i >= 2:
                        sp.wait_ge(*mixed.at(i - 1))
                    for a, b, o in ((0, CTX, 1), (CTX, T, 3)):
                        sp.dma_start(z[:, i % 2, a + o:b + o], g.zc[768 + i * P:768 + (i + 1) * P, a:b]).then_inc(*z_in[i % 2].up(16))

            @block.vector
            def _(dve):
                link = linker(dve, chain)
                nc.vector.memset(z[:], 0.0).then_inc(*pad.up())
                dve.wait_ge(*small.at(16 * 16))
                link(nc.vector.tensor_scalar(hmu[:], mu[:], 0.5, None, ALU.mult))
                link(nc.vector.tensor_scalar(omu[:], mu[:], -1.0, 1.0, ALU.mult, ALU.add))
                link(nc.vector.tensor_scalar(R["oka"][:], R["ka"][:], -1.0, 1.0, ALU.mult, ALU.add))
                for i in range(8):
                    zz = z[:, i % 2]
                    dve.wait_ge(*z_in[i % 2].at(32 * (i // 2 + 1)))
                    link(nc.vector.tensor_tensor(tmp[:], zz[:, 0:T + 2], zz[:, 2:T + 4], ALU.add))
                    link(nc.vector.tensor_scalar(tmp[:], tmp[:], hmu[:, i:i + 1], None, ALU.mult))
                    link(nc.vector.scalar_tensor_tensor(M[:, i, 0:CTX], zz[:, 1:CTX + 1], omu[:, i:i + 1], tmp[:, 0:CTX], ALU.mult, ALU.add))
                    nc.vector.scalar_tensor_tensor(M[:, i, CTX:T], zz[:, CTX + 3:T + 3], omu[:, i:i + 1], tmp[:, CTX + 2:T + 2],
                                                   ALU.mult, ALU.add).then_inc(*mixed.up())
                    dve.wait_ge(*mixed.at(i + 1))

            @block.scalar
            def _(act):
                act.wait_ge(*mixed.at(7))
                nc.scalar.activation(M[0:64, 6], M[0:64, 6], ACT.Tanh)
                act.wait_ge(*mixed.at(8))
                nc.scalar.activation(M[:, 7], M[:, 7], ACT.Sigmoid)
        sg.settle()


def stage_rwkv_prep(nc, g, I, l, R, p, d):
    sg, ps, M = g.sg, g.ps, R["M"]
    A, SG, G, GX, E, KK, KS = (R[n] for n in ("A", "SG", "G", "GX", "E", "KK", "KS"))
    KR, BK, ET = R["KR"][d], R["BK"][d], R["ET"][d]
    r, k = M[:, p], M[:, 2 + p]
    sqd, wm, am, ssm, acted, gxd, gd, exd, chain = (sg(n) for n in ("sq_done", "rw_wm", "rw_am", "rw_ssm", "evac_a", "rw_gx",
                                                                    "rw_g", "rw_ex", "dve_chain"))
    allv, lnd, small = views(True), sg("ln_done"), sg("small_in")
    with nc.Block() as block:
        @block.sync
        def _(sp):
            if d == 0:
                sp.dma_start(R["reset"][:], g.C["reset"]).then_inc(*small.up(16))
                sp.wait_ge(*small.at(16))

        @block.tensor
        def _(pe):
            for s, (t0, tw) in enumerate(SPANS):
                ins = nc.tensor.matmul(ps[:, s, 0:tw], R["wa2"][0:64, d, p * P:(p + 1) * P], M[0:64, 6, t0:t0 + tw], start=True, stop=True)
            ins.then_inc(*wm.up())
            for s, (t0, tw) in enumerate(SPANS):
                ins = nc.tensor.matmul(ps[:, 3 + s, 0:tw], R["wa2"][64:128, d, p * P:(p + 1) * P], M[64:128, 6, t0:t0 + tw], start=True, stop=True)
            ins.then_inc(*am.up())
            if d == 0:
                pe.wait_ge(*sqd.at(1))
                pe.wait_ge(*acted.at(1))
                for s, (t0, tw) in enumerate(SPANS):
                    ins = nc.tensor.matmul(ps[:, s, 0:tw], g.blk, GX[:, t0:t0 + tw], start=True, stop=True)
                ins.then_inc(*ssm.up())

        @block.scalar
        def _(act):
            if d == 0:
                nc.scalar.activation(GX[:], k, ACT.Square, scale=R["kk"][:, p:p + 1]).then_inc(*sqd.up())
            act.wait_ge(*wm.at(1))
            for t0, tw, b in allv:
                ins = nc.scalar.activation(SG[:, t0:t0 + tw], bank(ps, b, tw), ACT.Sigmoid, bias=R["w0"][:, d, p:p + 1])
            ins.then_inc(*acted.up())
            act.wait_ge(*am.at(1))
            for t0, tw, b in allv:
                ins = nc.scalar.activation(A[:, t0:t0 + tw], bank(ps, 3 + b, tw), ACT.Sigmoid, bias=R["a0"][:, d, p:p + 1])
            ins.then_inc(*acted.up())
            if d == 0:
                act.wait_ge(*g.vr.at(1))
                nc.scalar.activation(E[:], E[:], ACT.Ln).then_inc(*lnd.up())
                act.wait_ge(*lnd.at(1))
                nc.scalar.activation(E[:], E[:], ACT.Exp, scale=-0.5).then_inc(*g.rq.up())
            act.wait_ge(*gxd.at(1))
            nc.scalar.activation(KR[:, 0], GX[:], ACT.Exp, scale=LWC).then_inc(*exd.up())
            act.wait_ge(*gd.at(1))
            nc.scalar.activation(KR[:, 1], G[:], ACT.Exp, scale=LWC).then_inc(*exd.up())
            nc.scalar.activation(BK[:, 0], G[:], ACT.Exp, scale=-LWC).then_inc(*exd.up())
            nc.scalar.activation(ET[:, 1], ET[:, 0], ACT.Exp, scale=LWC)

        @block.vector
        def _(dve):
            link = linker(dve, chain)
            dve.wait_ge(*acted.at(1))
            if d == 0:
                dve.wait_ge(*small.at(16))
            scan = nc.vector.tensor_tensor_scan(G[:], R["reset"][:], SG[:], 0.0, ALU.mult, ALU.add)
            if d == 0:
                scan.then_inc(*gd.up())
                dve.wait_ge(*gd.at(1))
            else:
                link(scan)
            link(nc.vector.tensor_copy(ET[:, 0], G[:, CH - 1::CH]))
            if d == 0:
                dve.wait_ge(*ssm.at(1))
                for t0, tw, b in allv:
                    ins = nc.vector.tensor_scalar(E[:, t0:t0 + tw], bank(ps, b, tw), 1e-12, None, ALU.add)
                ins.then_inc(*g.vr.up())
                dve.wait_ge(*g.rq.at(1))
                link(nc.vector.scalar_tensor_tensor(KK[:], k, R["kk"][:, p:p + 1], E[:], ALU.mult, ALU.mult))
                nc.vector.tensor_tensor(GX[:], G[:], SG[:], ALU.subtract).then_inc(*gxd.up())
            else:
                g3 = G[:].rearrange("p (c n) -> p c n", n=CH)
                nc.vector.tensor_tensor(GX[:].rearrange("p (c n) -> p c n", n=CH), ET[:, 0].unsqueeze(2).broadcast_to([P, T // CH, CH]),
                                        g3, ALU.subtract).then_inc(*gxd.up())
                dve.wait_ge(*gxd.at(1))
                nc.vector.tensor_tensor(G[:], GX[:], SG[:], ALU.add).then_inc(*gd.up())
            dve.wait_ge(*acted.at(2))
            link(nc.vector.tensor_scalar(E[:], A[:], R["ka"][:, p:p + 1], R["oka"][:, p:p + 1], ALU.mult, ALU.add))
            link(nc.vector.tensor_tensor(E[:], E[:], k, ALU.mult))
            if d == 0:
                link(nc.vector.tensor_copy(KS[:], E[:]))
            else:
                link(nc.vector.tensor_tensor(KS[:], KS[:], E[:], ALU.add))
            dve.wait_ge(*exd.at(3))
            link(nc.vector.tensor_tensor(KR[:, 0], KR[:, 0], KK[:], ALU.mult))
            link(nc.vector.tensor_tensor(KR[:, 1], KR[:, 1], r, ALU.mult))
            link(nc.vector.tensor_tensor(BK[:, 1], E[:], BK[:, 0], ALU.mult))
            link(nc.vector.tensor_tensor(BK[:, 0], BK[:, 0], KK[:], ALU.mult))
            link(nc.vector.tensor_tensor(BK[:, 0], BK[:, 0], A[:], ALU.mult))
    sg.settle()


def stage_rwkv_scan(nc, g, I, l, R, p, need_ctx):
    sg, ps, M, yT = g.sg, g.ps, R["M"], g.yT
    KR, BK, ET = R["KR"], R["BK"], R["ET"]
    order = [list(range(NT)), [1, 0] + list(range(NT - 1, NCT - 1, -1))]
    chunks = [[0, 1], [1, 0]]
    DD = (0, 1)
    with ExitStack() as cx:
        sb = Bufs(nc, cx, f"s{l}{p}")
        UM = [sb(f"UM{d}", [P, 2, 2, 4, P]) for d in DD]
        TM = [sb(f"TM{d}", [P, 2, 4, P]) for d in DD]
        NL = [sb(f"NL{d}", [P, LEVELS, 2, P]) for d in DD]
        TS = [sb(f"TS{d}", [P, 2, 2, P]) for d in DD]
        X = [sb(f"X{d}", [P, 2, P]) for d in DD]
        W1 = [sb(f"W1{d}", [P, P]) for d in DD]
        W2 = [sb(f"W2{d}", [P, P]) for d in DD]
        MV = [sb(f"MV{d}", [P, P]) for d in DD]
        U = [sb(f"U{d}", [P, P]) for d in DD]
        S = [sb(f"S{d}", [P, 3, P]) for d in DD]
        Se = [sb(f"Se{d}", [P, P]) for d in DD]
        bX, bT, bS, bR = ([4 * d + n for d in DD] for n in range(4))

        def sig(name):
            return [sg(f"rw_{name}{d}") for d in DD]
        p1, tr, um, tme, nl, ts = sig("p1"), sig("tr"), sig("um"), sig("tme"), sig("nl"), sig("ts")
        xm, xe, tm, wm, we, mve, w2m = sig("xm"), sig("xe"), sig("tm"), sig("wm"), sig("we"), sig("mve"), sig("w2m")
        umm, ue, smm, su, ym, ye, chain = sig("umm"), sig("ue"), sig("smm"), sig("su"), sig("ym"), sig("ye"), sg("dve_chain")
        NLV = LEVELS - 1

        def n_y(d, s):
            return sum(need_ctx or t >= NCT for t in order[d][:s])

        with nc.Block() as block:
            @block.tensor
            def _(pe):
                def carry(d, s, piece):
                    t = order[d][s]
                    b = ps[:, bS[d]]
                    if piece < 4:
                        n = 2 * s + piece // 2
                        c = chunks[d][piece // 2]
                        cs = slice(CH * c, CH * c + CH)
                        if piece % 2 == 0:
                            pe.wait_ge(*su[d].at(n + 1))
                            if piece == 0:
                                pe.wait_ge(*ye[d].at(n_y(d, s)) if n_y(d, s) else su[d].at(n + 1))
                            nc.tensor.matmul(b[cs, 0:P], W1[d][:, cs], S[d][:, n % 3], start=True, stop=True).then_inc(*umm[d].up())
                        else:
                            pe.wait_ge(*ue[d].at(n + 1))
                            nc.tensor.matmul(b[:, P:2 * P], TM[d][cs, s % 2, 1], U[d][cs], start=True, stop=False)
                            nc.tensor.matmul(b[:, P:2 * P], TM[d][cs, s % 2, 2], TM[d][cs, s % 2, 3], start=False, stop=True) \
                                .then_inc(*smm[d].up())
                    elif need_ctx or t >= NCT:
                        pe.wait_ge(*su[d].at(2 * s + 3))
                        o = b[:, 2 * P:3 * P]
                        for q, c in enumerate(chunks[d]):
                            cs = slice(CH * c, CH * c + CH)
                            nc.tensor.matmul(o[:, cs], S[d][:, (2 * s + q) % 3], KR[d][:, 1, t * P + CH * c:t * P + CH * c + CH],
                                             start=(q == 0), stop=False, skip_group_check=True)
                        for h in range(2):
                            hp = slice(HD * h, HD * h + HD)
                            nc.tensor.matmul(o[hp], U[d][:, hp], UM[d][:, s % 2, h, 1], start=False, stop=False, skip_group_check=True)
                            ins = nc.tensor.matmul(o[hp], TM[d][:, s % 2, 3, hp], UM[d][:, s % 2, h, 3], start=False, stop=True,
                                                   skip_group_check=True)
                        ins.then_inc(*ym[d].up())

                for s in range(NT):
                    for d in DD:
                        tt = slice(order[d][s] * P, order[d][s] * P + P)
                        if s:
                            pe.wait_ge(*we[d].at(2 * s))
                            pe.wait_ge(*mve[d].at(s))
                        for h in range(2):
                            hp = slice(HD * h, HD * h + HD)
                            o = ps[:, (bX, bT)[h][d]]
                            nc.tensor.matmul(o[:, 0:256], BK[d][hp, 0, tt], KR[d][hp, :, tt], start=True, stop=True)
                            nc.tensor.matmul(o[:, 256:512], BK[d][hp, 1, tt], KR[d][hp, :, tt], start=True, stop=True).then_inc(*p1[d].up())
                        for a, src in enumerate((KR[d][:, 0, tt], BK[d][:, 0, tt], BK[d][:, 1, tt], M[:, 4 + p, tt])):
                            ins = nc.tensor.transpose(ps[:, bR[d], a * P:(a + 1) * P], src, g.ident)
                        ins.then_inc(*tr[d].up())
                    for v in range(1, LEVELS):
                        for d in DD:
                            pe.wait_ge(*um[d].at(2 * s + 2))
                            pe.wait_ge(*nl[d].at(s * LEVELS + v + 1))
                            pe.wait_ge(*ts[d].at(s * LEVELS + v))
                            for h in range(2):
                                ins = nc.tensor.matmul(ps[:, bX[d], h * P:(h + 1) * P], NL[d][:, v, h], TS[d][:, 0, h], start=True, stop=True)
                            ins.then_inc(*xm[d].up())
                        if s:
                            for d in DD:
                                carry(d, s - 1, v - 1)
                        for d in DD:
                            pe.wait_ge(*xe[d].at(s * NLV + v))
                            if v < LEVELS - 1:
                                for h in range(2):
                                    nc.tensor.matmul(ps[:, bT[d], h * P:(h + 1) * P], TS[d][:, 1, h], X[d][:, h], start=True, stop=True)
                            for h in range(2):
                                ins = nc.tensor.matmul(ps[:, bT[d], (2 + h) * P:(3 + h) * P], X[d][:, h], TS[d][:, 1, h], start=True, stop=True)
                            ins.then_inc(*tm[d].up())
                    for d in DD:
                        pe.wait_ge(*ts[d].at((s + 1) * LEVELS))
                        pe.wait_ge(*tme[d].at(s + 1))
                        for h in range(2):
                            hp = slice(HD * h, HD * h + HD)
                            nc.tensor.matmul(ps[hp, bX[d], 0:P], TM[d][:, s % 2, 0, hp], TS[d][:, 1, h], start=True, stop=True)
                            ins = nc.tensor.matmul(ps[:, bT[d], hp], UM[d][:, s % 2, h, 2], TM[d][:, s % 2, 3, hp], start=True, stop=True)
                        ins.then_inc(*wm[d].up())
                    for d in DD:
                        pe.wait_ge(*mve[d].at(s + 1))
                        for h in range(2):
                            hp = slice(HD * h, HD * h + HD)
                            ins = nc.tensor.matmul(ps[:, bR[d], hp], TS[d][:, 1, h], MV[d][:, hp], start=True, stop=True)
                        ins.then_inc(*w2m[d].up())
                for d in DD:
                    pe.wait_ge(*we[d].at(2 * NT))
                for piece in range(5):
                    for d in DD:
                        carry(d, NT - 1, piece)

            @block.vector
            def _(dve):
                link = linker(dve, chain)

                def carry(d, s, piece):
                    t = order[d][s]
                    b = ps[:, bS[d]]
                    n = 2 * s + piece // 2
                    if piece < 4:
                        c = chunks[d][piece // 2]
                        cs = slice(CH * c, CH * c + CH)
                        e = ET[d][:, 1, 2 * t + c:2 * t + c + 1]
                        if piece % 2 == 0:
                            dve.wait_ge(*su[d].at(n + 1))
                            link(nc.vector.tensor_scalar(Se[d][:], S[d][:, n % 3], e, None, ALU.mult))
                            dve.wait_ge(*umm[d].at(n + 1))
                            dve.wait_ge(*we[d].at(2 * (s + 1)))
                            nc.vector.scalar_tensor_tensor(U[d][cs], b[cs, 0:P], -1.0, W2[d][cs], ALU.mult, ALU.subtract).then_inc(*ue[d].up())
                        else:
                            dve.wait_ge(*smm[d].at(n + 1))
                            for h in range(2):
                                hp = slice(HD * h, HD * h + HD)
                                ins = nc.vector.scalar_tensor_tensor(S[d][hp, (n + 1) % 3, hp], b[hp, P + HD * h:P + HD * h + HD], e[hp],
                                                                     Se[d][hp, hp], ALU.mult, ALU.add)
                            ins.then_inc(*su[d].up())
                    elif need_ctx or t >= NCT:
                        dve.wait_ge(*ym[d].at(n_y(d, s) + 1))
                        y = yT[:, 4 + p, t * P:(t + 1) * P]
                        o = b[:, 2 * P:3 * P]
                        if s < order[1 - d].index(t):
                            nc.vector.tensor_copy(y, o).then_inc(*ye[d].up())
                        else:
                            dve.wait_ge(ye[1 - d].sem, ye[1 - d].made)
                            nc.vector.tensor_tensor(y, y, o, ALU.add).then_inc(*ye[d].up())

                for d in DD:
                    nc.vector.memset(S[d][:], 0.0).then_inc(*su[d].up())
                for s in range(NT):
                    for d in DD:
                        for h in range(2):
                            dve.wait_ge(*p1[d].at(2 * s + h + 1))
                            nc.vector.tensor_tensor(UM[d][:, s % 2, h], ps[:, (bX, bT)[h][d]].rearrange("p (a n) -> p a n", a=4),
                                                    R["masks"][:, d], ALU.mult).then_inc(*um[d].up())
                    for d in DD:
                        dve.wait_ge(*nl[d].at(s * LEVELS + 1))
                        link(nc.vector.tensor_tensor(TS[d][:, 1], NL[d][:, 0], g.ident.unsqueeze(1).broadcast_to([P, 2, P]), ALU.add))
                        nc.vector.transpose(TS[d][:, 0].rearrange("p u n -> p (u n)"), TS[d][:, 1].rearrange("p u n -> p (u n)")) \
                            .then_inc(*ts[d].up())
                    for v in range(1, LEVELS):
                        if s:
                            for d in DD:
                                carry(d, s - 1, v - 1)
                        for d in DD:
                            dve.wait_ge(*tm[d].at(s * NLV + v))
                            dve.wait_ge(*ts[d].at(s * LEVELS + v))
                            a = 0 if v < LEVELS - 1 else 1
                            T2 = TS[d][:, a:2].rearrange("p a u n -> p (a u n)")
                            nc.vector.tensor_tensor(T2, T2, ps[:, bT[d], 2 * P * a:4 * P], ALU.add).then_inc(*ts[d].up())
                    for d in DD:
                        dve.wait_ge(*wm[d].at(s + 1))
                        nc.vector.tensor_copy(MV[d][:], ps[:, bT[d], 0:P]).then_inc(*mve[d].up())
                for piece in range(5):
                    for d in DD:
                        carry(d, NT - 1, piece)

            @block.gpsimd
            def _(pool):
                for s in range(NT):
                    for d in DD:
                        pool.wait_ge(*um[d].at(2 * (s + 1)))
                        if s:
                            pool.wait_ge(*tm[d].at(s * NLV))
                        for v in range(LEVELS):
                            nc.gpsimd.tensor_tensor(NL[d][:, v], UM[d][:, s % 2, :, 0], R["nlev"][:, d, v].unsqueeze(1).broadcast_to([P, 2, P]),
                                                    ALU.mult).then_inc(*nl[d].up())

            @block.scalar
            def _(act):
                for s in range(NT):
                    for d in DD:
                        act.wait_ge(*tr[d].at(s + 1))
                        nc.scalar.copy(TM[d][:, s % 2], ps[:, bR[d]].rearrange("p (a n) -> p a n", a=4)).then_inc(*tme[d].up())
                    for v in range(1, LEVELS):
                        for d in DD:
                            act.wait_ge(*xm[d].at(s * NLV + v))
                            nc.scalar.copy(X[d][:].rearrange("p u n -> p (u n)"), ps[:, bX[d], 0:2 * P]).then_inc(*xe[d].up())
                    for d in DD:
                        act.wait_ge(*wm[d].at(s + 1))
                        nc.scalar.copy(W1[d][:], ps[:, bX[d], 0:P]).then_inc(*we[d].up())
                    for d in DD:
                        act.wait_ge(*w2m[d].at(s + 1))
                        nc.scalar.copy(W2[d][:], ps[:, bR[d], 0:P]).then_inc(*we[d].up())
        sg.settle()


def stage_rwkv_out(nc, g, I, l, R, p, need_ctx):
    sg, ps, M = g.sg, g.ps, R["M"]
    y, r, v = g.yT[:, 4 + p], M[:, p], M[:, 4 + p]
    YC, SQ, RS, RK = R["KR"][0][:, 0], R["KR"][0][:, 1], R["BK"][0][:, 0], R["BK"][0][:, 1]
    vw = views(need_ctx)
    spans = [(s, t0, tw) for s, (t0, tw) in enumerate(SPANS) if need_ctx or s > 0]
    lnd = sg("ln_done")
    mm, ycd, sqd, rkd, rsd, bon, chain = (sg(n) for n in ("mm_done", "normed", "sq_done", "coef", "evac_d", "rw_g", "dve_chain"))
    with nc.Block() as block:
        @block.tensor
        def _(pe):
            def grp(b, lhsT, rhs):
                for s, t0, tw in spans:
                    ins = nc.tensor.matmul(ps[:, b + s, 0:tw], lhsT, rhs[:, t0:t0 + tw], start=True, stop=True)
                ins.then_inc(*mm.up())
            grp(0, g.blk, y)
            pe.wait_ge(*sqd.at(1))
            grp(3, g.blk, SQ)
            pe.wait_ge(*rkd.at(1))
            grp(0, g.blk, RK)
            pe.wait_ge(*rsd.at(1))
            grp(3, R["g2"][:, p * P:(p + 1) * P], M[:, 7])

        @block.scalar
        def _(act):
            act.wait_ge(*ycd.at(1))
            for t0, tw, b in vw:
                ins = nc.scalar.activation(SQ[:, t0:t0 + tw], YC[:, t0:t0 + tw], ACT.Square)
            ins.then_inc(*sqd.up())
            act.wait_ge(*rsd.at(1))
            al = slice(vw[0][0], T)
            nc.scalar.activation(RS[:, al], RS[:, al], ACT.Ln).then_inc(*lnd.up())
            act.wait_ge(*lnd.at(1))
            nc.scalar.activation(RS[:, al], RS[:, al], ACT.Exp, scale=-0.5).then_inc(*g.rq.up())

        @block.vector
        def _(dve):
            link = linker(dve, chain)
            dve.wait_ge(*mm.at(1))
            for t0, tw, b in vw:
                t = slice(t0, t0 + tw)
                ins = nc.vector.scalar_tensor_tensor(YC[:, t], bank(ps, b, tw), -1.0 / HD, y[:, t], ALU.mult, ALU.add)
            ins.then_inc(*ycd.up())
            t0 = vw[0][0]
            al = slice(t0, T)
            nc.vector.scalar_tensor_tensor(RK[:, al], r[:, al], R["rk"][:, p:p + 1], R["KS"][:, al], ALU.mult, ALU.mult).then_inc(*rkd.up())
            dve.wait_ge(*mm.at(2))
            for t0, tw, b in vw:
                ins = nc.vector.tensor_scalar(RS[:, t0:t0 + tw], bank(ps, 3 + b, tw), 1.0 / HD, GN_EPS, ALU.mult, ALU.add)
            ins.then_inc(*rsd.up())
            dve.wait_ge(*rsd.at(1))
            dve.wait_ge(*g.rq.at(1))
            link(nc.vector.scalar_tensor_tensor(YC[:, al], YC[:, al], R["gln"][:, p:p + 1], RS[:, al], ALU.mult, ALU.mult))
            dve.wait_ge(*mm.at(3))
            for t0, tw, b in vw:
                t = slice(t0, t0 + tw)
                link(nc.vector.tensor_tensor(RS[:, t], bank(ps, b, tw), v[:, t], ALU.mult))
            link(nc.vector.tensor_tensor(YC[:, al], YC[:, al], RS[:, al], ALU.add))
            dve.wait_ge(*mm.at(4))
            for t0, tw, b in vw:
                t = slice(t0, t0 + tw)
                nc.vector.tensor_tensor(y[:, t], YC[:, t], bank(ps, 3 + b, tw), ALU.mult)
    sg.settle()


def stage_out(nc, g, I, l, need_ctx):
    sg, ps, yT = g.sg, g.ps, g.yT
    tiles = list(range(0 if need_ctx else NCT, NT))
    with ExitStack() as cx:
        sb = Bufs(nc, cx, f"o{l}")
        w = sb("w", [P, KT, D])
        rows = sb("rows", [P, 2, 3, D])
        gn = sb("gn", [P, D])
        wr = sb("wr", [P, KT, NE])
        br = sb("br", [P, NE])
        xi_ = sb("xi", [P, 2, D])
        xo = sb("xo", [P, 2, D])
        h2 = sb("h2", [P, 2, D])
        hT2 = sb("hT2", [P, KT, P])
        junk = sb("junk", [P, D])
        st = sb("st", [P, 4])
        lg = sb("lg", [P, NE])
        ex = sb("ex", [P, NE])
        w_in, small, x_in, chain = sg("z_in"), sg("small_in"), [sg(f"w_slot{i}") for i in range(2)], sg("dve_chain")
        om, xd, sqd, hd, tr, te = sg("mm_done"), sg("coef"), sg("sq_done"), sg("normed"), sg("transposed"), sg("evac_a")
        lm, lgd, exd, afd, at, ae = sg("ro_lm"), sg("ro_lg"), sg("ro_ex"), sg("ro_aff"), sg("ro_at"), sg("ro_ae")
        xs, hs = [sg(f"out_slot{i}") for i in range(2)], [sg(f"out_slot{2 + i}") for i in range(2)]
        with nc.Block() as block:
            @block.sync
            def _(sp):
                for s in range(2):
                    for n, c in enumerate((2, 3, 4)):
                        sp.dma_start(rows[:, s, n], row(g.mod[l, s, c * D:(c + 1) * D])).then_inc(*small.up(16))
                sp.dma_start(gn[:], row(I["g_norm2"][l])).then_inc(*small.up(16))
                sp.dma_start(wr[:], I["w_router"][l].rearrange("(k p) e -> p k e", p=P)).then_inc(*small.up(16))
                sp.dma_start(br[:], row(I["b_router"][l])).then_inc(*small.up(16))
                sp.dma_start(w[:], I["w_out"][l].rearrange("(k p) f -> p k f", p=P)).then_inc(*w_in.up(16))
                for n, t in enumerate(tiles):
                    if n >= 2:
                        sp.wait_ge(*xd.at(n - 1))
                    sp.dma_start(xi_[:, n % 2], g.x_rows(I, l, t)).then_inc(*x_in[n % 2].up(16))

            @block.gpsimd
            def _(pool):
                for n, t in enumerate(tiles):
                    ts = slice(t * P, (t + 1) * P)
                    pool.wait_ge(*xd.at(n + 1))
                    pool.dma_start(g.x[ts], xo[:, n % 2]).then_inc(*xs[n % 2].up(16))
                    pool.wait_ge(*g.vr.at(n + 1))
                    nc.gpsimd.tensor_tensor(st[:, 1:2], st[:, 1:2], g.mhalf[:, 0:1], ALU.pow).then_inc(*g.rq.up())
                    pool.wait_ge(*hd.at(n + 1))
                    pool.dma_start(g.h2[ts], h2[:, n % 2]).then_inc(*hs[n % 2].up(16))
                for s in xs + hs:
                    pool.wait_ge(s.sem, s.made)

            @block.tensor
            def _(pe):
                pe.wait_ge(*w_in.at(16))
                pe.wait_ge(*small.at(144))

                def proj(n):
                    t = tiles[n]
                    if n >= 2:
                        pe.wait_ge(*xd.at(n - 1))
                    for half in range(2):
                        for k in range(KT):
                            ins = nc.tensor.matmul(ps[:, 2 * (n % 2) + half, :], yT[:, k, t * P:(t + 1) * P], w[:, k, half * 512:(half + 1) * 512],
                                                   start=(k == 0), stop=(k == KT - 1))
                    ins.then_inc(*om.up())
                proj(0)
                for n, t in enumerate(tiles):
                    if n + 1 < len(tiles):
                        proj(n + 1)
                    pe.wait_ge(*hd.at(n + 1))
                    if n >= 1:
                        pe.wait_ge(*te.at(n))
                    for k in range(KT):
                        ins = nc.tensor.transpose(ps[:, 4 + k // 4, (k % 4) * P:(k % 4 + 1) * P], h2[:, n % 2, k * P:(k + 1) * P], g.ident)
                    ins.then_inc(*tr.up())
                    pe.wait_ge(*te.at(n + 1))
                    if n >= 1:
                        pe.wait_ge(*lgd.at(n))
                    for k in range(KT):
                        ins = nc.tensor.matmul(ps[:, 6, 0:NE], hT2[:, k], wr[:, k], start=(k == 0), stop=(k == KT - 1))
                    ins.then_inc(*lm.up())
                    pe.wait_ge(*afd.at(n + 1))
                    if n >= 1:
                        pe.wait_ge(*ae.at(n))
                    nc.tensor.transpose(ps[0:NE, 7, 0:P], ex[:], g.ident).then_inc(*at.up())

            @block.vector
            def _(dve):
                link = linker(dve, chain)
                dve.wait_ge(*small.at(144))
                for s in range(2):
                    link(nc.vector.scalar_tensor_tensor(rows[:, s, 2], rows[:, s, 2], 1.0, gn[:], ALU.add, ALU.mult))
                for n, t in enumerate(tiles):
                    s = 1 if t < NCT else 0
                    dve.wait_ge(*om.at(n + 1))
                    dve.wait_ge(*x_in[n % 2].at(16 * (n // 2 + 1)))
                    if n >= 2:
                        dve.wait_ge(*xs[n % 2].at(16 * (n // 2)))
                    link(nc.vector.tensor_tensor(xo[:, n % 2], bank(ps, 2 * (n % 2), D), rows[:, s, 0], ALU.mult))
                    nc.vector.tensor_tensor(xo[:, n % 2], xo[:, n % 2], xi_[:, n % 2], ALU.add).then_inc(*xd.up())
                    dve.wait_ge(*sqd.at(n + 1))
                    nc.vector.tensor_scalar(st[:, 1:2], st[:, 0:1], 1.0 / D, EPS, ALU.mult, ALU.add).then_inc(*g.vr.up())
                    dve.wait_ge(*g.rq.at(n + 1))
                    if n >= 2:
                        dve.wait_ge(*hs[n % 2].at(16 * (n // 2)))
                    link(nc.vector.scalar_tensor_tensor(h2[:, n % 2], xo[:, n % 2], st[:, 1:2], rows[:, s, 2], ALU.mult, ALU.mult))
                    nc.vector.tensor_tensor(h2[:, n % 2], h2[:, n % 2], rows[:, s, 1], ALU.add).then_inc(*hd.up())
                    dve.wait_ge(*lm.at(n + 1))
                    link(nc.vector.tensor_tensor(lg[:], ps[:, 6, 0:NE], br[:], ALU.add))
                    link(nc.vector.reduce_max(st[:, 2:3], lg[:], AX_X))
                    nc.vector.tensor_scalar(lg[:], lg[:], st[:, 2:3], None, ALU.subtract).then_inc(*lgd.up())
                    dve.wait_ge(*exd.at(n + 1))
                    link(nc.vector.reciprocal(st[:, 3:4], st[:, 3:4]))
                    nc.vector.tensor_scalar(ex[:], ex[:], st[:, 3:4], None, ALU.mult).then_inc(*afd.up())
                    dve.wait_ge(*at.at(n + 1))
                    nc.vector.tensor_copy(g.aff[:, t * P:(t + 1) * P], ps[0:NE, 7, 0:P]).then_inc(*ae.up())

            @block.scalar
            def _(act):
                for n, t in enumerate(tiles):
                    act.wait_ge(*xd.at(n + 1))
                    if n >= 1:
                        act.wait_ge(*sqd.at(n))
                    nc.scalar.activation(junk[:], xo[:, n % 2], ACT.Square, accum_out=st[:, 0:1]).then_inc(*sqd.up())
                    act.wait_ge(*tr.at(n + 1))
                    nc.scalar.copy(hT2[:].rearrange("p k n -> p (k n)"), bank(ps, 4, D)).then_inc(*te.up())
                    act.wait_ge(*lgd.at(n + 1))
                    nc.scalar.activation(ex[:], lg[:], ACT.Exp, accum_out=st[:, 3:4]).then_inc(*exd.up())
        sg.settle()


def stage_topk(nc, g, I, l, need_ctx):
    sg, ps = g.sg, g.ps
    sets = [("x", CTX, SEQ, CAPX)] + ([("c", 0, CTX, CAPC)] if need_ctx else [])
    with ExitStack() as cx:
        sb = Bufs(nc, cx, f"k{l}")
        val = sb("val", [NE, 2, P])
        idx = sb("idx", [NE, 2, P], U32)
        idf = sb("idf", [NE, 2, P])
        zero = sb("zero", [P, D])
        zd, zs, found, tr, chain = sg("coef"), sg("zeroed"), sg("normed"), sg("transposed"), sg("dve_chain")
        with nc.Block() as block:
            @block.vector
            def _(dve):
                link = linker(dve, chain)
                nc.vector.memset(zero[:], 0.0).then_inc(*zd.up())
                for n, (_, t0, tw, cap) in enumerate(sets):
                    a = g.aff[:, t0:t0 + tw]
                    for r in range(cap // 8):
                        v8 = val[:, n, 8 * r:8 * r + 8]
                        link(nc.vector.max(v8, a))
                        link(nc.vector.max_index(idx[:, n, 8 * r:8 * r + 8], v8, a))
                        link(nc.vector.match_replace(a, v8, a, -1.0))
                    link(nc.vector.tensor_copy(idf[:, n, 0:cap], idx[:, n, 0:cap]))
                    nc.vector.tensor_scalar(idf[:, n, 0:cap], idf[:, n, 0:cap], float(t0), None, ALU.add).then_inc(*found.up())
                for n, (_, t0, tw, cap) in enumerate(sets):
                    dve.wait_ge(*tr.at(n + 1))
                    nc.vector.tensor_copy(g.tok[0:cap, n], ps[0:cap, n, 0:NE])
                    nc.vector.tensor_copy(g.gate[0:cap, n], ps[0:cap, n, NE:2 * NE])

            @block.gpsimd
            def _(pool):
                pool.wait_ge(*zd.at(1))
                for t in range(0 if need_ctx else NCT, NT):
                    pool.dma_start(g.acc[t * P:(t + 1) * P], zero[:]).then_inc(*zs.up(16))
                pool.wait_ge(zs.sem, zs.made)

            @block.tensor
            def _(pe):
                for n, (_, t0, tw, cap) in enumerate(sets):
                    pe.wait_ge(*found.at(n + 1))
                    nc.tensor.transpose(ps[0:cap, n, 0:NE], idf[:, n, 0:cap], g.ident[0:NE, 0:NE])
                    nc.tensor.transpose(ps[0:cap, n, NE:2 * NE], val[:, n, 0:cap], g.ident[0:NE, 0:NE]).then_inc(*tr.up())
        sg.settle()


def stage_moe(nc, g, I, l, need_ctx):
    sg, ps = g.sg, g.ps
    sets = [(0, CAPX)] + ([(1, CAPC)] if need_ctx else [])
    passes = [(e, n, cap) for e in range(NE) for n, cap in sets]
    NP, RW = len(passes), 8
    parts = [(e, m, half) for e in range(NE) for m in range(3) for half in range(2)]
    names = ("w_gate", "w_up", "w_down")
    with ExitStack() as cx:
        sb = Bufs(nc, cx, f"e{l}")
        w = sb("w", [P, RW, 4, 1024])
        xe = sb("xe", [P, 2, D])
        xT = sb("xT", [P, KT, P])
        hid = sb("hid", [P, FF])
        hT2 = sb("hT2", [P, KT, P])
        ye = sb("ye", [P, 2, D])
        w_in = [sg(f"w_slot{i}") for i in range(RW)]
        ga, sc, gm, um, dm = sg("moe_gather"), sg("moe_scatter"), sg("moe_gm"), sg("moe_um"), sg("moe_dm")
        xtr, xte, si, hd, htr, hte, yd = (sg(n) for n in ("moe_xtr", "moe_xte", "moe_silu", "moe_hid", "moe_htr", "moe_hte", "moe_ye"))
        with nc.Block() as block:
            @block.sync
            def _(sp):
                for j, (e, m, half) in enumerate(parts):
                    if j >= RW:
                        eo, mo, _ = parts[j - RW]
                        last = (eo + 1) * len(sets)
                        sp.wait_ge(*(gm, um, dm)[mo].at(last))
                    sp.dma_start(w[:, j % RW], I[names[m]][l, e].rearrange("(k p) f -> p k f", p=P)[:, 4 * half:4 * half + 4]) \
                        .then_inc(*w_in[j % RW].up(16))

            @block.gpsimd
            def _(pool):
                def gather(i):
                    e, n, cap = passes[i]
                    if i >= 2:
                        pool.wait_ge(*xtr.at(i - 1))
                    pool.indirect_dma_start(xe[0:cap, i % 2], None, g.h2, bass.IndirectOffsetOnAxis(ap=g.tok[0:cap, n, e:e + 1], axis=0)) \
                        .then_inc(*ga.up(16))
                    pool.wait_ge(*ga.at(16 * (i + 1)))
                gather(0)
                for i, (e, n, cap) in enumerate(passes):
                    if i + 1 < NP:
                        gather(i + 1)
                    pool.wait_ge(*yd.at(i + 1))
                    pool.indirect_dma_start(g.acc, bass.IndirectOffsetOnAxis(ap=g.tok[0:cap, n, e:e + 1], axis=0), ye[0:cap, i % 2], None,
                                            compute_op=ALU.add).then_inc(*sc.up(16))
                    pool.wait_ge(*sc.at(16 * (i + 1)))

            @block.tensor
            def _(pe):
                def slot(e, m, half):
                    j = 6 * e + 2 * m + half
                    return j % RW, 16 * (j // RW + 1)

                def x_transposes(i):
                    e, n, cap = passes[i]
                    pe.wait_ge(*ga.at(16 * (i + 1)))
                    if i >= 1:
                        pe.wait_ge(*hte.at(i))
                    for k in range(KT):
                        ins = nc.tensor.transpose(ps[:, 4 + k // 4, (k % 4) * P:(k % 4) * P + cap], xe[0:cap, i % 2, k * P:(k + 1) * P],
                                                  g.ident[0:cap, 0:cap])
                    ins.then_inc(*xtr.up())
                x_transposes(0)
                for i, (e, n, cap) in enumerate(passes):
                    pe.wait_ge(*xte.at(i + 1))
                    if i >= 1:
                        pe.wait_ge(*hd.at(i))
                    for m in range(2):
                        for half in range(2):
                            s, v = slot(e, m, half)
                            pe.wait_ge(*w_in[s].at(v))
                            for c in range(2):
                                for k in range(4):
                                    kk = 4 * half + k
                                    ins = nc.tensor.matmul(ps[0:cap, 2 * m + c, :], xT[:, kk, 0:cap], w[:, s, k, c * 512:(c + 1) * 512],
                                                           start=(kk == 0), stop=(kk == KT - 1))
                        ins.then_inc(*(gm, um)[m].up())
                    pe.wait_ge(*hd.at(i + 1))
                    for k in range(KT):
                        ins = nc.tensor.transpose(ps[:, 4 + k // 4, (k % 4) * P:(k % 4) * P + cap], hid[0:cap, k * P:(k + 1) * P],
                                                  g.ident[0:cap, 0:cap])
                    ins.then_inc(*htr.up())
                    if i + 1 < NP:
                        x_transposes(i + 1)
                    pe.wait_ge(*hte.at(i + 1))
                    if i >= 1:
                        pe.wait_ge(*yd.at(i))
                    for half in range(2):
                        s, v = slot(e, 2, half)
                        pe.wait_ge(*w_in[s].at(v))
                        for c in range(2):
                            for k in range(4):
                                kk = 4 * half + k
                                ins = nc.tensor.matmul(ps[0:cap, 6 + c, :], hT2[:, kk, 0:cap], w[:, s, k, c * 512:(c + 1) * 512],
                                                       start=(kk == 0), stop=(kk == KT - 1))
                    ins.then_inc(*dm.up())

            def x_copy(act, i):
                cap = passes[i][2]
                act.wait_ge(*xtr.at(i + 1))
                nc.scalar.copy(xT[:, :, 0:cap], bank(ps, 4, D).rearrange("p (k n) -> p k n", k=KT)[:, :, 0:cap]).then_inc(*xte.up())

            @block.scalar
            def _(act):
                for i, (e, n, cap) in enumerate(passes):
                    if i == 0:
                        x_copy(act, 0)
                    act.wait_ge(*gm.at(i + 1))
                    if i >= 1:
                        act.wait_ge(*htr.at(i))
                    nc.scalar.activation(hid[0:cap], bank(ps, 0, FF)[0:cap], ACT.Silu).then_inc(*si.up())
                    act.wait_ge(*htr.at(i + 1))
                    nc.scalar.copy(hT2[:, :, 0:cap], bank(ps, 4, D).rearrange("p (k n) -> p k n", k=KT)[:, :, 0:cap]).then_inc(*hte.up())
                    if i + 1 < NP:
                        x_copy(act, i + 1)

            @block.vector
            def _(dve):
                for i, (e, n, cap) in enumerate(passes):
                    dve.wait_ge(*um.at(i + 1))
                    dve.wait_ge(*si.at(i + 1))
                    nc.vector.tensor_tensor(hid[0:cap], hid[0:cap], bank(ps, 2, FF)[0:cap], ALU.mult).then_inc(*hd.up())
                    dve.wait_ge(*dm.at(i + 1))
                    if i >= 2:
                        dve.wait_ge(*sc.at(16 * (i - 1)))
                    nc.vector.tensor_scalar(ye[0:cap, i % 2], bank(ps, 6, D)[0:cap], g.gate[0:cap, n, e:e + 1], None, ALU.mult).then_inc(*yd.up())
        sg.settle()


def stage_residual(nc, g, I, l, need_ctx):
    sg = g.sg
    tiles = list(range(0 if need_ctx else NCT, NT))
    with ExitStack() as cx:
        sb = Bufs(nc, cx, f"f{l}")
        rows = sb("rows", [P, 2, D])
        xb = sb("xb", [P, 3, D])
        ab = sb("ab", [P, 3, D])
        small, x_in, done, st, chain = sg("small_in"), [sg(f"w_slot{i}") for i in range(3)], sg("normed"), [sg(f"out_slot{i}") for i in range(3)], sg("dve_chain")
        with nc.Block() as block:
            @block.sync
            def _(sp):
                for s in range(2):
                    sp.dma_start(rows[:, s], row(g.mod[l, s, 5 * D:6 * D])).then_inc(*small.up(16))
                for n, t in enumerate(tiles):
                    ts = slice(t * P, (t + 1) * P)
                    if n >= 3:
                        sp.wait_ge(*st[n % 3].at(16 * (n // 3)))
                    sp.dma_start(xb[:, n % 3], g.x[ts]).then_inc(*x_in[n % 3].up(16))
                    sp.dma_start(ab[:, n % 3], g.acc[ts]).then_inc(*x_in[n % 3].up(16))

            @block.vector
            def _(dve):
                link = linker(dve, chain)
                dve.wait_ge(*small.at(32))
                for n, t in enumerate(tiles):
                    dve.wait_ge(*x_in[n % 3].at(32 * (n // 3 + 1)))
                    link(nc.vector.tensor_tensor(ab[:, n % 3], ab[:, n % 3], rows[:, 1 if t < NCT else 0], ALU.mult))
                    nc.vector.tensor_tensor(ab[:, n % 3], ab[:, n % 3], xb[:, n % 3], ALU.add).then_inc(*done.up())

            @block.gpsimd
            def _(pool):
                for n, t in enumerate(tiles):
                    pool.wait_ge(*done.at(n + 1))
                    dst = g.out[0, (t - NCT) * P:(t - NCT + 1) * P] if l == DEPTH - 1 else g.x[t * P:(t + 1) * P]
                    pool.dma_start(dst, ab[:, n % 3]).then_inc(*st[n % 3].up(16))
                for s in st:
                    pool.wait_ge(s.sem, s.made)
        sg.settle()


class Core:
    pass


def build(nc, I, C, out, dbg=None):
    g = Core()
    kind = "Internal"
    def dram(name, shape):
        if dbg is not None and name in dbg:
            return nc.dram_tensor("out_dbg_" + name, shape, F32, kind="ExternalOutput").ap()
        return nc.dram_tensor(name, shape, F32, kind=kind).ap()
    g.mod = dram("mod_rows", [DEPTH, 2, 6 * D])
    g.x = dram("x_rows", [T, D])
    g.h2 = dram("h2_rows", [T, D])
    g.acc = dram("acc_rows", [T, D])
    g.zc = dram("z_cols", [14 * P, T])
    g.zt = dram("z_rows", [T, W_MLA + W_RET])
    g.C, g.out = C, out

    def x_rows(I, l, t):
        if l == 0:
            return I["ctx"][0, t * P:(t + 1) * P] if t < NCT else I["x"][0, (t - NCT) * P:(t - NCT + 1) * P]
        return g.x[t * P:(t + 1) * P]
    g.x_rows = x_rows
    with ExitStack() as ctx:
        g.sg = Signals(ctx, nc)
        fixed = Bufs(nc, ctx, "all")
        g.ps = ctx.enter_context(nc.psum_tensor("ps", [P, 8, 512], F32))
        tabs = fixed("tabs", [P, 3, P])
        g.ident, g.ones, g.blk = tabs[:, 0], tabs[:, 1], tabs[:, 2]
        g.aff = fixed("aff", [NE, T])
        g.tok = fixed("tok", [P, 2, NE], I32)
        g.gate = fixed("gate", [P, 2, NE])
        g.mhalf = fixed("mhalf", [P, 8])
        g.vr, g.rq = g.sg("var_ready"), g.sg("rsqrt_done")
        small = g.sg("small_in")
        with nc.Block() as block:
            @block.vector
            def _(dve):
                nc.vector.memset(g.mhalf[:], -0.5)

            @block.sync
            def _(sp):
                for n, name in enumerate(("ident", "ones", "blk")):
                    sp.dma_start(tabs[:, n], C[name]).then_inc(*small.up(16))
                sp.wait_ge(*small.at(48))
        g.sg.settle()
        stage_modulation(nc, g, I)
        for l in range(DEPTH):
            need_ctx = l < DEPTH - 1
            with ExitStack() as lay:
                hT = lay.enter_context(nc.sbuf_tensor(f"hT{l}", [P, KT, T], F32))
                g.hT = hT
                stage_norm1(nc, g, I, l)
                stage_project(nc, g, I, l)
            with ExitStack() as lay:
                yT = lay.enter_context(nc.sbuf_tensor(f"yT{l}", [P, KT, T], F32))
                g.yT = yT
                stage_conv(nc, g, I, l)
                with ExitStack() as mla:
                    sb = Bufs(nc, mla, f"mla{l}")
                    S = dict(QT=sb("QT", [P, H, T]), KT=sb("KT", [P, H, T]), V=sb("V", [P, NT, H, 65]))
                    stage_mla_prep(nc, g, I, l, S)
                    stage_mla_attend(nc, g, I, l, S, need_ctx)
                stage_retention(nc, g, I, l, need_ctx)
                with ExitStack() as rw:
                    sb = Bufs(nc, rw, f"rw{l}")
                    R = dict(M=sb("M", [P, 8, T]), w0=sb("w0", [P, 2, 2]), a0=sb("a0", [P, 2, 2]), wa2=sb("wa2", [P, 2, GW]),
                             kk=sb("kk", [P, 2]), ka=sb("ka", [P, 2]), oka=sb("oka", [P, 2]), rk=sb("rk", [P, 2]), gln=sb("gln", [P, 2]),
                             g2=sb("g2", [P, GW]), masks=sb("masks", [P, 2, 4, P]),
                             nlev=sb("nlev", [P, 2, LEVELS, P]))
                    stage_rwkv_mix(nc, g, I, l, R)
                    R.update(KR=[sb(f"KR{d}", [P, 2, T]) for d in range(2)], BK=[sb(f"BK{d}", [P, 2, T]) for d in range(2)],
                             ET=[sb(f"ET{d}", [P, 2, T // CH]) for d in range(2)], KS=sb("KS", [P, T]))
                    for p in range(2):
                        with ExitStack() as pr:
                            tb = Bufs(nc, pr, f"rp{l}{p}")
                            R.update((n, tb(n, [P, T])) for n in ("A", "SG", "G", "GX", "E", "KK", "reset"))
                            for d in range(2):
                                stage_rwkv_prep(nc, g, I, l, R, p, d)
                        stage_rwkv_scan(nc, g, I, l, R, p, need_ctx)
                        stage_rwkv_out(nc, g, I, l, R, p, need_ctx)
                stage_out(nc, g, I, l, need_ctx)
            stage_topk(nc, g, I, l, need_ctx)
            stage_moe(nc, g, I, l, need_ctx)
            stage_residual(nc, g, I, l, need_ctx)


_INS = ['x', 'c', 'ctx', 'c_ctx', 'w_ada', 'b_ada', 'g_norm1', 'g_norm2', 'w_in', 'w_out', 'conv_w', 'g_out_conv', 'g_kv_norm',
        'w_uk', 'w_uv', 'g_q_norm', 'g_k_norm', 'g_out_mla', 'rwkv_mu', 'rwkv_w0', 'rwkv_w2', 'rwkv_a0', 'rwkv_a2', 'rwkv_g2',
        'rwkv_k_k', 'rwkv_k_a', 'rwkv_r_k', 'g_ln_x', 'g_ret_norm', 'w_router', 'b_router', 'w_gate', 'w_up', 'w_down']


def kernel(**inputs):
    import numpy as _np
    import concourse.bacc as _bacc
    from concourse import mybir as _mybir
    from concourse.bass_utils import run_bass_kernel_spmd as _run

    nc = _bacc.Bacc("TRN2", target_bir_lowering=False, num_devices=1)
    arrays, I, C = {}, {}, {}
    for name in _INS:
        a = _np.ascontiguousarray(inputs[name])
        arrays[f"in_{name}_dram"] = a
        I[name] = nc.dram_tensor(f"in_{name}_dram", a.shape, _mybir.dt.from_np(a.dtype), kind="ExternalInput").ap()
    for name, a in constants().items():
        arrays[f"const_{name}_dram"] = a
        C[name] = nc.dram_tensor(f"const_{name}_dram", a.shape, _mybir.dt.from_np(a.dtype), kind="ExternalInput").ap()
    out = nc.dram_tensor("out_0_dram", (1, SEQ, D), F32, kind="ExternalOutput").ap()
    build(nc, I, C, out)
    r = _run(nc, [arrays], core_ids=[0])
    return r.results[0]["out_0_dram"]
```

```python
from contextlib import ExitStack

import numpy as np

import concourse.bass as bass
from concourse import mybir

ALU = mybir.AluOpType
ACT = mybir.ActivationFunctionType
F32 = mybir.dt.float32
I32 = mybir.dt.int32
U32 = mybir.dt.uint32
AX_X = mybir.AxisListType.X

P = 128
D = 1024
KT = D // P
CTX, SEQ = 256, 1024
T = CTX + SEQ
NT = T // P
NCT = CTX // P
DEPTH = 2
GRID_W = 64
EPS = 1e-6
GW = 256
HD = 64
H = 4
QK = 96
C_MLA, C_RWKV, C_RET = 768, 1312, 2336
W_MLA, W_RET = 544, 1024
NE, FF = 16, 1024
CAPX, CAPC = 2 * SEQ // NE, 2 * CTX // NE
CH = 64
LEVELS = 6
LWC = -float(np.exp(-0.5))
GN_EPS = 64e-5
SPANS = [(0, 256), (256, 512), (768, 512)]


class Signal:

    def __init__(self, ctx, nc, name):
        self.sem = ctx.enter_context(nc.semaphore(name))
        self.base = 0
        self.made = 0

    def up(self, n=1):
        self.made += n
        return self.sem, n

    def at(self, k):
        return self.sem, self.base + k


class Signals:

    def __init__(self, ctx, nc):
        self.ctx, self.nc, self.by = ctx, nc, {}

    def __call__(self, name):
        if name not in self.by:
            self.by[name] = Signal(self.ctx, self.nc, name)
        return self.by[name]

    def settle(self):
        for s in self.by.values():
            s.base = s.made


def linker(eng, sig):
    def link(ins):
        ins.then_inc(*sig.up())
        eng.wait_ge(sig.sem, sig.made)
    return link




def constants():
    f = np.float32
    i = np.arange(P)
    same = (i[:, None] // CH) == (i[None, :] // CH)
    strict = same & (i[:, None] < i[None, :])
    incl = same & (i[:, None] <= i[None, :])
    masks = np.zeros((P, 2, 4, P), f)
    masks[:, 0] = np.stack([strict, incl, strict, incl], 1)
    masks[:, 1] = np.stack([strict.T, incl.T, strict.T, incl.T], 1)
    nlev = np.zeros((P, 2, LEVELS, P), f)
    for s in range(LEVELS):
        w = 1 << s
        m = ((i[None, :] // w) % 2 == 1) & ((i[:, None] // w) == (i[None, :] // w) - 1)
        nlev[:, 0, s] = -m.astype(f)
        nlev[:, 1, s] = -m.T.astype(f)
    blk = np.zeros((P, P), f)
    blk[:HD, :HD] = 1
    blk[HD:, HD:] = 1
    lg = np.log1p(-np.exp2(-5.0 - np.arange(H)))
    dist = np.abs(i[:, None] - i[None, :])
    sc = HD ** -0.5
    dmat = (np.exp(dist[:, None, :] * lg[None, :, None]) * sc).astype(f)
    head = np.arange(GW) // HD
    xi = np.zeros((P, 2, 2, P), f)
    gdec = np.zeros((P, 2), f)
    for p in range(2):
        g = lg[head[p * P:(p + 1) * P]]
        xi[:, p, 0] = np.exp(g[:, None] * (i[None, :] + 1)) * sc
        xi[:, p, 1] = np.exp(g[:, None] * (P - i[None, :])) * sc
        gdec[:, p] = np.exp(g * P)
    zeta = np.zeros((P, 2, GW), f)
    zeta[:, 0] = np.exp((P - 1 - i)[:, None] * lg[head][None, :])
    zeta[:, 1] = np.exp(i[:, None] * lg[head][None, :])
    reset = np.ones((P, T), f)
    reset[:, ::CH] = 0
    tok = np.arange(SEQ, dtype=f)
    ax = 10000.0 ** (-np.arange(0, 16, 2, dtype=f) / f(16))
    pos = [np.floor(tok / GRID_W), tok % GRID_W]
    rm = np.zeros((SEQ, 2, 2, 2, 8), f)
    for a in range(2):
        ang = (pos[a].astype(f)[:, None] * ax.astype(f)[None, :]).astype(f)
        rm[:, 0, a, :] = np.cos(ang)[:, None]
        rm[:, 1, a, 0] = -np.sin(ang)
        rm[:, 1, a, 1] = np.sin(ang)
    th = (1.0 / (10000.0 ** np.linspace(0.0, 1.0, HD // 2, dtype=f))).astype(f)
    ang = (tok[:, None] * th[None, :]).astype(f)
    rr = np.zeros((SEQ, 2, 2, HD // 2), f)
    rr[:, 0] = np.cos(ang)[:, None]
    rr[:, 1, 0] = -np.sin(ang)
    rr[:, 1, 1] = np.sin(ang)
    out = dict(sel=np.tile(np.eye(32, dtype=f), (4, 1)), ident=np.eye(P, dtype=f), ones=np.ones((P, P), f), blk=blk, masks=masks.reshape(P, -1),
               nlev=nlev.reshape(P, -1), reset=reset, dmat=dmat.reshape(P, -1), xi=xi.reshape(P, -1),
               zeta=zeta.reshape(P, -1), gdec=gdec, rope_m=rm.reshape(SEQ, -1), rope_r=rr.reshape(SEQ, -1))
    return {k: np.ascontiguousarray(v.astype(f)) for k, v in out.items()}


class Bufs:

    def __init__(self, nc, ctx, stage):
        self.nc, self.ctx, self.stage = nc, ctx, stage

    def __call__(self, name, shape, dt=F32):
        return self.ctx.enter_context(self.nc.sbuf_tensor(f"{self.stage}_{name}", shape, dt))


def col(v, n):
    return v.rearrange("(k p) -> p k", k=n)


def row(v):
    return v.partition_broadcast(P)


def stage_modulation(nc, g, I):
    sg, ps = g.sg, g.ps
    NCH = 6 * D // 512
    RW = 4
    with ExitStack() as cx:
        sb = Bufs(nc, cx, "mod")
        cc = sb("cc", [P, KT, 2])
        sc = sb("sc", [P, KT, 2])
        wa = sb("wa", [P, RW, KT, 512])
        ba = sb("ba", [2, DEPTH, 6 * D])
        mo = sb("mo", [2, 6 * D])
        w_in, c_in = [sg(f"w_slot{i}") for i in range(RW)], sg("small_in")
        silu_done, mm, used, stored = sg("silu_done"), sg("mod_mm"), sg("mod_used"), sg("stored")
        jobs = [(l, n) for l in range(DEPTH) for n in range(NCH)]
        with nc.Block() as block:
            @block.sync
            def _(sp):
                with nc.allow_non_contiguous_dma(reason="vectors into columns"):
                    sp.dma_start(cc[:, :, 0], col(I["c"][0], KT)).then_inc(*c_in.up(16))
                    sp.dma_start(cc[:, :, 1], col(I["c_ctx"], KT)).then_inc(*c_in.up(16))
                for l in range(DEPTH):
                    sp.dma_start(ba[:, l, :], I["b_ada"][l].partition_broadcast(2)).then_inc(*c_in.up(16))
                for j, (l, n) in enumerate(jobs):
                    if j >= RW:
                        sp.wait_ge(*mm.at(j - RW + 1))
                    sp.dma_start(wa[:, j % RW], I["w_ada"][l].rearrange("(k p) f -> p k f", p=P)
                                 [:, :, n * 512:(n + 1) * 512]).then_inc(*w_in[j % RW].up(16))

            @block.scalar
            def _(act):
                act.wait_ge(*c_in.at(16 * (2 + DEPTH)))
                nc.scalar.activation(sc[:], cc[:], ACT.Silu).then_inc(*silu_done.up())
                for l in range(DEPTH):
                    act.wait_ge(*used.at((l + 1) * NCH))
                    act.dma_start(g.mod[l], mo[:]).then_inc(*stored.up(16))
                act.wait_ge(*stored.at(16 * DEPTH))

            @block.tensor
            def _(pe):
                pe.wait_ge(*silu_done.at(1))
                for j, (l, n) in enumerate(jobs):
                    pe.wait_ge(*w_in[j % RW].at(16 * (j // RW + 1)))
                    if j >= 4:
                        pe.wait_ge(*used.at(j - 3))
                    for k in range(KT):
                        ins = nc.tensor.matmul(ps[0:2, j % 4, :], sc[:, k, :], wa[:, j % RW, k, :],
                                               start=(k == 0), stop=(k == KT - 1))
                    ins.then_inc(*mm.up())

            @block.vector
            def _(dve):
                dve.wait_ge(*c_in.at(16 * (2 + DEPTH)))
                for j, (l, n) in enumerate(jobs):
                    dve.wait_ge(*mm.at(j + 1))
                    if j == NCH:
                        dve.wait_ge(*stored.at(16))
                    s = slice(n * 512, (n + 1) * 512)
                    nc.vector.tensor_tensor(mo[:, s], ps[0:2, j % 4, :], ba[:, l, s], ALU.add).then_inc(*used.up())
        sg.settle()


def stage_norm1(nc, g, I, l):
    sg, ps, hT = g.sg, g.ps, g.hT
    with ExitStack() as cx:
        sb = Bufs(nc, cx, f"n{l}")
        xb = sb("xb", [P, 3, D])
        xn = sb("xn", [P, 2, D])
        junk = sb("junk", [P, D])
        ss = sb("ss", [P, NT])
        rs = sb("rs", [P, NT])
        mc = sb("mc", [P, 2, 2, KT])
        gn = sb("gn", [P, KT])
        G = sb("G", [P, 2, KT])
        x_in, small, sq, normed = [sg(f"w_slot{i}") for i in range(3)], sg("small_in"), sg("sq_done"), sg("normed")
        tr, ev_a, ev_d, coef, chain = sg("transposed"), sg("evac_a"), sg("evac_d"), sg("coef"), sg("dve_chain")
        with nc.Block() as block:
            @block.sync
            def _(sp):
                with nc.allow_non_contiguous_dma(reason="vectors into columns"):
                    for s in range(2):
                        for w in range(2):
                            sp.dma_start(mc[:, s, w], col(g.mod[l, s, w * D:(w + 1) * D], KT)).then_inc(*small.up(16))
                    sp.dma_start(gn[:], col(I["g_norm1"][l], KT)).then_inc(*small.up(16))
                for t in range(NT):
                    if t >= 3:
                        sp.wait_ge(*normed.at(t - 2))
                    sp.dma_start(xb[:, t % 3], g.x_rows(I, l, t)).then_inc(*x_in[t % 3].up(16))

            def evac_act(act, t):
                act.wait_ge(*tr.at(2 * t + 1))
                s = 1 if t < NCT else 0
                for k in range(4):
                    ins = nc.scalar.activation(hT[:, k, t * P:(t + 1) * P], ps[:, 2 * (t % 2), k * P:(k + 1) * P],
                                               ACT.Identity, bias=mc[:, s, 0, k:k + 1], scale=G[:, s, k:k + 1])
                ins.then_inc(*ev_a.up())

            @block.scalar
            def _(act):
                act.wait_ge(*coef.at(2))
                for t in range(NT):
                    act.wait_ge(*x_in[t % 3].at(16 * (t // 3 + 1)))
                    if t >= 1:
                        act.wait_ge(*sq.at(t))
                    nc.scalar.activation(junk[:], xb[:, t % 3], ACT.Square, accum_out=ss[:, t:t + 1]).then_inc(*sq.up())
                    if t >= 1:
                        evac_act(act, t - 1)
                evac_act(act, NT - 1)

            def evac_dve(dve, t):
                dve.wait_ge(*tr.at(2 * t + 2))
                s = 1 if t < NCT else 0
                for k in range(4, 8):
                    ins = nc.vector.tensor_scalar(hT[:, k, t * P:(t + 1) * P], ps[:, 2 * (t % 2) + 1, (k - 4) * P:(k - 3) * P],
                                                  G[:, s, k:k + 1], mc[:, s, 0, k:k + 1], ALU.mult, ALU.add)
                ins.then_inc(*ev_d.up())

            @block.vector
            def _(dve):
                link = linker(dve, chain)
                dve.wait_ge(*small.at(16 * 5))
                for s in range(2):
                    nc.vector.scalar_tensor_tensor(G[:, s], mc[:, s, 1], 1.0, gn[:], ALU.add, ALU.mult).then_inc(*coef.up())
                dve.wait_ge(*coef.at(2))
                for t in range(NT):
                    dve.wait_ge(*sq.at(t + 1))
                    nc.vector.tensor_scalar(rs[:, t:t + 1], ss[:, t:t + 1], 1.0 / D, EPS, ALU.mult, ALU.add).then_inc(*g.vr.up())
                    dve.wait_ge(*g.rq.at(t + 1))
                    if t >= 2:
                        dve.wait_ge(*tr.at(2 * (t - 1)))
                    nc.vector.tensor_scalar(xn[:, t % 2], xb[:, t % 3], rs[:, t:t + 1], None, ALU.mult).then_inc(*normed.up())
                    if t >= 1:
                        evac_dve(dve, t - 1)
                evac_dve(dve, NT - 1)

            @block.gpsimd
            def _(pool):
                for t in range(NT):
                    pool.wait_ge(*g.vr.at(t + 1))
                    nc.gpsimd.tensor_tensor(rs[:, t:t + 1], rs[:, t:t + 1], g.mhalf[:, 0:1], ALU.pow).then_inc(*g.rq.up())

            @block.tensor
            def _(pe):
                for t in range(NT):
                    pe.wait_ge(*normed.at(t + 1))
                    for half in range(2):
                        if t >= 2:
                            pe.wait_ge(*(ev_d if half else ev_a).at(t - 1))
                        for k in range(4):
                            ins = nc.tensor.transpose(ps[:, 2 * (t % 2) + half, k * P:(k + 1) * P],
                                                      xn[:, t % 2, (4 * half + k) * P:(4 * half + k + 1) * P], g.ident)
                        ins.then_inc(*tr.up())
        sg.settle()


def stage_project(nc, g, I, l, M):
    sg, ps, hT, yT = g.sg, g.ps, g.hT, g.yT
    groups = [(0, 512, "conv", 0), (512, 256, "conv", 4),
              (C_MLA, 272, "tok", 0), (C_MLA + 272, 272, "tok", 272), (C_RET, 512, "tok", W_MLA), (C_RET + 512, 512, "tok", W_MLA + 512),
              (C_RWKV, 512, "rwkv", 0), (C_RWKV + 512, 512, "rwkv", 4)]
    jobs = []
    for n, (c0, w, kind, o) in enumerate(groups):
        if kind == "tok":
            jobs += [(n, t, None) for t in range(NT)]
        else:
            jobs += [(n, m, s) for m in range(w // P) for s in range(3)]
    lastjob = [max(j for j, x in enumerate(jobs) if x[0] == n) for n in range(len(groups))]
    tok0 = lastjob[1] + 1
    rw0 = lastjob[5] + 1
    NB, RW, RO = 6, 3, 6
    SQ_AT, SUM_AT, SUM2_AT = 14, 18, 24
    with ExitStack() as cx:
        sb = Bufs(nc, cx, f"p{l}")
        w = sb("w", [P, RW, KT, 512])
        zo = sb("zo", [P, RO, 512])
        z = sb("z", [P, 2, T + 4])
        tmp = sb("tmp", [P, T + 2])
        mu, hmu, omu = sb("mu", [P, 8]), sb("hmu", [P, 8]), sb("omu", [P, 8])
        cw, go = sb("cw", [P, 3, 2]), sb("go", [P, 2])
        w_in = [sg(f"w_slot{i}") for i in range(RW)]
        st = [sg(f"out_slot{i}") for i in range(RO)]
        mm, ev, small, chain = sg("mm_done"), [sg("evac_a"), sg("evac_d")], sg("small_in"), sg("dve_chain")
        pad, prod, sqd, csum, vard, lnd, mixed = (sg(n) for n in ("coef", "cv_prod", "sq_done", "cv_sum", "cv_var", "ln_done", "mixed"))

        def tile_of(j):
            return groups[jobs[j][0]][3] + jobs[j][1]

        def target(j):
            n, m, s = jobs[j]
            kind, o = groups[n][2], groups[n][3]
            if kind == "tok":
                return zo[:, (j - tok0) % RO, 0:groups[n][1]], groups[n][1]
            t0, tw = SPANS[s]
            if kind == "conv":
                return M[:, o + m, t0:t0 + tw], tw
            a = t0 + (1 if t0 < CTX else 3)
            return z[:, (o + m) % 2, a:a + tw], tw

        def wait_target(eng, j):
            if j >= rw0:
                if tile_of(j) >= 2:
                    eng.wait_ge(*mixed.at(tile_of(j) - 1))
                else:
                    eng.wait_ge(*vard.at(2))
            elif j >= tok0 + RO:
                k = j - tok0
                eng.wait_ge(*st[k % RO].at(16 * (k // RO)))

        with nc.Block() as block:
            @block.sync
            def _(sp):
                for n, (c0, wd, kind, o) in enumerate(groups):
                    if n >= RW:
                        sp.wait_ge(*mm.at(lastjob[n - RW] + 1))
                    sp.dma_start(w[:, n % RW, :, 0:wd], I["w_in"][l].rearrange("(k p) f -> p k f", p=P)[:, :, c0:c0 + wd]) \
                        .then_inc(*w_in[n % RW].up(16))
                    if n == 1:
                        with nc.allow_non_contiguous_dma(reason="vectors into columns"):
                            sp.dma_start(mu[:], col(I["rwkv_mu"][l], 8)).then_inc(*small.up(16))
                            for i in range(3):
                                sp.dma_start(cw[:, i], col(I["conv_w"][l, i], 2)).then_inc(*small.up(16))
                            sp.dma_start(go[:], col(I["g_out_conv"][l], 2)).then_inc(*small.up(16))

            @block.tensor
            def _(pe):
                def squares_sum(s, b):
                    t0, tw = SPANS[s]
                    for i in range(2):
                        ins = nc.tensor.matmul(ps[:, b, 0:tw], g.ones, M[:, 4 + i, t0:t0 + tw], start=(i == 0), stop=(i == 1))
                    ins.then_inc(*csum.up())

                for j, (n, m, s) in enumerate(jobs):
                    if j == 0 or jobs[j - 1][0] != n:
                        pe.wait_ge(*w_in[n % RW].at(16 * (n // RW + 1)))
                    if j >= NB:
                        pe.wait_ge(*ev[j % 2].at((j - NB) // 2 + 1))
                    wd = groups[n][1]
                    for k in range(KT):
                        if s is not None:
                            t0, tw = SPANS[s]
                            ins = nc.tensor.matmul(ps[:, j % NB, 0:tw], w[:, n % RW, k, m * P:(m + 1) * P], hT[:, k, t0:t0 + tw],
                                                   start=(k == 0), stop=(k == KT - 1))
                        else:
                            ins = nc.tensor.matmul(ps[:, j % NB, 0:wd], hT[:, k, m * P:(m + 1) * P], w[:, n % RW, k, 0:wd],
                                                   start=(k == 0), stop=(k == KT - 1))
                    ins.then_inc(*mm.up())
                    if j == tok0 + SUM_AT:
                        pe.wait_ge(*sqd.at(2))
                        squares_sum(0, 6)
                        squares_sum(1, 7)
                    if j == tok0 + SUM2_AT:
                        pe.wait_ge(*vard.at(1))
                        squares_sum(2, 6)

            @block.scalar
            def _(act):
                for j in range(0, len(jobs), 2):
                    act.wait_ge(*mm.at(j + 1))
                    wait_target(act, j)
                    dst, wd = target(j)
                    nc.scalar.copy(dst, ps[:, j % NB, 0:wd]).then_inc(*ev[0].up())
                    if j == tok0 + SQ_AT:
                        for i in range(2):
                            act.wait_ge(*prod.at(i + 1))
                            nc.scalar.activation(M[:, 4 + i], M[:, 2 + i], ACT.Square).then_inc(*sqd.up())
                    if j == tok0 + SUM2_AT + 4:
                        act.wait_ge(*vard.at(2))
                        nc.scalar.activation(M[:, 0], M[:, 0], ACT.Ln).then_inc(*lnd.up())
                        act.wait_ge(*lnd.at(1))
                        nc.scalar.activation(M[:, 0], M[:, 0], ACT.Exp, scale=-0.5).then_inc(*g.rq.up())
                act.wait_ge(*mixed.at(7))
                nc.scalar.activation(M[0:64, 6], M[0:64, 6], ACT.Tanh)
                act.wait_ge(*mixed.at(8))
                nc.scalar.activation(M[:, 7], M[:, 7], ACT.Sigmoid)

            @block.vector
            def _(dve):
                link = linker(dve, chain)

                def conv(n):
                    i, part = divmod(n, 5)
                    u, y = z[:, i], M[:, 2 + i]
                    if part == 0:
                        if i == 0:
                            dve.wait_ge(*ev[0].at(tok0 // 2))
                            dve.wait_ge(*ev[1].at(tok0 // 2))
                            dve.wait_ge(*small.at(80))
                        link(nc.vector.tensor_tensor(u[:, 1:CTX + 1], M[:, 2 + i, 0:CTX], M[:, 4 + i, 0:CTX], ALU.mult))
                        link(nc.vector.tensor_tensor(u[:, CTX + 3:T + 3], M[:, 2 + i, CTX:T], M[:, 4 + i, CTX:T], ALU.mult))
                    elif part < 4:
                        for a, b, o in ((0, CTX, part - 1), (CTX, T, part + 1)):
                            if part == 1:
                                ins = nc.vector.tensor_scalar(y[:, a:b], u[:, a + o:b + o], cw[:, 0, i:i + 1], None, ALU.mult)
                            else:
                                ins = nc.vector.scalar_tensor_tensor(y[:, a:b], u[:, a + o:b + o], cw[:, part - 1, i:i + 1], y[:, a:b],
                                                                     ALU.mult, ALU.add)
                            link(ins)
                    else:
                        nc.vector.tensor_tensor(y, y, M[:, i], ALU.mult).then_inc(*prod.up())

                def variance(spans, b):
                    for s in spans:
                        t0, tw = SPANS[s]
                        dve.wait_ge(*csum.at(s + 1))
                        ins = nc.vector.tensor_scalar(M[:, 0, t0:t0 + tw], ps[:, 6 + s % 2, 0:tw], 1.0 / GW, EPS, ALU.mult, ALU.add)
                    ins.then_inc(*vard.up())

                def mix(i):
                    zz = z[:, i % 2]
                    last = rw0 + 3 * i + 2
                    for j in (last, last - 1):
                        dve.wait_ge(*ev[j % 2].at(j // 2 + 1))
                    link(nc.vector.tensor_tensor(tmp[:], zz[:, 0:T + 2], zz[:, 2:T + 4], ALU.add))
                    link(nc.vector.tensor_scalar(tmp[:], tmp[:], hmu[:, i:i + 1], None, ALU.mult))
                    link(nc.vector.scalar_tensor_tensor(M[:, i, 0:CTX], zz[:, 1:CTX + 1], omu[:, i:i + 1], tmp[:, 0:CTX], ALU.mult, ALU.add))
                    nc.vector.scalar_tensor_tensor(M[:, i, CTX:T], zz[:, CTX + 3:T + 3], omu[:, i:i + 1], tmp[:, CTX + 2:T + 2],
                                                   ALU.mult, ALU.add).then_inc(*mixed.up())
                    dve.wait_ge(*mixed.at(i + 1))

                link(nc.vector.memset(z[:], 0.0))
                for j in range(1, len(jobs), 2):
                    dve.wait_ge(*mm.at(j + 1))
                    wait_target(dve, j)
                    dst, wd = target(j)
                    nc.vector.tensor_copy(dst, ps[:, j % NB, 0:wd]).then_inc(*ev[1].up())
                    k = (j - tok0) // 2
                    if j > tok0 and k < 5:
                        conv(2 * k)
                        conv(2 * k + 1)
                    if j == tok0 + SUM_AT + 1:
                        variance((0, 1), 6)
                    if j == tok0 + SUM2_AT + 1:
                        variance((2,), 6)
                        link(nc.vector.tensor_scalar(hmu[:], mu[:], 0.5, None, ALU.mult))
                        link(nc.vector.tensor_scalar(omu[:], mu[:], -1.0, 1.0, ALU.mult, ALU.add))
                    if j == tok0 + SUM2_AT + 7:
                        dve.wait_ge(*g.rq.at(1))
                        for i in range(2):
                            ins = nc.vector.scalar_tensor_tensor(yT[:, i], M[:, 2 + i], go[:, i:i + 1], M[:, 0], ALU.mult, ALU.mult)
                            link(ins)
                    if j >= rw0 and tile_of(j) >= 1 and (j + 2 >= len(jobs) or tile_of(j + 2) > tile_of(j)):
                        mix(tile_of(j) - 1)
                mix(7)

            @block.gpsimd
            def _(pool):
                for j in range(tok0, rw0):
                    n, t, _ = jobs[j]
                    pool.wait_ge(*ev[j % 2].at(j // 2 + 1))
                    o, wd = groups[n][3], groups[n][1]
                    pool.dma_start(g.zt[t * P:(t + 1) * P, o:o + wd], zo[:, (j - tok0) % RO, 0:wd]).then_inc(*st[(j - tok0) % RO].up(16))
                for s in st:
                    pool.wait_ge(s.sem, s.made)
        sg.settle()


def stage_mla_prep(nc, g, I, l, S):
    sg, ps = g.sg, g.ps
    QT, KTr, V = S["QT"], S["KT"], S["V"]
    with ExitStack() as cx:
        sb = Bufs(nc, cx, f"m{l}")
        z = sb("z", [P, 3, W_MLA])
        rope = sb("rope", [P, SEQ // P, 2, 32])
        wkv = sb("wkv", [P, 512])
        gkv = sb("gkv", [P, 1])
        gqk = sb("gqk", [P, 2, QK])
        junk = sb("junk", [P, P])
        st = sb("st", [P, NT, 2])
        cn = sb("cn", [P, P])
        cT = sb("cT", [P, P])
        qk = sb("qk", [P, 2, 8, QK])
        sq = sb("sq", [P, 8, QK])
        s8 = sb("s8", [P, 8])
        ra = sb("ra", [P, 8, 32])
        rb = sb("rb", [P, 8, 32])
        z_in, small, chain = [sg(f"w_slot{i}") for i in range(3)], sg("small_in"), sg("dve_chain")
        sqd, cnd, ctd, cte, kvd, gath = sg("sq_done"), sg("normed"), sg("mla_ct"), sg("mla_cte"), sg("mm_done"), sg("mla_gath")
        kvr, qkd, tr, ev_a, ev_d = sg("mla_kvr"), sg("mla_qk"), sg("transposed"), sg("evac_a"), sg("evac_d")
        with nc.Block() as block:
            @block.sync
            def _(sp):
                sp.dma_start(wkv[:, 0:GW], I["w_uk"][l]).then_inc(*small.up(16))
                sp.dma_start(wkv[:, GW:2 * GW], I["w_uv"][l]).then_inc(*small.up(16))
                with nc.allow_non_contiguous_dma(reason="vectors into columns"):
                    sp.dma_start(gkv[:], col(I["g_kv_norm"][l], 1)).then_inc(*small.up(16))
                sp.dma_start(gqk[:, 0], row(I["g_q_norm"][l])).then_inc(*small.up(16))
                sp.dma_start(gqk[:, 1], row(I["g_k_norm"][l])).then_inc(*small.up(16))
                sp.dma_start(rope[:], g.C["rope_m"].rearrange("(t p) (c f) -> p t c f", p=P, c=2)).then_inc(*small.up(16))
                for t in range(NT):
                    if t >= 3:
                        sp.wait_ge(*gath.at(t - 2))
                    sp.dma_start(z[:, t % 3], g.zt[t * P:(t + 1) * P, 0:W_MLA]).then_inc(*z_in[t % 3].up(16))

            @block.scalar
            def _(act):
                act.wait_ge(*small.at(96))
                for t in range(NT):
                    zz = z[:, t % 3]
                    act.wait_ge(*z_in[t % 3].at(16 * (t // 3 + 1)))
                    if t >= 1:
                        act.wait_ge(*sqd.at(t))
                    nc.scalar.activation(junk[:], zz[:, 384:512], ACT.Square, accum_out=st[:, t, 0:1]).then_inc(*sqd.up())
                    if t >= 2:
                        act.wait_ge(*tr.at(2 * (t - 1)))
                    q = qk[:, t % 2]
                    nc.scalar.copy(q[:, 0:4, 0:64], zz[:, 0:256].rearrange("p (h d) -> p h d", h=4))
                    nc.scalar.copy(q[:, 0:4, 64:96], zz[:, 256:384].rearrange("p (h d) -> p h d", h=4))
                    act.wait_ge(*cnd.at(t + 1))
                    nc.scalar.copy(q[:, 4:8, 64:96], zz[:, 512:544].unsqueeze(1).broadcast_to([P, 4, 32])).then_inc(*gath.up())
                    act.wait_ge(*ctd.at(t + 1))
                    nc.scalar.activation(cT[:], ps[:, 0, 0:P], ACT.Copy, scale=gkv[:, 0:1]).then_inc(*cte.up())
                    act.wait_ge(*kvd.at(t + 1))
                    nc.scalar.copy(q[:, 4:8, 0:64], ps[:, 1, 0:256].rearrange("p (h d) -> p h d", h=4))
                    nc.scalar.copy(V[:, t, :, 0:64], ps[:, 1, 256:512].rearrange("p (h d) -> p h d", h=4)).then_inc(*kvr.up())
                    act.wait_ge(*tr.at(2 * t + 1))
                    nc.scalar.copy(QT[0:QK, :, t * P:(t + 1) * P], ps[0:QK, 2, :].rearrange("p (h d) -> p h d", h=4)).then_inc(*ev_a.up())

            @block.vector
            def _(dve):
                link = linker(dve, chain)
                link(nc.vector.memset(V[:, :, :, 64:65], 1.0))
                link(nc.vector.memset(KTr[QK:QK + 1], 1.0))
                dve.wait_ge(*small.at(96))
                for t in range(NT):
                    zz, q = z[:, t % 3], qk[:, t % 2]
                    dve.wait_ge(*sqd.at(t + 1))
                    nc.vector.tensor_scalar(st[:, t, 1:2], st[:, t, 0:1], 1.0 / P, EPS, ALU.mult, ALU.add).then_inc(*g.vr.up())
                    dve.wait_ge(*g.rq.at(2 * t + 1))
                    if t >= 1:
                        dve.wait_ge(*ctd.at(t))
                    nc.vector.tensor_scalar(cn[:], zz[:, 384:512], st[:, t, 1:2], None, ALU.mult).then_inc(*cnd.up())
                    dve.wait_ge(*kvr.at(t + 1))
                    link(nc.vector.tensor_tensor(sq[:], q, q, ALU.mult))
                    link(nc.vector.tensor_reduce(s8[:], sq[:], AX_X, ALU.add))
                    nc.vector.tensor_scalar(s8[:], s8[:], 1.0 / QK, EPS, ALU.mult, ALU.add).then_inc(*g.vr.up())
                    dve.wait_ge(*g.rq.at(2 * t + 2))
                    link(nc.vector.tensor_tensor(q, q, s8[:].unsqueeze(2).broadcast_to([P, 8, QK]), ALU.mult))
                    for i in range(2):
                        link(nc.vector.tensor_tensor(q[:, 4 * i:4 * i + 4], q[:, 4 * i:4 * i + 4],
                                                     gqk[:, i].unsqueeze(1).broadcast_to([P, 4, QK]), ALU.mult))
                    if t >= NCT:
                        r = rope[:, t - NCT]
                        link(nc.vector.tensor_tensor(ra[:], q[:, :, 64:96], r[:, 0].unsqueeze(1).broadcast_to([P, 8, 32]), ALU.mult))
                        q5 = q[:, :, 64:96].rearrange("p h (a s f) -> p h a s f", a=2, s=2)
                        b5 = rb[:].rearrange("p h (a s f) -> p h a s f", a=2, s=2)
                        r5 = r[:, 1].rearrange("p (a s f) -> p a s f", a=2, s=2)
                        for s in range(2):
                            link(nc.vector.tensor_tensor(b5[:, :, :, s], q5[:, :, :, 1 - s],
                                                         r5[:, :, s].unsqueeze(1).broadcast_to([P, 8, 2, 8]), ALU.mult))
                        link(nc.vector.tensor_tensor(q[:, :, 64:96], ra[:], rb[:], ALU.add))
                    nc.vector.tensor_copy(s8[0:1, 0:1], s8[0:1, 0:1]).then_inc(*qkd.up())
                    dve.wait_ge(*tr.at(2 * t + 2))
                    nc.vector.tensor_copy(KTr[0:QK, :, t * P:(t + 1) * P], ps[0:QK, 3, :].rearrange("p (h d) -> p h d", h=4)).then_inc(*ev_d.up())

            @block.gpsimd
            def _(pool):
                for t in range(NT):
                    pool.wait_ge(*g.vr.at(2 * t + 1))
                    nc.gpsimd.tensor_tensor(st[:, t, 1:2], st[:, t, 1:2], g.mhalf[:, 0:1], ALU.pow).then_inc(*g.rq.up())
                    pool.wait_ge(*g.vr.at(2 * t + 2))
                    nc.gpsimd.tensor_tensor(s8[:], s8[:], g.mhalf[:, 0:8], ALU.pow).then_inc(*g.rq.up())

            @block.tensor
            def _(pe):
                for t in range(NT):
                    pe.wait_ge(*cnd.at(t + 1))
                    if t >= 1:
                        pe.wait_ge(*cte.at(t))
                    nc.tensor.transpose(ps[:, 0, 0:P], cn[:], g.ident).then_inc(*ctd.up())
                    pe.wait_ge(*cte.at(t + 1))
                    if t >= 1:
                        pe.wait_ge(*kvr.at(t))
                    nc.tensor.matmul(ps[:, 1, :], cT[:], wkv[:], start=True, stop=True).then_inc(*kvd.up())
                    pe.wait_ge(*qkd.at(t + 1))
                    for i in range(2):
                        if t >= 1:
                            pe.wait_ge(*(ev_d if i else ev_a).at(t))
                        for h in range(4):
                            ins = nc.tensor.transpose(ps[0:QK, 2 + i, h * P:(h + 1) * P], qk[:, t % 2, 4 * i + h], g.ident)
                        ins.then_inc(*tr.up())
        sg.settle()


def stage_mla_attend(nc, g, I, l, S, need_ctx):
    sg, ps, yT = g.sg, g.ps, g.yT
    QT, KTr, V = S["QT"], S["KT"], S["V"]
    SCALE = QK ** -0.5
    groups = ([(0, CTX, NCT)] if need_ctx else []) + [(CTX, 512, NT), (CTX + 512, 512, NT)]
    NP = 3
    with ExitStack() as cx:
        sb = Bufs(nc, cx, f"a{l}")
        mx = sb("mx", [P, 2, H])
        pt = sb("pt", [P, NP, 512])
        ot = sb("ot", [65, H, 512])
        o = sb("o", [P, GW])
        on = sb("on", [P, 2, GW])
        junk = sb("junk", [P, GW])
        rc = sb("rc", [P, H])
        ss = sb("ss", [P, 2])
        go = sb("go", [P, 2])
        small, chain = sg("small_in"), sg("dve_chain")
        sc, mxd, mt, mrow = sg("at_sc"), sg("at_mx"), sg("at_mt"), sg("at_mrow")
        st, ex, pv, ote = sg("at_st"), sg("at_ex"), sg("at_pv"), sg("at_ote")
        otr, od, sqd, ond, ytr, ye = sg("at_otr"), sg("at_od"), sg("sq_done"), sg("normed"), sg("transposed"), sg("evac_a")
        with nc.Block() as block:
            @block.sync
            def _(sp):
                with nc.allow_non_contiguous_dma(reason="vectors into columns"):
                    sp.dma_start(go[:], col(I["g_out_mla"][l], 2)).then_inc(*small.up(16))

            @block.tensor
            def _(pe):
                nsc = nst = nq = nh = 0
                for q0, qw, nk in groups:
                    keys = nk * P
                    if nq:
                        pe.wait_ge(*ye.at(nq))
                    for qt in range(qw // P):
                        qs = slice(q0 + qt * P, q0 + (qt + 1) * P)
                        for h in range(H):
                            if nsc >= 2:
                                pe.wait_ge(*mxd.at(nsc - 1))
                            b = 3 * (nsc % 2)
                            for n in range(0, keys, 512):
                                kw = min(512, keys - n)
                                ins = nc.tensor.matmul(ps[:, b + n // 512, 0:kw], QT[0:QK, h, qs], KTr[0:QK, h, n:n + kw],
                                                       start=True, stop=True)
                            ins.then_inc(*sc.up())
                            nsc += 1
                        pe.wait_ge(*mxd.at(nsc))
                        if nq >= 1:
                            pe.wait_ge(*mrow.at(nq))
                        for h in range(H):
                            ins = nc.tensor.matmul(ps[96:97, 6, h * P:(h + 1) * P], mx[:, nq % 2, h:h + 1], g.ident,
                                                   start=True, stop=True)
                        ins.then_inc(*mt.up())
                        nq += 1
                    pe.wait_ge(*mrow.at(nq))
                    for h in range(H):
                        def scores_t(kt):
                            n = nst + kt
                            if n >= 4:
                                pe.wait_ge(*ex.at(n - 3))
                            nc.tensor.matmul(ps[:, n % 4, 0:qw], KTr[0:QK + 1, h, kt * P:(kt + 1) * P],
                                             QT[0:QK + 1, h, q0:q0 + qw], start=True, stop=True).then_inc(*st.up())
                        for kt in range(min(2, nk)):
                            scores_t(kt)
                        for kt in range(nk):
                            if kt + 2 < nk:
                                scores_t(kt + 2)
                            pe.wait_ge(*ex.at(nst + kt + 1))
                            if kt == 0 and nh >= 2:
                                pe.wait_ge(*ote.at(nh - 1))
                            nc.tensor.matmul(ps[0:65, 4 + nh % 2, 0:qw], V[:, kt, h], pt[:, (nst + kt) % NP, 0:qw],
                                             start=(kt == 0), stop=(kt == nk - 1)).then_inc(*pv.up())
                        nst += nk
                        nh += 1
                    pe.wait_ge(*ote.at(nh))
                    for qt in range(qw // P):
                        n = nq - qw // P + qt
                        if n >= 1:
                            pe.wait_ge(*od.at(n))
                        for h in range(H):
                            ins = nc.tensor.transpose(ps[:, 7, h * 65:(h + 1) * 65], ot[:, h, qt * P:(qt + 1) * P], g.ident[0:65, 0:65])
                        ins.then_inc(*otr.up())
                        pe.wait_ge(*ond.at(n + 1))
                        if n >= 1:
                            pe.wait_ge(*ye.at(n))
                        for i in range(2):
                            ins = nc.tensor.transpose(ps[:, 6, i * P:(i + 1) * P], on[:, n % 2, i * P:(i + 1) * P], g.ident)
                        ins.then_inc(*ytr.up())

            @block.gpsimd
            def _(pool):
                for n in range(sum(qw // P for _, qw, _ in groups)):
                    pool.wait_ge(*g.vr.at(n + 1))
                    nc.gpsimd.tensor_tensor(ss[:, 1:2], ss[:, 1:2], g.mhalf[:, 0:1], ALU.pow).then_inc(*g.rq.up())

            @block.vector
            def _(dve):
                link = linker(dve, chain)
                nsc = nq = 0
                for q0, qw, nk in groups:
                    keys = nk * P
                    for qt in range(qw // P):
                        for h in range(H):
                            dve.wait_ge(*sc.at(nsc + 1))
                            if h == 0 and nq >= 2:
                                dve.wait_ge(*mt.at(nq - 1))
                            b = 3 * (nsc % 2)
                            src = ps[:, b:b + 3, :].rearrange("p b n -> p (b n)")[:, 0:keys]
                            nc.vector.reduce_max(mx[:, nq % 2, h:h + 1], src, AX_X).then_inc(*mxd.up())
                            nsc += 1
                        nq += 1
                    for qt in range(qw // P):
                        n = nq - qw // P + qt
                        dve.wait_ge(*otr.at(n + 1))
                        pss = ps[:, 7, 0:260].rearrange("p (h d) -> p h d", h=H)
                        link(nc.vector.reciprocal(rc[:], pss[:, :, 64]))
                        nc.vector.tensor_tensor(o[:].rearrange("p (h d) -> p h d", h=H), pss[:, :, 0:64],
                                                rc[:].unsqueeze(2).broadcast_to([P, H, 64]), ALU.mult).then_inc(*od.up())
                        dve.wait_ge(*sqd.at(n + 1))
                        nc.vector.tensor_scalar(ss[:, 1:2], ss[:, 0:1], 1.0 / GW, EPS, ALU.mult, ALU.add).then_inc(*g.vr.up())
                        dve.wait_ge(*g.rq.at(n + 1))
                        if n >= 2:
                            dve.wait_ge(*ytr.at(n - 1))
                        nc.vector.tensor_scalar(on[:, n % 2], o[:], ss[:, 1:2], None, ALU.mult).then_inc(*ond.up())

            @block.scalar
            def _(act):
                act.wait_ge(*small.at(16))
                nq = nst = nh = 0
                for q0, qw, nk in groups:
                    for qt in range(qw // P):
                        act.wait_ge(*mt.at(nq + 1))
                        nc.scalar.activation(QT[96:97, :, q0 + qt * P:q0 + (qt + 1) * P],
                                             ps[96:97, 6, :].rearrange("p (h d) -> p h d", h=H), ACT.Copy, scale=-1.0).then_inc(*mrow.up())
                        nq += 1
                    for h in range(H):
                        for kt in range(nk):
                            act.wait_ge(*st.at(nst + 1))
                            if nst >= NP:
                                act.wait_ge(*pv.at(nst - NP + 1))
                            nc.scalar.activation(pt[:, nst % NP, 0:qw], ps[:, nst % 4, 0:qw], ACT.Exp, scale=SCALE).then_inc(*ex.up())
                            nst += 1
                        act.wait_ge(*pv.at(nst))
                        nc.scalar.copy(ot[:, h, 0:qw], ps[0:65, 4 + nh % 2, 0:qw]).then_inc(*ote.up())
                        nh += 1
                    for qt in range(qw // P):
                        n = nq - qw // P + qt
                        act.wait_ge(*od.at(n + 1))
                        if n >= 1:
                            act.wait_ge(*sqd.at(n))
                        nc.scalar.activation(junk[:], o[:], ACT.Square, accum_out=ss[:, 0:1]).then_inc(*sqd.up())
                        act.wait_ge(*ytr.at(n + 1))
                        for i in range(2):
                            ins = nc.scalar.activation(yT[:, 2 + i, q0 + qt * P:q0 + (qt + 1) * P], ps[:, 6, i * P:(i + 1) * P],
                                                       ACT.Copy, scale=go[:, i:i + 1])
                        ins.then_inc(*ye.up())
        sg.settle()


def stage_retention(nc, g, I, l, need_ctx):
    sg, ps, yT = g.sg, g.ps, g.yT
    t_first = 0 if need_ctx else NCT
    with ExitStack() as cx:
        sb = Bufs(nc, cx, f"r{l}")
        z = sb("z", [P, 2, W_RET])
        rope = sb("rope", [P, 2, 2, HD])
        ra = sb("ra", [P, 8, HD])
        rb = sb("rb", [P, 8, HD])
        qk = sb("qk", [P, 2, 8, HD])
        QT = sb("QT", [P, 4, T])
        QX = sb("QX", [P, 2, 2, T])
        kz = sb("kz", [P, 2, GW])
        V = sb("V", [P, NT, GW])
        G = sb("G", [P, NT, GW])
        R = sb("R", [P, NT, 4, P])
        St = sb("St", [P, 2, 2, P])
        dm = sb("dm", [P, H, P])
        xi = sb("xi", [P, 2, 2, P])
        ze = sb("ze", [P, 2, GW])
        gd = sb("gd", [P, 2])
        pt = sb("pt", [P, H, P])
        o = sb("o", [P, GW])
        sq = sb("sq", [P, GW])
        s4 = sb("s4", [P, H])
        on = sb("on", [P, GW])
        gr = sb("gr", [P, GW])
        z_in, small, chain = [sg(f"w_slot{i}") for i in range(2)], sg("small_in"), sg("dve_chain")
        qkd, tr, ev_a, ev_d, zd, gd_s = sg("normed"), sg("transposed"), sg("evac_a"), sg("evac_d"), sg("rt_zd"), sg("rt_g")
        kzd, rm, rev = sg("rt_kz"), sg("rt_rm"), sg("rt_rev")
        with nc.Block() as block:
            @block.sync
            def _(sp):
                for name, dst in (("dmat", dm), ("xi", xi), ("zeta", ze), ("gdec", gd)):
                    shape = list(dst.shape)
                    sp.dma_start(dst[:], g.C[name].rearrange("p (a b c) -> p a b c", a=2, b=2) if name == "xi" else
                                 g.C[name] if name == "gdec" else
                                 g.C[name].rearrange("p (a b) -> p a b", a=shape[1])).then_inc(*small.up(16))
                sp.dma_start(gr[:], row(I["g_ret_norm"][l])).then_inc(*small.up(16))
                for t in range(NT):
                    if t >= 2:
                        sp.wait_ge(*zd.at(t - 1))
                        sp.wait_ge(*gd_s.at(t - 1))
                    sp.dma_start(z[:, t % 2], g.zt[t * P:(t + 1) * P, W_MLA:W_MLA + W_RET]).then_inc(*z_in[t % 2].up(16))
                    if t >= NCT:
                        sp.dma_start(rope[:, t % 2], g.C["rope_r"].rearrange("(t p) (c f) -> p t c f", p=P, c=2)[:, t - NCT]) \
                            .then_inc(*z_in[t % 2].up(16))

            def z_at(t):
                n = 0
                for u in range(t % 2, t + 1, 2):
                    n += 16 if u < NCT else 32
                return n

            @block.vector
            def _(dve):
                link = linker(dve, chain)
                dve.wait_ge(*small.at(80))
                for t in range(NT):
                    zz, q = z[:, t % 2], qk[:, t % 2]
                    dve.wait_ge(*z_in[t % 2].at(z_at(t)))
                    z8 = zz[:, 0:512].rearrange("p (h d) -> p h d", h=8)
                    if t >= 2:
                        dve.wait_ge(*tr.at(t - 1))
                    if t < NCT:
                        link(nc.vector.tensor_copy(q, z8))
                    else:
                        r = rope[:, t % 2]
                        link(nc.vector.tensor_tensor(ra[:], z8, r[:, 0].unsqueeze(1).broadcast_to([P, 8, HD]), ALU.mult))
                        for s in range(2):
                            a, b = 32 * s, 32 * (1 - s)
                            link(nc.vector.tensor_tensor(rb[:, :, a:a + 32], z8[:, :, b:b + 32],
                                                         r[:, 1, a:a + 32].unsqueeze(1).broadcast_to([P, 8, 32]), ALU.mult))
                        link(nc.vector.tensor_tensor(q, ra[:], rb[:], ALU.add))
                    if t >= 1:
                        dve.wait_ge(*rm.at(t))
                    for d in range(2):
                        link(nc.vector.tensor_tensor(kz[:, d], q[:, 4:8].rearrange("p h d -> p (h d)"), ze[:, d], ALU.mult))
                    nc.vector.tensor_copy(V[:, t], zz[:, 512:768]).then_inc(*zd.up())
                    dve.wait_ge(*zd.at(t + 1))
                    nc.vector.tensor_copy(s4[0:1, 0:1], gr[0:1, 0:1]).then_inc(*qkd.up())
                    dve.wait_ge(*ev_a.at(t + 1))
                    for d in range(2):
                        link(nc.vector.tensor_tensor(QX[:, :, d, t * P:(t + 1) * P],
                                                     ps[:, t % 2, 0:2 * P].rearrange("p (a n) -> p a n", a=2), xi[:, :, d], ALU.mult))
                    nc.vector.tensor_copy(s4[0:1, 0:1], gr[0:1, 0:1]).then_inc(*ev_d.up())
                    dve.wait_ge(*rm.at(t + 1))
                    nc.vector.tensor_tensor(R[:, t], ps[:, 2 + t % 2].rearrange("p (a n) -> p a n", a=4),
                                            g.blk.unsqueeze(1).broadcast_to([P, 4, P]), ALU.mult).then_inc(*rev.up())
                dve.wait_ge(*rev.at(NT))
                for d, order in ((0, list(range(NT))), (1, [1, 0] + list(range(NT - 1, NCT - 1, -1)))):
                    link(nc.vector.memset(St[:, 0], 0.0))
                    for n, t in enumerate(order):
                        for p in range(2):
                            ins = nc.vector.scalar_tensor_tensor(St[:, (n + 1) % 2, p], St[:, n % 2, p], gd[:, p:p + 1],
                                                                 R[:, t, 2 * d + p], ALU.mult, ALU.add)
                        link(ins)
                        link(nc.vector.tensor_copy(R[:, t, 2 * d:2 * d + 2], St[:, n % 2]))

            @block.scalar
            def _(act):
                for t in range(NT):
                    act.wait_ge(*z_in[t % 2].at(z_at(t)))
                    nc.scalar.activation(G[:, t], z[:, t % 2, 768:1024], ACT.Silu).then_inc(*gd_s.up())
                    act.wait_ge(*tr.at(t + 1))
                    nc.scalar.copy(QT[:, :, t * P:(t + 1) * P], ps[:, t % 2].rearrange("p (a n) -> p a n", a=4)).then_inc(*ev_a.up())

            @block.tensor
            def _(pe):
                for t in range(NT):
                    pe.wait_ge(*qkd.at(t + 1))
                    if t >= 2:
                        pe.wait_ge(*ev_a.at(t - 1))
                        pe.wait_ge(*ev_d.at(t - 1))
                        pe.wait_ge(*rev.at(t - 1))
                    for a in range(4):
                        ins = nc.tensor.transpose(ps[:, t % 2, a * P:(a + 1) * P],
                                                  qk[:, t % 2, 2 * a:2 * a + 2].rearrange("p h d -> p (h d)"), g.ident)
                    ins.then_inc(*tr.up())
                    for d in range(2):
                        for p in range(2):
                            n = 2 * d + p
                            ins = nc.tensor.matmul(ps[:, 2 + t % 2, n * P:(n + 1) * P], kz[:, d, p * P:(p + 1) * P],
                                                   V[:, t, p * P:(p + 1) * P], start=True, stop=True)
                    ins.then_inc(*rm.up())
        sg.settle()
        sc, ptd, om, oe, od, ytr, ye = sg("at_sc"), sg("at_ex"), sg("at_pv"), sg("at_ote"), sg("normed"), sg("transposed"), sg("evac_a")
        tiles = list(range(t_first, NT))
        with nc.Block() as block:
            @block.tensor
            def _(pe):
                for n, t in enumerate(tiles):
                    ts = slice(t * P, (t + 1) * P)
                    if n >= 1:
                        pe.wait_ge(*ptd.at(n))
                    for h in range(H):
                        hp = slice(HD * (h % 2), HD * (h % 2) + HD)
                        b = 3 * (h % 2)
                        ins = nc.tensor.matmul(ps[:, b, (h // 2) * P:(h // 2 + 1) * P], QT[hp, 2 + h // 2, ts], QT[hp, h // 2, ts],
                                               start=True, stop=True)
                    ins.then_inc(*sc.up())
                    pe.wait_ge(*ptd.at(n + 1))
                    if n >= 1:
                        pe.wait_ge(*oe.at(n))
                    for p in range(2):
                        for d in range(2):
                            nc.tensor.matmul(ps[:, 1, p * P:(p + 1) * P], QX[:, p, d, ts], R[:, t, 2 * d + p], start=(d == 0), stop=False)
                        for h in (2 * p, 2 * p + 1):
                            ins = nc.tensor.matmul(ps[:, 1, h * HD:(h + 1) * HD], pt[:, h], V[:, t, h * HD:(h + 1) * HD],
                                                   start=False, stop=(h == 2 * p + 1))
                    ins.then_inc(*om.up())
                    pe.wait_ge(*od.at(n + 1))
                    if n >= 1:
                        pe.wait_ge(*ye.at(n))
                    for i in range(2):
                        ins = nc.tensor.transpose(ps[:, 2, i * P:(i + 1) * P], on[:, i * P:(i + 1) * P], g.ident)
                    ins.then_inc(*ytr.up())

            @block.vector
            def _(dve):
                link = linker(dve, chain)
                for n, t in enumerate(tiles):
                    dve.wait_ge(*sc.at(n + 1))
                    if n >= 1:
                        dve.wait_ge(*om.at(n))
                    for a in range(2):
                        ins = nc.vector.tensor_tensor(pt[:, a::2], ps[:, 3 * a, 0:2 * P].rearrange("p (h n) -> p h n", h=2), dm[:, a::2], ALU.mult)
                    ins.then_inc(*ptd.up())
                    dve.wait_ge(*oe.at(n + 1))
                    o4 = o[:].rearrange("p (h d) -> p h d", h=H)
                    link(nc.vector.tensor_tensor(sq[:], o[:], o[:], ALU.mult))
                    link(nc.vector.tensor_reduce(s4[:], sq[:].rearrange("p (h d) -> p h d", h=H), AX_X, ALU.add))
                    nc.vector.tensor_scalar(s4[:], s4[:], 1.0 / HD, EPS, ALU.mult, ALU.add).then_inc(*g.vr.up())
                    dve.wait_ge(*g.rq.at(n + 1))
                    link(nc.vector.tensor_tensor(o4, o4, s4[:].unsqueeze(2).broadcast_to([P, H, HD]), ALU.mult))
                    link(nc.vector.tensor_tensor(o[:], o[:], gr[:], ALU.mult))
                    if n >= 1:
                        dve.wait_ge(*ytr.at(n))
                    nc.vector.tensor_tensor(on[:], o[:], G[:, t], ALU.mult).then_inc(*od.up())

            @block.gpsimd
            def _(pool):
                for n in range(len(tiles)):
                    pool.wait_ge(*g.vr.at(n + 1))
                    nc.gpsimd.tensor_tensor(s4[:], s4[:], g.mhalf[:, 0:H], ALU.pow).then_inc(*g.rq.up())

            @block.scalar
            def _(act):
                for n, t in enumerate(tiles):
                    act.wait_ge(*om.at(n + 1))
                    if n >= 1:
                        act.wait_ge(*od.at(n))
                    nc.scalar.copy(o[:], ps[:, 1, 0:GW]).then_inc(*oe.up())
                    act.wait_ge(*ytr.at(n + 1))
                    nc.scalar.copy(yT[:, 6:8, t * P:(t + 1) * P], ps[:, 2, 0:2 * P].rearrange("p (a n) -> p a n", a=2)).then_inc(*ye.up())
        sg.settle()


def views(need_ctx):
    return ([(0, CTX, 0)] if need_ctx else []) + [(CTX, SEQ, 1)]


def bank(ps, b, w):
    return ps[:, b:b + (w + 511) // 512, :].rearrange("p b n -> p (b n)")[:, 0:w]


def stage_rwkv_params(nc, g, I, l, R):
    sg = g.sg
    small = sg("small_in")
    with nc.Block() as block:
        @block.sync
        def _(sp):
            with nc.allow_non_contiguous_dma(reason="vectors into columns"):
                for d in range(2):
                    sp.dma_start(R["w0"][:, d], col(I["rwkv_w0"][l, d], 2)).then_inc(*small.up(16))
                    sp.dma_start(R["a0"][:, d], col(I["rwkv_a0"][l, d], 2)).then_inc(*small.up(16))
                    sp.dma_start(R["wa2"][0:64, d], I["rwkv_w2"][l, d]).then_inc(*small.up(16))
                    sp.dma_start(R["wa2"][64:128, d], I["rwkv_a2"][l, d]).then_inc(*small.up(16))
                for name, n in (("rwkv_k_k", "kk"), ("rwkv_k_a", "ka"), ("rwkv_r_k", "rk"), ("g_ln_x", "gln")):
                    sp.dma_start(R[n][:], col(I[name][l], 2)).then_inc(*small.up(16))
            sp.dma_start(R["g2"][:], I["rwkv_g2"][l]).then_inc(*small.up(16))
            sp.dma_start(R["masks"][:], g.C["masks"].rearrange("p (d a n) -> p d a n", d=2, a=4)).then_inc(*small.up(16))
            sp.dma_start(R["nlev"][:], g.C["nlev"].rearrange("p (d a n) -> p d a n", d=2, a=LEVELS)).then_inc(*small.up(16))
            sp.wait_ge(*small.at(16 * 15))

        @block.vector
        def _(dve):
            dve.wait_ge(*small.at(16 * 15))
            nc.vector.tensor_scalar(R["oka"][:], R["ka"][:], -1.0, 1.0, ALU.mult, ALU.add)
    sg.settle()


def stage_rwkv_prep(nc, g, I, l, R, p, d):
    sg, ps, M = g.sg, g.ps, R["M"]
    A, SG, G, GX, E, KK, KS = (R[n] for n in ("A", "SG", "G", "GX", "E", "KK", "KS"))
    KR, BK, ET = R["KR"][d], R["BK"][d], R["ET"][d]
    r, k = M[:, p], M[:, 2 + p]
    sqd, wm, am, ssm, acted, gxd, gd, exd, chain = (sg(n) for n in ("sq_done", "rw_wm", "rw_am", "rw_ssm", "evac_a", "rw_gx",
                                                                    "rw_g", "rw_ex", "dve_chain"))
    allv, lnd, small = views(True), sg("ln_done"), sg("small_in")
    with nc.Block() as block:
        @block.sync
        def _(sp):
            if d == 0:
                sp.dma_start(R["reset"][:], g.C["reset"]).then_inc(*small.up(16))
                sp.wait_ge(*small.at(16))

        @block.tensor
        def _(pe):
            for s, (t0, tw) in enumerate(SPANS):
                ins = nc.tensor.matmul(ps[:, s, 0:tw], R["wa2"][0:64, d, p * P:(p + 1) * P], M[0:64, 6, t0:t0 + tw], start=True, stop=True)
            ins.then_inc(*wm.up())
            for s, (t0, tw) in enumerate(SPANS):
                ins = nc.tensor.matmul(ps[:, 3 + s, 0:tw], R["wa2"][64:128, d, p * P:(p + 1) * P], M[64:128, 6, t0:t0 + tw], start=True, stop=True)
            ins.then_inc(*am.up())
            if d == 0:
                pe.wait_ge(*sqd.at(1))
                pe.wait_ge(*acted.at(1))
                for s, (t0, tw) in enumerate(SPANS):
                    ins = nc.tensor.matmul(ps[:, s, 0:tw], g.blk, GX[:, t0:t0 + tw], start=True, stop=True)
                ins.then_inc(*ssm.up())

        @block.scalar
        def _(act):
            if d == 0:
                nc.scalar.activation(GX[:], k, ACT.Square, scale=R["kk"][:, p:p + 1]).then_inc(*sqd.up())
            act.wait_ge(*wm.at(1))
            for t0, tw, b in allv:
                ins = nc.scalar.activation(SG[:, t0:t0 + tw], bank(ps, b, tw), ACT.Sigmoid, bias=R["w0"][:, d, p:p + 1])
            ins.then_inc(*acted.up())
            act.wait_ge(*am.at(1))
            for t0, tw, b in allv:
                ins = nc.scalar.activation(A[:, t0:t0 + tw], bank(ps, 3 + b, tw), ACT.Sigmoid, bias=R["a0"][:, d, p:p + 1])
            ins.then_inc(*acted.up())
            if d == 0:
                act.wait_ge(*g.vr.at(1))
                nc.scalar.activation(E[:], E[:], ACT.Ln).then_inc(*lnd.up())
                act.wait_ge(*lnd.at(1))
                nc.scalar.activation(E[:], E[:], ACT.Exp, scale=-0.5).then_inc(*g.rq.up())
            act.wait_ge(*gxd.at(1))
            nc.scalar.activation(KR[:, 0], GX[:], ACT.Exp, scale=LWC).then_inc(*exd.up())
            act.wait_ge(*gd.at(1))
            nc.scalar.activation(KR[:, 1], G[:], ACT.Exp, scale=LWC).then_inc(*exd.up())
            nc.scalar.activation(BK[:, 0], G[:], ACT.Exp, scale=-LWC).then_inc(*exd.up())
            nc.scalar.activation(ET[:, 1], ET[:, 0], ACT.Exp, scale=LWC)

        @block.vector
        def _(dve):
            link = linker(dve, chain)
            dve.wait_ge(*acted.at(1))
            if d == 0:
                dve.wait_ge(*small.at(16))
            scan = nc.vector.tensor_tensor_scan(G[:], R["reset"][:], SG[:], 0.0, ALU.mult, ALU.add)
            if d == 0:
                scan.then_inc(*gd.up())
                dve.wait_ge(*gd.at(1))
            else:
                link(scan)
            link(nc.vector.tensor_copy(ET[:, 0], G[:, CH - 1::CH]))
            if d == 0:
                dve.wait_ge(*ssm.at(1))
                for t0, tw, b in allv:
                    ins = nc.vector.tensor_scalar(E[:, t0:t0 + tw], bank(ps, b, tw), 1e-12, None, ALU.add)
                ins.then_inc(*g.vr.up())
                dve.wait_ge(*g.rq.at(1))
                link(nc.vector.scalar_tensor_tensor(KK[:], k, R["kk"][:, p:p + 1], E[:], ALU.mult, ALU.mult))
                nc.vector.tensor_tensor(GX[:], G[:], SG[:], ALU.subtract).then_inc(*gxd.up())
            else:
                g3 = G[:].rearrange("p (c n) -> p c n", n=CH)
                nc.vector.tensor_tensor(GX[:].rearrange("p (c n) -> p c n", n=CH), ET[:, 0].unsqueeze(2).broadcast_to([P, T // CH, CH]),
                                        g3, ALU.subtract).then_inc(*gxd.up())
                dve.wait_ge(*gxd.at(1))
                nc.vector.tensor_tensor(G[:], GX[:], SG[:], ALU.add).then_inc(*gd.up())
            dve.wait_ge(*acted.at(2))
            link(nc.vector.tensor_scalar(E[:], A[:], R["ka"][:, p:p + 1], R["oka"][:, p:p + 1], ALU.mult, ALU.add))
            link(nc.vector.tensor_tensor(E[:], E[:], k, ALU.mult))
            if d == 0:
                link(nc.vector.tensor_copy(KS[:], E[:]))
            else:
                link(nc.vector.tensor_tensor(KS[:], KS[:], E[:], ALU.add))
            dve.wait_ge(*exd.at(3))
            link(nc.vector.tensor_tensor(KR[:, 0], KR[:, 0], KK[:], ALU.mult))
            link(nc.vector.tensor_tensor(KR[:, 1], KR[:, 1], r, ALU.mult))
            link(nc.vector.tensor_tensor(BK[:, 1], E[:], BK[:, 0], ALU.mult))
            link(nc.vector.tensor_tensor(BK[:, 0], BK[:, 0], KK[:], ALU.mult))
            link(nc.vector.tensor_tensor(BK[:, 0], BK[:, 0], A[:], ALU.mult))
    sg.settle()


def stage_rwkv_scan(nc, g, I, l, R, p, need_ctx):
    sg, ps, M, yT = g.sg, g.ps, R["M"], g.yT
    KR, BK, ET = R["KR"], R["BK"], R["ET"]
    order = [list(range(NT)), [1, 0] + list(range(NT - 1, NCT - 1, -1))]
    chunks = [[0, 1], [1, 0]]
    DD = (0, 1)
    with ExitStack() as cx:
        sb = Bufs(nc, cx, f"s{l}{p}")
        UM = [sb(f"UM{d}", [P, 2, 2, 4, P]) for d in DD]
        TM = [sb(f"TM{d}", [P, 2, 4, P]) for d in DD]
        NL = [sb(f"NL{d}", [P, LEVELS, 2, P]) for d in DD]
        TS = [sb(f"TS{d}", [P, 2, 2, P]) for d in DD]
        X = [sb(f"X{d}", [P, 2, P]) for d in DD]
        W1 = [sb(f"W1{d}", [P, P]) for d in DD]
        W2 = [sb(f"W2{d}", [P, P]) for d in DD]
        MV = [sb(f"MV{d}", [P, P]) for d in DD]
        U = [sb(f"U{d}", [P, P]) for d in DD]
        S = [sb(f"S{d}", [P, 3, P]) for d in DD]
        Se = [sb(f"Se{d}", [P, P]) for d in DD]
        bX, bT, bS, bR = ([4 * d + n for d in DD] for n in range(4))

        def sig(name):
            return [sg(f"rw_{name}{d}") for d in DD]
        p1, tr, um, tme, nl, ts = sig("p1"), sig("tr"), sig("um"), sig("tme"), sig("nl"), sig("ts")
        xm, xe, tm, wm, we, mve, w2m = sig("xm"), sig("xe"), sig("tm"), sig("wm"), sig("we"), sig("mve"), sig("w2m")
        umm, ue, smm, su, ym, ye, chain = sig("umm"), sig("ue"), sig("smm"), sig("su"), sig("ym"), sig("ye"), sg("dve_chain")
        NLV = LEVELS - 1

        def n_y(d, s):
            return sum(need_ctx or t >= NCT for t in order[d][:s])

        with nc.Block() as block:
            @block.tensor
            def _(pe):
                def carry(d, s, piece):
                    t = order[d][s]
                    b = ps[:, bS[d]]
                    if piece < 4:
                        n = 2 * s + piece // 2
                        c = chunks[d][piece // 2]
                        cs = slice(CH * c, CH * c + CH)
                        if piece % 2 == 0:
                            pe.wait_ge(*su[d].at(n + 1))
                            if piece == 0:
                                pe.wait_ge(*ye[d].at(n_y(d, s)) if n_y(d, s) else su[d].at(n + 1))
                            nc.tensor.matmul(b[cs, 0:P], W1[d][:, cs], S[d][:, n % 3], start=True, stop=True).then_inc(*umm[d].up())
                        else:
                            pe.wait_ge(*ue[d].at(n + 1))
                            nc.tensor.matmul(b[:, P:2 * P], TM[d][cs, s % 2, 1], U[d][cs], start=True, stop=False)
                            nc.tensor.matmul(b[:, P:2 * P], TM[d][cs, s % 2, 2], TM[d][cs, s % 2, 3], start=False, stop=True) \
                                .then_inc(*smm[d].up())
                    elif need_ctx or t >= NCT:
                        pe.wait_ge(*su[d].at(2 * s + 3))
                        o = b[:, 2 * P:3 * P]
                        for q, c in enumerate(chunks[d]):
                            cs = slice(CH * c, CH * c + CH)
                            nc.tensor.matmul(o[:, cs], S[d][:, (2 * s + q) % 3], KR[d][:, 1, t * P + CH * c:t * P + CH * c + CH],
                                             start=(q == 0), stop=False, skip_group_check=True)
                        for h in range(2):
                            hp = slice(HD * h, HD * h + HD)
                            nc.tensor.matmul(o[hp], U[d][:, hp], UM[d][:, s % 2, h, 1], start=False, stop=False, skip_group_check=True)
                            ins = nc.tensor.matmul(o[hp], TM[d][:, s % 2, 3, hp], UM[d][:, s % 2, h, 3], start=False, stop=True,
                                                   skip_group_check=True)
                        ins.then_inc(*ym[d].up())

                for s in range(NT):
                    for d in DD:
                        tt = slice(order[d][s] * P, order[d][s] * P + P)
                        if s:
                            pe.wait_ge(*we[d].at(2 * s))
                            pe.wait_ge(*mve[d].at(s))
                        for h in range(2):
                            hp = slice(HD * h, HD * h + HD)
                            o = ps[:, (bX, bT)[h][d]]
                            nc.tensor.matmul(o[:, 0:256], BK[d][hp, 0, tt], KR[d][hp, :, tt], start=True, stop=True)
                            nc.tensor.matmul(o[:, 256:512], BK[d][hp, 1, tt], KR[d][hp, :, tt], start=True, stop=True).then_inc(*p1[d].up())
                        for a, src in enumerate((KR[d][:, 0, tt], BK[d][:, 0, tt], BK[d][:, 1, tt], M[:, 4 + p, tt])):
                            ins = nc.tensor.transpose(ps[:, bR[d], a * P:(a + 1) * P], src, g.ident)
                        ins.then_inc(*tr[d].up())
                    for v in range(1, LEVELS):
                        for d in DD:
                            pe.wait_ge(*um[d].at(2 * s + 2))
                            pe.wait_ge(*nl[d].at(s * LEVELS + v + 1))
                            pe.wait_ge(*ts[d].at(s * LEVELS + v))
                            for h in range(2):
                                ins = nc.tensor.matmul(ps[:, bX[d], h * P:(h + 1) * P], NL[d][:, v, h], TS[d][:, 0, h], start=True, stop=True)
                            ins.then_inc(*xm[d].up())
                        if s:
                            for d in DD:
                                carry(d, s - 1, v - 1)
                        for d in DD:
                            pe.wait_ge(*xe[d].at(s * NLV + v))
                            if v < LEVELS - 1:
                                for h in range(2):
                                    nc.tensor.matmul(ps[:, bT[d], h * P:(h + 1) * P], TS[d][:, 1, h], X[d][:, h], start=True, stop=True)
                            for h in range(2):
                                ins = nc.tensor.matmul(ps[:, bT[d], (2 + h) * P:(3 + h) * P], X[d][:, h], TS[d][:, 1, h], start=True, stop=True)
                            ins.then_inc(*tm[d].up())
                    for d in DD:
                        pe.wait_ge(*ts[d].at((s + 1) * LEVELS))
                        pe.wait_ge(*tme[d].at(s + 1))
                        for h in range(2):
                            hp = slice(HD * h, HD * h + HD)
                            nc.tensor.matmul(ps[hp, bX[d], 0:P], TM[d][:, s % 2, 0, hp], TS[d][:, 1, h], start=True, stop=True)
                            ins = nc.tensor.matmul(ps[:, bT[d], hp], UM[d][:, s % 2, h, 2], TM[d][:, s % 2, 3, hp], start=True, stop=True)
                        ins.then_inc(*wm[d].up())
                    for d in DD:
                        pe.wait_ge(*mve[d].at(s + 1))
                        for h in range(2):
                            hp = slice(HD * h, HD * h + HD)
                            ins = nc.tensor.matmul(ps[:, bR[d], hp], TS[d][:, 1, h], MV[d][:, hp], start=True, stop=True)
                        ins.then_inc(*w2m[d].up())
                for d in DD:
                    pe.wait_ge(*we[d].at(2 * NT))
                for piece in range(5):
                    for d in DD:
                        carry(d, NT - 1, piece)

            @block.vector
            def _(dve):
                link = linker(dve, chain)

                def carry(d, s, piece):
                    t = order[d][s]
                    b = ps[:, bS[d]]
                    n = 2 * s + piece // 2
                    if piece < 4:
                        c = chunks[d][piece // 2]
                        cs = slice(CH * c, CH * c + CH)
                        e = ET[d][:, 1, 2 * t + c:2 * t + c + 1]
                        if piece % 2 == 0:
                            dve.wait_ge(*su[d].at(n + 1))
                            link(nc.vector.tensor_scalar(Se[d][:], S[d][:, n % 3], e, None, ALU.mult))
                            dve.wait_ge(*umm[d].at(n + 1))
                            dve.wait_ge(*we[d].at(2 * (s + 1)))
                            nc.vector.scalar_tensor_tensor(U[d][cs], b[cs, 0:P], -1.0, W2[d][cs], ALU.mult, ALU.subtract).then_inc(*ue[d].up())
                        else:
                            dve.wait_ge(*smm[d].at(n + 1))
                            for h in range(2):
                                hp = slice(HD * h, HD * h + HD)
                                ins = nc.vector.scalar_tensor_tensor(S[d][hp, (n + 1) % 3, hp], b[hp, P + HD * h:P + HD * h + HD], e[hp],
                                                                     Se[d][hp, hp], ALU.mult, ALU.add)
                            ins.then_inc(*su[d].up())
                    elif need_ctx or t >= NCT:
                        dve.wait_ge(*ym[d].at(n_y(d, s) + 1))
                        y = yT[:, 4 + p, t * P:(t + 1) * P]
                        o = b[:, 2 * P:3 * P]
                        if s < order[1 - d].index(t):
                            nc.vector.tensor_copy(y, o).then_inc(*ye[d].up())
                        else:
                            dve.wait_ge(ye[1 - d].sem, ye[1 - d].made)
                            nc.vector.tensor_tensor(y, y, o, ALU.add).then_inc(*ye[d].up())

                for d in DD:
                    nc.vector.memset(S[d][:], 0.0).then_inc(*su[d].up())
                for s in range(NT):
                    for d in DD:
                        for h in range(2):
                            dve.wait_ge(*p1[d].at(2 * s + h + 1))
                            nc.vector.tensor_tensor(UM[d][:, s % 2, h], ps[:, (bX, bT)[h][d]].rearrange("p (a n) -> p a n", a=4),
                                                    R["masks"][:, d], ALU.mult).then_inc(*um[d].up())
                    for d in DD:
                        dve.wait_ge(*nl[d].at(s * LEVELS + 1))
                        link(nc.vector.tensor_tensor(TS[d][:, 1], NL[d][:, 0], g.ident.unsqueeze(1).broadcast_to([P, 2, P]), ALU.add))
                        nc.vector.transpose(TS[d][:, 0].rearrange("p u n -> p (u n)"), TS[d][:, 1].rearrange("p u n -> p (u n)")) \
                            .then_inc(*ts[d].up())
                    for v in range(1, LEVELS):
                        if s:
                            for d in DD:
                                carry(d, s - 1, v - 1)
                        for d in DD:
                            dve.wait_ge(*tm[d].at(s * NLV + v))
                            dve.wait_ge(*ts[d].at(s * LEVELS + v))
                            a = 0 if v < LEVELS - 1 else 1
                            T2 = TS[d][:, a:2].rearrange("p a u n -> p (a u n)")
                            nc.vector.tensor_tensor(T2, T2, ps[:, bT[d], 2 * P * a:4 * P], ALU.add).then_inc(*ts[d].up())
                    for d in DD:
                        dve.wait_ge(*wm[d].at(s + 1))
                        nc.vector.tensor_copy(MV[d][:], ps[:, bT[d], 0:P]).then_inc(*mve[d].up())
                for piece in range(5):
                    for d in DD:
                        carry(d, NT - 1, piece)

            @block.gpsimd
            def _(pool):
                for s in range(NT):
                    for d in DD:
                        pool.wait_ge(*um[d].at(2 * (s + 1)))
                        if s:
                            pool.wait_ge(*tm[d].at(s * NLV))
                        for v in range(LEVELS):
                            nc.gpsimd.tensor_tensor(NL[d][:, v], UM[d][:, s % 2, :, 0], R["nlev"][:, d, v].unsqueeze(1).broadcast_to([P, 2, P]),
                                                    ALU.mult).then_inc(*nl[d].up())

            @block.scalar
            def _(act):
                for s in range(NT):
                    for d in DD:
                        act.wait_ge(*tr[d].at(s + 1))
                        nc.scalar.copy(TM[d][:, s % 2], ps[:, bR[d]].rearrange("p (a n) -> p a n", a=4)).then_inc(*tme[d].up())
                    for v in range(1, LEVELS):
                        for d in DD:
                            act.wait_ge(*xm[d].at(s * NLV + v))
                            nc.scalar.copy(X[d][:].rearrange("p u n -> p (u n)"), ps[:, bX[d], 0:2 * P]).then_inc(*xe[d].up())
                    for d in DD:
                        act.wait_ge(*wm[d].at(s + 1))
                        nc.scalar.copy(W1[d][:], ps[:, bX[d], 0:P]).then_inc(*we[d].up())
                    for d in DD:
                        act.wait_ge(*w2m[d].at(s + 1))
                        nc.scalar.copy(W2[d][:], ps[:, bR[d], 0:P]).then_inc(*we[d].up())
        sg.settle()


def stage_rwkv_out(nc, g, I, l, R, p, need_ctx):
    sg, ps, M = g.sg, g.ps, R["M"]
    y, r, v = g.yT[:, 4 + p], M[:, p], M[:, 4 + p]
    YC, SQ, RS, RK = R["KR"][0][:, 0], R["KR"][0][:, 1], R["BK"][0][:, 0], R["BK"][0][:, 1]
    vw = views(need_ctx)
    spans = [(s, t0, tw) for s, (t0, tw) in enumerate(SPANS) if need_ctx or s > 0]
    lnd = sg("ln_done")
    mm, ycd, sqd, rkd, rsd, bon, chain = (sg(n) for n in ("mm_done", "normed", "sq_done", "coef", "evac_d", "rw_g", "dve_chain"))
    with nc.Block() as block:
        @block.tensor
        def _(pe):
            def grp(b, lhsT, rhs):
                for s, t0, tw in spans:
                    ins = nc.tensor.matmul(ps[:, b + s, 0:tw], lhsT, rhs[:, t0:t0 + tw], start=True, stop=True)
                ins.then_inc(*mm.up())
            grp(0, g.blk, y)
            pe.wait_ge(*sqd.at(1))
            grp(3, g.blk, SQ)
            pe.wait_ge(*rkd.at(1))
            grp(0, g.blk, RK)
            pe.wait_ge(*rsd.at(1))
            grp(3, R["g2"][:, p * P:(p + 1) * P], M[:, 7])

        @block.scalar
        def _(act):
            act.wait_ge(*ycd.at(1))
            for t0, tw, b in vw:
                ins = nc.scalar.activation(SQ[:, t0:t0 + tw], YC[:, t0:t0 + tw], ACT.Square)
            ins.then_inc(*sqd.up())
            act.wait_ge(*rsd.at(1))
            al = slice(vw[0][0], T)
            nc.scalar.activation(RS[:, al], RS[:, al], ACT.Ln).then_inc(*lnd.up())
            act.wait_ge(*lnd.at(1))
            nc.scalar.activation(RS[:, al], RS[:, al], ACT.Exp, scale=-0.5).then_inc(*g.rq.up())

        @block.vector
        def _(dve):
            link = linker(dve, chain)
            dve.wait_ge(*mm.at(1))
            for t0, tw, b in vw:
                t = slice(t0, t0 + tw)
                ins = nc.vector.scalar_tensor_tensor(YC[:, t], bank(ps, b, tw), -1.0 / HD, y[:, t], ALU.mult, ALU.add)
            ins.then_inc(*ycd.up())
            t0 = vw[0][0]
            al = slice(t0, T)
            nc.vector.scalar_tensor_tensor(RK[:, al], r[:, al], R["rk"][:, p:p + 1], R["KS"][:, al], ALU.mult, ALU.mult).then_inc(*rkd.up())
            dve.wait_ge(*mm.at(2))
            for t0, tw, b in vw:
                ins = nc.vector.tensor_scalar(RS[:, t0:t0 + tw], bank(ps, 3 + b, tw), 1.0 / HD, GN_EPS, ALU.mult, ALU.add)
            ins.then_inc(*rsd.up())
            dve.wait_ge(*rsd.at(1))
            dve.wait_ge(*g.rq.at(1))
            link(nc.vector.scalar_tensor_tensor(YC[:, al], YC[:, al], R["gln"][:, p:p + 1], RS[:, al], ALU.mult, ALU.mult))
            dve.wait_ge(*mm.at(3))
            for t0, tw, b in vw:
                t = slice(t0, t0 + tw)
                link(nc.vector.tensor_tensor(RS[:, t], bank(ps, b, tw), v[:, t], ALU.mult))
            link(nc.vector.tensor_tensor(YC[:, al], YC[:, al], RS[:, al], ALU.add))
            dve.wait_ge(*mm.at(4))
            for t0, tw, b in vw:
                t = slice(t0, t0 + tw)
                nc.vector.tensor_tensor(y[:, t], YC[:, t], bank(ps, 3 + b, tw), ALU.mult)
    sg.settle()


def stage_out(nc, g, I, l, need_ctx):
    sg, ps, yT = g.sg, g.ps, g.yT
    tiles = list(range(0 if need_ctx else NCT, NT))
    with ExitStack() as cx:
        sb = Bufs(nc, cx, f"o{l}")
        w = sb("w", [P, KT, D])
        rows = sb("rows", [P, 2, 3, D])
        gn = sb("gn", [P, D])
        wr = sb("wr", [P, KT, NE])
        br = sb("br", [P, NE])
        xi_ = sb("xi", [P, 2, D])
        xo = sb("xo", [P, 2, D])
        h2 = sb("h2", [P, 2, D])
        hT2 = sb("hT2", [P, KT, P])
        junk = sb("junk", [P, D])
        st = sb("st", [P, 4])
        lg = sb("lg", [P, NE])
        ex = sb("ex", [P, NE])
        w_in, small, x_in, chain = sg("z_in"), sg("small_in"), [sg(f"w_slot{i}") for i in range(2)], sg("dve_chain")
        om, xd, sqd, hd, tr, te = sg("mm_done"), sg("coef"), sg("sq_done"), sg("normed"), sg("transposed"), sg("evac_a")
        lm, lgd, exd, afd, at, ae = sg("ro_lm"), sg("ro_lg"), sg("ro_ex"), sg("ro_aff"), sg("ro_at"), sg("ro_ae")
        xs, hs = [sg(f"out_slot{i}") for i in range(2)], [sg(f"out_slot{2 + i}") for i in range(2)]
        with nc.Block() as block:
            @block.sync
            def _(sp):
                for s in range(2):
                    for n, c in enumerate((2, 3, 4)):
                        sp.dma_start(rows[:, s, n], row(g.mod[l, s, c * D:(c + 1) * D])).then_inc(*small.up(16))
                sp.dma_start(gn[:], row(I["g_norm2"][l])).then_inc(*small.up(16))
                sp.dma_start(wr[:], I["w_router"][l].rearrange("(k p) e -> p k e", p=P)).then_inc(*small.up(16))
                sp.dma_start(br[:], row(I["b_router"][l])).then_inc(*small.up(16))
                sp.dma_start(w[:], I["w_out"][l].rearrange("(k p) f -> p k f", p=P)).then_inc(*w_in.up(16))
                for n, t in enumerate(tiles):
                    if n >= 2:
                        sp.wait_ge(*xd.at(n - 1))
                    sp.dma_start(xi_[:, n % 2], g.x_rows(I, l, t)).then_inc(*x_in[n % 2].up(16))

            @block.gpsimd
            def _(pool):
                for n, t in enumerate(tiles):
                    ts = slice(t * P, (t + 1) * P)
                    pool.wait_ge(*xd.at(n + 1))
                    pool.dma_start(g.x[ts], xo[:, n % 2]).then_inc(*xs[n % 2].up(16))
                    pool.wait_ge(*g.vr.at(n + 1))
                    nc.gpsimd.tensor_tensor(st[:, 1:2], st[:, 1:2], g.mhalf[:, 0:1], ALU.pow).then_inc(*g.rq.up())
                    pool.wait_ge(*hd.at(n + 1))
                    pool.dma_start(g.h2[ts], h2[:, n % 2]).then_inc(*hs[n % 2].up(16))
                for s in xs + hs:
                    pool.wait_ge(s.sem, s.made)

            @block.tensor
            def _(pe):
                pe.wait_ge(*w_in.at(16))
                pe.wait_ge(*small.at(144))

                def proj(n):
                    t = tiles[n]
                    if n >= 2:
                        pe.wait_ge(*xd.at(n - 1))
                    for half in range(2):
                        for k in range(KT):
                            ins = nc.tensor.matmul(ps[:, 2 * (n % 2) + half, :], yT[:, k, t * P:(t + 1) * P], w[:, k, half * 512:(half + 1) * 512],
                                                   start=(k == 0), stop=(k == KT - 1))
                    ins.then_inc(*om.up())
                proj(0)
                for n, t in enumerate(tiles):
                    if n + 1 < len(tiles):
                        proj(n + 1)
                    pe.wait_ge(*hd.at(n + 1))
                    if n >= 1:
                        pe.wait_ge(*te.at(n))
                    for k in range(KT):
                        ins = nc.tensor.transpose(ps[:, 4 + k // 4, (k % 4) * P:(k % 4 + 1) * P], h2[:, n % 2, k * P:(k + 1) * P], g.ident)
                    ins.then_inc(*tr.up())
                    pe.wait_ge(*te.at(n + 1))
                    if n >= 1:
                        pe.wait_ge(*lgd.at(n))
                    for k in range(KT):
                        ins = nc.tensor.matmul(ps[:, 6, 0:NE], hT2[:, k], wr[:, k], start=(k == 0), stop=(k == KT - 1))
                    ins.then_inc(*lm.up())
                    pe.wait_ge(*afd.at(n + 1))
                    if n >= 1:
                        pe.wait_ge(*ae.at(n))
                    nc.tensor.transpose(ps[0:NE, 7, 0:P], ex[:], g.ident).then_inc(*at.up())

            @block.vector
            def _(dve):
                link = linker(dve, chain)
                dve.wait_ge(*small.at(144))
                for s in range(2):
                    link(nc.vector.scalar_tensor_tensor(rows[:, s, 2], rows[:, s, 2], 1.0, gn[:], ALU.add, ALU.mult))
                for n, t in enumerate(tiles):
                    s = 1 if t < NCT else 0
                    dve.wait_ge(*om.at(n + 1))
                    dve.wait_ge(*x_in[n % 2].at(16 * (n // 2 + 1)))
                    if n >= 2:
                        dve.wait_ge(*xs[n % 2].at(16 * (n // 2)))
                    link(nc.vector.tensor_tensor(xo[:, n % 2], bank(ps, 2 * (n % 2), D), rows[:, s, 0], ALU.mult))
                    nc.vector.tensor_tensor(xo[:, n % 2], xo[:, n % 2], xi_[:, n % 2], ALU.add).then_inc(*xd.up())
                    dve.wait_ge(*sqd.at(n + 1))
                    nc.vector.tensor_scalar(st[:, 1:2], st[:, 0:1], 1.0 / D, EPS, ALU.mult, ALU.add).then_inc(*g.vr.up())
                    dve.wait_ge(*g.rq.at(n + 1))
                    if n >= 2:
                        dve.wait_ge(*hs[n % 2].at(16 * (n // 2)))
                    link(nc.vector.scalar_tensor_tensor(h2[:, n % 2], xo[:, n % 2], st[:, 1:2], rows[:, s, 2], ALU.mult, ALU.mult))
                    nc.vector.tensor_tensor(h2[:, n % 2], h2[:, n % 2], rows[:, s, 1], ALU.add).then_inc(*hd.up())
                    dve.wait_ge(*lm.at(n + 1))
                    link(nc.vector.tensor_tensor(lg[:], ps[:, 6, 0:NE], br[:], ALU.add))
                    link(nc.vector.reduce_max(st[:, 2:3], lg[:], AX_X))
                    nc.vector.tensor_scalar(lg[:], lg[:], st[:, 2:3], None, ALU.subtract).then_inc(*lgd.up())
                    dve.wait_ge(*exd.at(n + 1))
                    link(nc.vector.reciprocal(st[:, 3:4], st[:, 3:4]))
                    nc.vector.tensor_scalar(ex[:], ex[:], st[:, 3:4], None, ALU.mult).then_inc(*afd.up())
                    dve.wait_ge(*at.at(n + 1))
                    nc.vector.tensor_copy(g.aff[:, t * P:(t + 1) * P], ps[0:NE, 7, 0:P]).then_inc(*ae.up())

            @block.scalar
            def _(act):
                for n, t in enumerate(tiles):
                    act.wait_ge(*xd.at(n + 1))
                    if n >= 1:
                        act.wait_ge(*sqd.at(n))
                    nc.scalar.activation(junk[:], xo[:, n % 2], ACT.Square, accum_out=st[:, 0:1]).then_inc(*sqd.up())
                    act.wait_ge(*tr.at(n + 1))
                    nc.scalar.copy(hT2[:].rearrange("p k n -> p (k n)"), bank(ps, 4, D)).then_inc(*te.up())
                    act.wait_ge(*lgd.at(n + 1))
                    nc.scalar.activation(ex[:], lg[:], ACT.Exp, accum_out=st[:, 3:4]).then_inc(*exd.up())
        sg.settle()


def stage_topk(nc, g, I, l, need_ctx):
    sg, ps = g.sg, g.ps
    sets = [("x", CTX, SEQ, CAPX)] + ([("c", 0, CTX, CAPC)] if need_ctx else [])
    with ExitStack() as cx:
        sb = Bufs(nc, cx, f"k{l}")
        val = sb("val", [NE, 2, P])
        idx = sb("idx", [NE, 2, P], U32)
        idf = sb("idf", [NE, 2, P])
        zero = sb("zero", [P, D])
        zd, zs, found, tr, chain = sg("coef"), sg("zeroed"), sg("normed"), sg("transposed"), sg("dve_chain")
        with nc.Block() as block:
            @block.vector
            def _(dve):
                link = linker(dve, chain)
                nc.vector.memset(zero[:], 0.0).then_inc(*zd.up())
                for n, (_, t0, tw, cap) in enumerate(sets):
                    a = g.aff[:, t0:t0 + tw]
                    for r in range(cap // 8):
                        v8 = val[:, n, 8 * r:8 * r + 8]
                        link(nc.vector.max(v8, a))
                        link(nc.vector.max_index(idx[:, n, 8 * r:8 * r + 8], v8, a))
                        link(nc.vector.match_replace(a, v8, a, -1.0))
                    link(nc.vector.tensor_copy(idf[:, n, 0:cap], idx[:, n, 0:cap]))
                    nc.vector.tensor_scalar(idf[:, n, 0:cap], idf[:, n, 0:cap], float(t0), None, ALU.add).then_inc(*found.up())
                for n, (_, t0, tw, cap) in enumerate(sets):
                    dve.wait_ge(*tr.at(n + 1))
                    nc.vector.tensor_copy(g.tok[0:cap, n], ps[0:cap, n, 0:NE])
                    nc.vector.tensor_copy(g.gate[0:cap, n], ps[0:cap, n, NE:2 * NE])

            @block.gpsimd
            def _(pool):
                pool.wait_ge(*zd.at(1))
                for t in range(0 if need_ctx else NCT, NT):
                    pool.dma_start(g.acc[t * P:(t + 1) * P], zero[:]).then_inc(*zs.up(16))
                pool.wait_ge(zs.sem, zs.made)

            @block.tensor
            def _(pe):
                for n, (_, t0, tw, cap) in enumerate(sets):
                    pe.wait_ge(*found.at(n + 1))
                    nc.tensor.transpose(ps[0:cap, n, 0:NE], idf[:, n, 0:cap], g.ident[0:NE, 0:NE])
                    nc.tensor.transpose(ps[0:cap, n, NE:2 * NE], val[:, n, 0:cap], g.ident[0:NE, 0:NE]).then_inc(*tr.up())
        sg.settle()


def stage_moe(nc, g, I, l, need_ctx):
    sg, ps = g.sg, g.ps
    sets = [(0, CAPX)] + ([(1, CAPC)] if need_ctx else [])
    passes = [(e, n, cap) for e in range(NE) for n, cap in sets]
    NP, RW = len(passes), 8
    parts = [(e, m, half) for e in range(NE) for m in range(3) for half in range(2)]
    names = ("w_gate", "w_up", "w_down")
    with ExitStack() as cx:
        sb = Bufs(nc, cx, f"e{l}")
        w = sb("w", [P, RW, 4, 1024])
        xe = sb("xe", [P, 3, D])
        xT = sb("xT", [P, KT, P])
        hid = sb("hid", [P, FF])
        hT2 = sb("hT2", [P, KT, P])
        ye = sb("ye", [P, 2, D])
        pg = sb("pg", [P, FF])
        pu = sb("pu", [P, FF])
        gs = sb("gs", [P, KT, CAPC])
        w_in = [sg(f"w_slot{i}") for i in range(RW)]
        ga = [sg(f"moe_gather{b}") for b in range(3)]
        sc, gm, um, dm = sg("moe_scatter"), sg("moe_gm"), sg("moe_um"), sg("moe_dm")
        xtr, xte, si, hd, htr, hte, yd = (sg(n) for n in ("moe_xtr", "moe_xte", "moe_silu", "moe_hid", "moe_htr", "moe_hte", "moe_ye"))
        gsd, dpm, pdd = sg("moe_gs"), sg("moe_dp"), sg("moe_pd")
        with nc.Block() as block:
            @block.sync
            def _(sp):
                for j, (e, m, half) in enumerate(parts):
                    if j >= RW:
                        eo, mo, _ = parts[j - RW]
                        last = (eo + 1) * len(sets)
                        sp.wait_ge(*(gm, um, dm)[mo].at(last if mo == 2 else 2 * last))
                    sp.dma_start(w[:, j % RW], I[names[m]][l, e].rearrange("(k p) f -> p k f", p=P)[:, 4 * half:4 * half + 4]) \
                        .then_inc(*w_in[j % RW].up(16))

            @block.gpsimd
            def _(pool):
                def gather(i):
                    e, n, cap = passes[i]
                    if i >= 3:
                        pool.wait_ge(*xtr.at(i - 2))
                    pool.indirect_dma_start(xe[0:cap, i % 3], None, g.h2, bass.IndirectOffsetOnAxis(ap=g.tok[0:cap, n, e:e + 1], axis=0)) \
                        .then_inc(*ga[i % 3].up(16))
                gather(0)
                gather(1)
                for i, (e, n, cap) in enumerate(passes):
                    if i + 2 < NP:
                        gather(i + 2)
                    pool.wait_ge(*yd.at(i + 1))
                    if i:
                        pool.wait_ge(*sc.at(16 * i))
                    pool.indirect_dma_start(g.acc, bass.IndirectOffsetOnAxis(ap=g.tok[0:cap, n, e:e + 1], axis=0), ye[0:cap, i % 2], None,
                                            compute_op=ALU.add).then_inc(*sc.up(16))
                pool.wait_ge(*sc.at(16 * NP))

            @block.tensor
            def _(pe):
                def slot(e, m, half):
                    j = 6 * e + 2 * m + half
                    return j % RW, 16 * (j // RW + 1)

                def product(n, cap, half, k, b, xs, rhs):
                    kk = 4 * half + k
                    if n == 1:
                        return nc.tensor.matmul(ps[32 * k:32 * k + 32, b, :], xs[:, kk, 0:cap], rhs, start=(half == 0), stop=(half == 1))
                    return nc.tensor.matmul(ps[0:cap, b, :], xs[:, kk, 0:cap], rhs, start=(kk == 0), stop=(kk == KT - 1))

                def x_transposes(i):
                    e, n, cap = passes[i]
                    pe.wait_ge(*ga[i % 3].at(16 * (i // 3 + 1)))
                    if i >= 2:
                        pe.wait_ge(*yd.at(i - 1))
                    for k in range(KT):
                        ins = nc.tensor.transpose(ps[:, 6 + k // 4, (k % 4) * P:(k % 4) * P + cap], xe[0:cap, i % 3, k * P:(k + 1) * P],
                                                  g.ident[0:cap, 0:cap])
                    ins.then_inc(*xtr.up())
                x_transposes(0)
                for i, (e, n, cap) in enumerate(passes):
                    pe.wait_ge(*xte.at(i + 1))
                    if i >= 1:
                        pe.wait_ge(*hd.at(2 * i))
                    for c in range(2):
                        for m in range(2):
                            for half in range(2):
                                s, v = slot(e, m, half)
                                pe.wait_ge(*w_in[s].at(v))
                                for k in range(4):
                                    ins = product(n, cap, half, k, 2 * m + c, xT, w[:, s, k, c * 512:(c + 1) * 512])
                            ins.then_inc(*(gm, um)[m].up())
                    if i + 1 < NP:
                        x_transposes(i + 1)
                    if n == 1:
                        pe.wait_ge(*hd.at(2 * i + 2))
                        for src, b in ((pg, 4), (pu, 5)):
                            for k in range(KT):
                                ins = nc.tensor.matmul(ps[:, b, k * CAPC:(k + 1) * CAPC], src[:, k * P:(k + 1) * P], g.sel[:],
                                                       start=True, stop=True)
                    for k in range(KT if n == 0 else 0):
                        if k % 4 == 0:
                            pe.wait_ge(*hd.at(2 * i + 1 + k // 4))
                        ins = nc.tensor.transpose(ps[:, 4 + k // 4, (k % 4) * P:(k % 4) * P + cap], hid[0:cap, k * P:(k + 1) * P],
                                                  g.ident[0:cap, 0:cap])
                    ins.then_inc(*htr.up())
                    pe.wait_ge(*hte.at(i + 1))
                    if i + 1 < NP:
                        pe.wait_ge(*xte.at(i + 2))
                    for half in range(2):
                        s, v = slot(e, 2, half)
                        pe.wait_ge(*w_in[s].at(v))
                        for c in range(2):
                            for k in range(4):
                                ins = product(n, cap, half, k, 6 + c, hT2, w[:, s, k, c * 512:(c + 1) * 512])
                    if n == 1:
                        ins.then_inc(*dpm.up())
                        pe.wait_ge(*pdd.at(e + 1))
                        for c in range(2):
                            ins = nc.tensor.matmul(ps[0:CAPC, 6 + c, :], g.sel[:], pg[:, c * 512:(c + 1) * 512], start=True, stop=True)
                    ins.then_inc(*dm.up())

            def x_copy(act, i):
                cap = passes[i][2]
                act.wait_ge(*xtr.at(i + 1))
                if i:
                    act.wait_ge(*um.at(2 * i))
                nc.scalar.copy(xT[:, :, 0:cap], bank(ps, 6, D).rearrange("p (k n) -> p k n", k=KT)[:, :, 0:cap]).then_inc(*xte.up())

            @block.scalar
            def _(act):
                for i, (e, n, cap) in enumerate(passes):
                    if i == 0:
                        x_copy(act, 0)
                    if i >= 1:
                        act.wait_ge(*htr.at(i))
                    for c in range(2):
                        act.wait_ge(*gm.at(2 * i + c + 1))
                        dst, fn = ((hid, ACT.Silu), (pg, ACT.Copy))[n]
                        nc.scalar.activation(dst[:, c * 512:(c + 1) * 512], ps[:, c], fn).then_inc(*si.up())
                    if i + 1 < NP:
                        x_copy(act, i + 1)
                    if n == 0:
                        act.wait_ge(*htr.at(i + 1))
                        nc.scalar.copy(hT2[:, :, 0:cap], bank(ps, 4, D).rearrange("p (k n) -> p k n", k=KT)[:, :, 0:cap]).then_inc(*hte.up())
                    else:
                        act.wait_ge(*htr.at(i + 1))
                        nc.scalar.activation(gs[:].rearrange("p k n -> p (k n)"), ps[:, 4, 0:KT * CAPC], ACT.Silu).then_inc(*gsd.up())
                    if n == 1:
                        act.wait_ge(*dpm.at(e + 1))
                        nc.scalar.copy(pg[:], bank(ps, 6, D)).then_inc(*pdd.up())

            @block.vector
            def _(dve):
                for i, (e, n, cap) in enumerate(passes):
                    for c in range(2):
                        dve.wait_ge(*um.at(2 * i + c + 1))
                        dve.wait_ge(*si.at(2 * i + c + 1))
                        h = slice(c * 512, (c + 1) * 512)
                        if n == 0:
                            nc.vector.tensor_tensor(hid[:, h], hid[:, h], ps[:, 2 + c], ALU.mult).then_inc(*hd.up())
                        else:
                            nc.vector.tensor_copy(pu[:, h], ps[:, 2 + c]).then_inc(*hd.up())
                    if n == 1:
                        dve.wait_ge(*gsd.at(e + 1))
                        nc.vector.tensor_tensor(hT2[:, :, 0:CAPC], gs[:], ps[:, 5, 0:KT * CAPC].rearrange("p (k n) -> p k n", k=KT),
                                                ALU.mult).then_inc(*hte.up())
                    dve.wait_ge(*dm.at(i + 1))
                    if i >= 2:
                        dve.wait_ge(*sc.at(16 * (i - 1)))
                    nc.vector.tensor_scalar(ye[0:cap, i % 2], bank(ps, 6, D)[0:cap], g.gate[0:cap, n, e:e + 1], None, ALU.mult).then_inc(*yd.up())
        sg.settle()


def stage_residual(nc, g, I, l, need_ctx):
    sg = g.sg
    tiles = list(range(0 if need_ctx else NCT, NT))
    with ExitStack() as cx:
        sb = Bufs(nc, cx, f"f{l}")
        rows = sb("rows", [P, 2, D])
        xb = sb("xb", [P, 3, D])
        ab = sb("ab", [P, 3, D])
        small, x_in, done, st, chain = sg("small_in"), [sg(f"w_slot{i}") for i in range(3)], sg("normed"), [sg(f"out_slot{i}") for i in range(3)], sg("dve_chain")
        with nc.Block() as block:
            @block.sync
            def _(sp):
                for s in range(2):
                    sp.dma_start(rows[:, s], row(g.mod[l, s, 5 * D:6 * D])).then_inc(*small.up(16))
                for n, t in enumerate(tiles):
                    ts = slice(t * P, (t + 1) * P)
                    if n >= 3:
                        sp.wait_ge(*st[n % 3].at(16 * (n // 3)))
                    sp.dma_start(xb[:, n % 3], g.x[ts]).then_inc(*x_in[n % 3].up(16))
                    sp.dma_start(ab[:, n % 3], g.acc[ts]).then_inc(*x_in[n % 3].up(16))

            @block.vector
            def _(dve):
                link = linker(dve, chain)
                dve.wait_ge(*small.at(32))
                for n, t in enumerate(tiles):
                    dve.wait_ge(*x_in[n % 3].at(32 * (n // 3 + 1)))
                    link(nc.vector.tensor_tensor(ab[:, n % 3], ab[:, n % 3], rows[:, 1 if t < NCT else 0], ALU.mult))
                    nc.vector.tensor_tensor(ab[:, n % 3], ab[:, n % 3], xb[:, n % 3], ALU.add).then_inc(*done.up())

            @block.gpsimd
            def _(pool):
                for n, t in enumerate(tiles):
                    pool.wait_ge(*done.at(n + 1))
                    dst = g.out[0, (t - NCT) * P:(t - NCT + 1) * P] if l == DEPTH - 1 else g.x[t * P:(t + 1) * P]
                    pool.dma_start(dst, ab[:, n % 3]).then_inc(*st[n % 3].up(16))
                for s in st:
                    pool.wait_ge(s.sem, s.made)
        sg.settle()


class Core:
    pass


def build(nc, I, C, out, dbg=None):
    g = Core()
    kind = "Internal"
    def dram(name, shape):
        if dbg is not None and name in dbg:
            return nc.dram_tensor("out_dbg_" + name, shape, F32, kind="ExternalOutput").ap()
        return nc.dram_tensor(name, shape, F32, kind=kind).ap()
    g.mod = dram("mod_rows", [DEPTH, 2, 6 * D])
    g.x = dram("x_rows", [T, D])
    g.h2 = dram("h2_rows", [T, D])
    g.acc = dram("acc_rows", [T, D])
    g.zt = dram("z_rows", [T, W_MLA + W_RET])
    g.C, g.out = C, out

    def x_rows(I, l, t):
        if l == 0:
            return I["ctx"][0, t * P:(t + 1) * P] if t < NCT else I["x"][0, (t - NCT) * P:(t - NCT + 1) * P]
        return g.x[t * P:(t + 1) * P]
    g.x_rows = x_rows
    with ExitStack() as ctx:
        g.sg = Signals(ctx, nc)
        fixed = Bufs(nc, ctx, "all")
        g.ps = ctx.enter_context(nc.psum_tensor("ps", [P, 8, 512], F32))
        tabs = fixed("tabs", [P, 3, P])
        g.ident, g.ones, g.blk = tabs[:, 0], tabs[:, 1], tabs[:, 2]
        g.aff = fixed("aff", [NE, T])
        g.tok = fixed("tok", [P, 2, NE], I32)
        g.gate = fixed("gate", [P, 2, NE])
        g.mhalf = fixed("mhalf", [P, 8])
        g.sel = fixed("sel", [P, 32])
        g.vr, g.rq = g.sg("var_ready"), g.sg("rsqrt_done")
        small = g.sg("small_in")
        with nc.Block() as block:
            @block.vector
            def _(dve):
                nc.vector.memset(g.mhalf[:], -0.5)

            @block.sync
            def _(sp):
                for n, name in enumerate(("ident", "ones", "blk")):
                    sp.dma_start(tabs[:, n], C[name]).then_inc(*small.up(16))
                sp.dma_start(g.sel[:], C["sel"]).then_inc(*small.up(16))
                sp.wait_ge(*small.at(64))
        g.sg.settle()
        stage_modulation(nc, g, I)
        for l in range(DEPTH):
            need_ctx = l < DEPTH - 1
            with ExitStack() as lay:
                g.yT = lay.enter_context(nc.sbuf_tensor(f"yT{l}", [P, KT, T], F32))
                with ExitStack() as mix:
                    M = mix.enter_context(nc.sbuf_tensor(f"M{l}", [P, 8, T], F32))
                    with ExitStack() as norm:
                        g.hT = norm.enter_context(nc.sbuf_tensor(f"hT{l}", [P, KT, T], F32))
                        stage_norm1(nc, g, I, l)
                        stage_project(nc, g, I, l, M)
                    with ExitStack() as mla:
                        sb = Bufs(nc, mla, f"mla{l}")
                        S = dict(QT=sb("QT", [P, H, T]), KT=sb("KT", [P, H, T]), V=sb("V", [P, NT, H, 65]))
                        stage_mla_prep(nc, g, I, l, S)
                        stage_mla_attend(nc, g, I, l, S, need_ctx)
                    stage_retention(nc, g, I, l, need_ctx)
                    sb = Bufs(nc, mix, f"rw{l}")
                    R = dict(M=M, w0=sb("w0", [P, 2, 2]), a0=sb("a0", [P, 2, 2]), wa2=sb("wa2", [P, 2, GW]),
                             kk=sb("kk", [P, 2]), ka=sb("ka", [P, 2]), oka=sb("oka", [P, 2]), rk=sb("rk", [P, 2]), gln=sb("gln", [P, 2]),
                             g2=sb("g2", [P, GW]), masks=sb("masks", [P, 2, 4, P]), nlev=sb("nlev", [P, 2, LEVELS, P]),
                             KR=[sb(f"KR{d}", [P, 2, T]) for d in range(2)], BK=[sb(f"BK{d}", [P, 2, T]) for d in range(2)],
                             ET=[sb(f"ET{d}", [P, 2, T // CH]) for d in range(2)], KS=sb("KS", [P, T]))
                    stage_rwkv_params(nc, g, I, l, R)
                    for p in range(2):
                        with ExitStack() as pr:
                            tb = Bufs(nc, pr, f"rp{l}{p}")
                            R.update((n, tb(n, [P, T])) for n in ("A", "SG", "G", "GX", "E", "KK", "reset"))
                            for d in range(2):
                                stage_rwkv_prep(nc, g, I, l, R, p, d)
                        stage_rwkv_scan(nc, g, I, l, R, p, need_ctx)
                        stage_rwkv_out(nc, g, I, l, R, p, need_ctx)
                stage_out(nc, g, I, l, need_ctx)
            stage_topk(nc, g, I, l, need_ctx)
            stage_moe(nc, g, I, l, need_ctx)
            stage_residual(nc, g, I, l, need_ctx)


_INS = ['x', 'c', 'ctx', 'c_ctx', 'w_ada', 'b_ada', 'g_norm1', 'g_norm2', 'w_in', 'w_out', 'conv_w', 'g_out_conv', 'g_kv_norm',
        'w_uk', 'w_uv', 'g_q_norm', 'g_k_norm', 'g_out_mla', 'rwkv_mu', 'rwkv_w0', 'rwkv_w2', 'rwkv_a0', 'rwkv_a2', 'rwkv_g2',
        'rwkv_k_k', 'rwkv_k_a', 'rwkv_r_k', 'g_ln_x', 'g_ret_norm', 'w_router', 'b_router', 'w_gate', 'w_up', 'w_down']


def kernel(**inputs):
    import numpy as _np
    import concourse.bacc as _bacc
    from concourse import mybir as _mybir
    from concourse.bass_utils import run_bass_kernel_spmd as _run

    nc = _bacc.Bacc("TRN2", target_bir_lowering=False, num_devices=1)
    arrays, I, C = {}, {}, {}
    for name in _INS:
        a = _np.ascontiguousarray(inputs[name])
        arrays[f"in_{name}_dram"] = a
        I[name] = nc.dram_tensor(f"in_{name}_dram", a.shape, _mybir.dt.from_np(a.dtype), kind="ExternalInput").ap()
    for name, a in constants().items():
        arrays[f"const_{name}_dram"] = a
        C[name] = nc.dram_tensor(f"const_{name}_dram", a.shape, _mybir.dt.from_np(a.dtype), kind="ExternalInput").ap()
    out = nc.dram_tensor("out_0_dram", (1, SEQ, D), F32, kind="ExternalOutput").ap()
    build(nc, I, C, out)
    r = _run(nc, [arrays], core_ids=[0])
    return r.results[0]["out_0_dram"]
```

```python
from contextlib import ExitStack

import numpy as np

import concourse.bass as bass
from concourse import mybir

ALU = mybir.AluOpType
ACT = mybir.ActivationFunctionType
F32 = mybir.dt.float32
I32 = mybir.dt.int32
U32 = mybir.dt.uint32
AX_X = mybir.AxisListType.X

P = 128
D = 1024
KT = D // P
CTX, SEQ = 256, 1024
T = CTX + SEQ
NT = T // P
NCT = CTX // P
DEPTH = 2
GRID_W = 64
EPS = 1e-6
GW = 256
HD = 64
H = 4
QK = 96
C_MLA, C_RWKV, C_RET = 768, 1312, 2336
W_MLA, W_RET = 544, 1024
NE, FF = 16, 1024
CAPX, CAPC = 2 * SEQ // NE, 2 * CTX // NE
CH = 64
LEVELS = 6
LWC = -float(np.exp(-0.5))
GN_EPS = 64e-5
SPANS = [(0, 256), (256, 512), (768, 512)]


class Signal:

    def __init__(self, ctx, nc, name):
        self.sem = ctx.enter_context(nc.semaphore(name))
        self.base = 0
        self.made = 0

    def up(self, n=1):
        self.made += n
        return self.sem, n

    def at(self, k):
        return self.sem, self.base + k


class Signals:

    def __init__(self, ctx, nc):
        self.ctx, self.nc, self.by = ctx, nc, {}

    def __call__(self, name):
        if name not in self.by:
            self.by[name] = Signal(self.ctx, self.nc, name)
        return self.by[name]

    def settle(self):
        for s in self.by.values():
            s.base = s.made


def linker(eng, sig):
    def link(ins):
        ins.then_inc(*sig.up())
        eng.wait_ge(sig.sem, sig.made)
    return link




def constants():
    f = np.float32
    i = np.arange(P)
    same = (i[:, None] // CH) == (i[None, :] // CH)
    strict = same & (i[:, None] < i[None, :])
    incl = same & (i[:, None] <= i[None, :])
    masks = np.zeros((P, 2, 4, P), f)
    masks[:, 0] = np.stack([strict, incl, strict, incl], 1)
    masks[:, 1] = np.stack([strict.T, incl.T, strict.T, incl.T], 1)
    nlev = np.zeros((P, 2, LEVELS, P), f)
    for s in range(LEVELS):
        w = 1 << s
        m = ((i[None, :] // w) % 2 == 1) & ((i[:, None] // w) == (i[None, :] // w) - 1)
        nlev[:, 0, s] = -m.astype(f)
        nlev[:, 1, s] = -m.T.astype(f)
    blk = np.zeros((P, P), f)
    blk[:HD, :HD] = 1
    blk[HD:, HD:] = 1
    lg = np.log1p(-np.exp2(-5.0 - np.arange(H)))
    dist = np.abs(i[:, None] - i[None, :])
    sc = HD ** -0.5
    dmat = (np.exp(dist[:, None, :] * lg[None, :, None]) * sc).astype(f)
    head = np.arange(GW) // HD
    xi = np.zeros((P, 2, 2, P), f)
    gdec = np.zeros((P, 2), f)
    for p in range(2):
        g = lg[head[p * P:(p + 1) * P]]
        xi[:, p, 0] = np.exp(g[:, None] * (i[None, :] + 1)) * sc
        xi[:, p, 1] = np.exp(g[:, None] * (P - i[None, :])) * sc
        gdec[:, p] = np.exp(g * P)
    zeta = np.zeros((P, 2, GW), f)
    zeta[:, 0] = np.exp((P - 1 - i)[:, None] * lg[head][None, :])
    zeta[:, 1] = np.exp(i[:, None] * lg[head][None, :])
    reset = np.ones((P, T), f)
    reset[:, ::CH] = 0
    tok = np.arange(SEQ, dtype=f)
    ax = 10000.0 ** (-np.arange(0, 16, 2, dtype=f) / f(16))
    pos = [np.floor(tok / GRID_W), tok % GRID_W]
    rm = np.zeros((SEQ, 2, 2, 2, 8), f)
    for a in range(2):
        ang = (pos[a].astype(f)[:, None] * ax.astype(f)[None, :]).astype(f)
        rm[:, 0, a, :] = np.cos(ang)[:, None]
        rm[:, 1, a, 0] = -np.sin(ang)
        rm[:, 1, a, 1] = np.sin(ang)
    th = (1.0 / (10000.0 ** np.linspace(0.0, 1.0, HD // 2, dtype=f))).astype(f)
    ang = (tok[:, None] * th[None, :]).astype(f)
    rr = np.zeros((SEQ, 2, 2, HD // 2), f)
    rr[:, 0] = np.cos(ang)[:, None]
    rr[:, 1, 0] = -np.sin(ang)
    rr[:, 1, 1] = np.sin(ang)
    out = dict(sel=np.tile(np.eye(32, dtype=f), (4, 1)), ident=np.eye(P, dtype=f), ones=np.ones((P, P), f), blk=blk, masks=masks.reshape(P, -1),
               nlev=nlev.reshape(P, -1), reset=reset, dmat=dmat.reshape(P, -1), xi=xi.reshape(P, -1),
               zeta=zeta.reshape(P, -1), gdec=gdec, rope_m=rm.reshape(SEQ, -1), rope_r=rr.reshape(SEQ, -1))
    return {k: np.ascontiguousarray(v.astype(f)) for k, v in out.items()}


class Bufs:

    def __init__(self, nc, ctx, stage):
        self.nc, self.ctx, self.stage = nc, ctx, stage

    def __call__(self, name, shape, dt=F32):
        return self.ctx.enter_context(self.nc.sbuf_tensor(f"{self.stage}_{name}", shape, dt))


def col(v, n):
    return v.rearrange("(k p) -> p k", k=n)


def row(v):
    return v.partition_broadcast(P)


def stage_modulation(nc, g, I):
    sg, ps = g.sg, g.ps
    NCH = 6 * D // 512
    RW = 4
    with ExitStack() as cx:
        sb = Bufs(nc, cx, "mod")
        cc = sb("cc", [P, KT, 2])
        sc = sb("sc", [P, KT, 2])
        wa = sb("wa", [P, RW, KT, 512])
        ba = sb("ba", [2, DEPTH, 6 * D])
        mo = sb("mo", [2, 6 * D])
        w_in, c_in = [sg(f"w_slot{i}") for i in range(RW)], sg("small_in")
        silu_done, mm, used, stored = sg("silu_done"), sg("mod_mm"), sg("mod_used"), sg("stored")
        jobs = [(l, n) for l in range(DEPTH) for n in range(NCH)]
        with nc.Block() as block:
            @block.sync
            def _(sp):
                with nc.allow_non_contiguous_dma(reason="vectors into columns"):
                    sp.dma_start(cc[:, :, 0], col(I["c"][0], KT)).then_inc(*c_in.up(16))
                    sp.dma_start(cc[:, :, 1], col(I["c_ctx"], KT)).then_inc(*c_in.up(16))
                for l in range(DEPTH):
                    sp.dma_start(ba[:, l, :], I["b_ada"][l].partition_broadcast(2)).then_inc(*c_in.up(16))
                for j, (l, n) in enumerate(jobs):
                    if j >= RW:
                        sp.wait_ge(*mm.at(j - RW + 1))
                    sp.dma_start(wa[:, j % RW], I["w_ada"][l].rearrange("(k p) f -> p k f", p=P)
                                 [:, :, n * 512:(n + 1) * 512]).then_inc(*w_in[j % RW].up(16))

            @block.scalar
            def _(act):
                act.wait_ge(*c_in.at(16 * (2 + DEPTH)))
                nc.scalar.activation(sc[:], cc[:], ACT.Silu).then_inc(*silu_done.up())
                for l in range(DEPTH):
                    act.wait_ge(*used.at((l + 1) * NCH))
                    act.dma_start(g.mod[l], mo[:]).then_inc(*stored.up(16))
                act.wait_ge(*stored.at(16 * DEPTH))

            @block.tensor
            def _(pe):
                pe.wait_ge(*silu_done.at(1))
                for j, (l, n) in enumerate(jobs):
                    pe.wait_ge(*w_in[j % RW].at(16 * (j // RW + 1)))
                    if j >= 4:
                        pe.wait_ge(*used.at(j - 3))
                    for k in range(KT):
                        ins = nc.tensor.matmul(ps[0:2, j % 4, :], sc[:, k, :], wa[:, j % RW, k, :],
                                               start=(k == 0), stop=(k == KT - 1))
                    ins.then_inc(*mm.up())

            @block.vector
            def _(dve):
                dve.wait_ge(*c_in.at(16 * (2 + DEPTH)))
                for j, (l, n) in enumerate(jobs):
                    dve.wait_ge(*mm.at(j + 1))
                    if j == NCH:
                        dve.wait_ge(*stored.at(16))
                    s = slice(n * 512, (n + 1) * 512)
                    nc.vector.tensor_tensor(mo[:, s], ps[0:2, j % 4, :], ba[:, l, s], ALU.add).then_inc(*used.up())
        sg.settle()


def stage_norm1(nc, g, I, l):
    sg, ps, hT = g.sg, g.ps, g.hT
    with ExitStack() as cx:
        sb = Bufs(nc, cx, f"n{l}")
        xb = sb("xb", [P, 3, D])
        xn = sb("xn", [P, 2, D])
        junk = sb("junk", [P, D])
        ss = sb("ss", [P, NT])
        rs = sb("rs", [P, NT])
        mc = sb("mc", [P, 2, 2, KT])
        gn = sb("gn", [P, KT])
        G = sb("G", [P, 2, KT])
        join = l > 0
        if join:
            rows = sb("rows", [P, 2, D])
            ab = sb("ab", [P, 3, D])
        joined, xs = sg("x_joined"), [sg(f"out_slot{i}") for i in range(3)]
        n_small, n_x = (7, 32) if join else (5, 16)
        x_in, small, sq, normed = [sg(f"w_slot{i}") for i in range(3)], sg("small_in"), sg("sq_done"), sg("normed")
        tr, ev_a, ev_d, coef, chain = sg("transposed"), sg("evac_a"), sg("evac_d"), sg("coef"), sg("dve_chain")
        with nc.Block() as block:
            @block.sync
            def _(sp):
                with nc.allow_non_contiguous_dma(reason="vectors into columns"):
                    for s in range(2):
                        for w in range(2):
                            sp.dma_start(mc[:, s, w], col(g.mod[l, s, w * D:(w + 1) * D], KT)).then_inc(*small.up(16))
                    sp.dma_start(gn[:], col(I["g_norm1"][l], KT)).then_inc(*small.up(16))
                for s in range(2 if join else 0):
                    sp.dma_start(rows[:, s], row(g.mod[l - 1, s, 5 * D:6 * D])).then_inc(*small.up(16))
                for t in range(NT):
                    if t >= 3:
                        sp.wait_ge(*normed.at(t - 2))
                        if join:
                            sp.wait_ge(*xs[t % 3].at(16 * (t // 3)))
                    sp.dma_start(xb[:, t % 3], g.x_rows(I, l, t)).then_inc(*x_in[t % 3].up(16))
                    if join:
                        sp.dma_start(ab[:, t % 3], g.acc[t * P:(t + 1) * P]).then_inc(*x_in[t % 3].up(16))

            def evac_act(act, t):
                act.wait_ge(*tr.at(2 * t + 1))
                s = 1 if t < NCT else 0
                for k in range(4):
                    ins = nc.scalar.activation(hT[:, k, t * P:(t + 1) * P], ps[:, 2 * (t % 2), k * P:(k + 1) * P],
                                               ACT.Identity, bias=mc[:, s, 0, k:k + 1], scale=G[:, s, k:k + 1])
                ins.then_inc(*ev_a.up())

            @block.scalar
            def _(act):
                act.wait_ge(*coef.at(2))
                for t in range(NT):
                    if join:
                        act.wait_ge(*joined.at(t + 1))
                    else:
                        act.wait_ge(*x_in[t % 3].at(n_x * (t // 3 + 1)))
                    if t >= 1:
                        act.wait_ge(*sq.at(t))
                    nc.scalar.activation(junk[:], xb[:, t % 3], ACT.Square, accum_out=ss[:, t:t + 1]).then_inc(*sq.up())
                    if t >= 1:
                        evac_act(act, t - 1)
                evac_act(act, NT - 1)

            def evac_dve(dve, t):
                dve.wait_ge(*tr.at(2 * t + 2))
                s = 1 if t < NCT else 0
                for k in range(4, 8):
                    ins = nc.vector.tensor_scalar(hT[:, k, t * P:(t + 1) * P], ps[:, 2 * (t % 2) + 1, (k - 4) * P:(k - 3) * P],
                                                  G[:, s, k:k + 1], mc[:, s, 0, k:k + 1], ALU.mult, ALU.add)
                ins.then_inc(*ev_d.up())

            @block.vector
            def _(dve):
                link = linker(dve, chain)
                dve.wait_ge(*small.at(16 * n_small))
                for s in range(2):
                    nc.vector.scalar_tensor_tensor(G[:, s], mc[:, s, 1], 1.0, gn[:], ALU.add, ALU.mult).then_inc(*coef.up())
                dve.wait_ge(*coef.at(2))

                def add_experts(t):
                    dve.wait_ge(*x_in[t % 3].at(n_x * (t // 3 + 1)))
                    link(nc.vector.tensor_tensor(ab[:, t % 3], ab[:, t % 3], rows[:, 1 if t < NCT else 0], ALU.mult))
                    nc.vector.tensor_tensor(xb[:, t % 3], xb[:, t % 3], ab[:, t % 3], ALU.add).then_inc(*joined.up())

                if join:
                    add_experts(0)
                for t in range(NT):
                    if join and t + 1 < NT:
                        add_experts(t + 1)
                    dve.wait_ge(*sq.at(t + 1))
                    nc.vector.tensor_scalar(rs[:, t:t + 1], ss[:, t:t + 1], 1.0 / D, EPS, ALU.mult, ALU.add).then_inc(*g.vr.up())
                    dve.wait_ge(*g.rq.at(t + 1))
                    if t >= 2:
                        dve.wait_ge(*tr.at(2 * (t - 1)))
                    nc.vector.tensor_scalar(xn[:, t % 2], xb[:, t % 3], rs[:, t:t + 1], None, ALU.mult).then_inc(*normed.up())
                    if t >= 1:
                        evac_dve(dve, t - 1)
                evac_dve(dve, NT - 1)

            @block.gpsimd
            def _(pool):
                def store(t):
                    pool.wait_ge(*joined.at(t + 1))
                    pool.dma_start(g.x[t * P:(t + 1) * P], xb[:, t % 3]).then_inc(*xs[t % 3].up(16))

                if join:
                    store(0)
                for t in range(NT):
                    if join and t + 1 < NT:
                        store(t + 1)
                    pool.wait_ge(*g.vr.at(t + 1))
                    nc.gpsimd.tensor_tensor(rs[:, t:t + 1], rs[:, t:t + 1], g.mhalf[:, 0:1], ALU.pow).then_inc(*g.rq.up())
                for s in xs if join else []:
                    pool.wait_ge(s.sem, s.made)

            @block.tensor
            def _(pe):
                for t in range(NT):
                    pe.wait_ge(*normed.at(t + 1))
                    for half in range(2):
                        if t >= 2:
                            pe.wait_ge(*(ev_d if half else ev_a).at(t - 1))
                        for k in range(4):
                            ins = nc.tensor.transpose(ps[:, 2 * (t % 2) + half, k * P:(k + 1) * P],
                                                      xn[:, t % 2, (4 * half + k) * P:(4 * half + k + 1) * P], g.ident)
                        ins.then_inc(*tr.up())
        sg.settle()


def stage_project(nc, g, I, l, M):
    sg, ps, hT, yT = g.sg, g.ps, g.hT, g.yT
    groups = [(0, 512, "conv", 0), (512, 256, "conv", 4),
              (C_MLA, 272, "tok", 0), (C_MLA + 272, 272, "tok", 272), (C_RET, 512, "tok", W_MLA), (C_RET + 512, 512, "tok", W_MLA + 512),
              (C_RWKV, 512, "rwkv", 0), (C_RWKV + 512, 512, "rwkv", 4)]
    jobs = []
    for n, (c0, w, kind, o) in enumerate(groups):
        if kind == "tok":
            jobs += [(n, t, None) for t in range(NT)]
        else:
            jobs += [(n, m, s) for m in range(w // P) for s in range(3)]
    lastjob = [max(j for j, x in enumerate(jobs) if x[0] == n) for n in range(len(groups))]
    tok0 = lastjob[1] + 1
    rw0 = lastjob[5] + 1
    NB, RW, RO = 6, 3, 6
    SQ_AT, SUM_AT, SUM2_AT = 14, 18, 24
    with ExitStack() as cx:
        sb = Bufs(nc, cx, f"p{l}")
        w = sb("w", [P, RW, KT, 512])
        zo = sb("zo", [P, RO, 512])
        z = sb("z", [P, 2, T + 4])
        tmp = sb("tmp", [P, T + 2])
        mu, hmu, omu = sb("mu", [P, 8]), sb("hmu", [P, 8]), sb("omu", [P, 8])
        cw, go = sb("cw", [P, 3, 2]), sb("go", [P, 2])
        w_in = [sg(f"w_slot{i}") for i in range(RW)]
        st = [sg(f"out_slot{i}") for i in range(RO)]
        mm, ev, small, chain = sg("mm_done"), [sg("evac_a"), sg("evac_d")], sg("small_in"), sg("dve_chain")
        pad, prod, sqd, csum, vard, lnd, mixed = (sg(n) for n in ("coef", "cv_prod", "sq_done", "cv_sum", "cv_var", "ln_done", "mixed"))

        def tile_of(j):
            return groups[jobs[j][0]][3] + jobs[j][1]

        def target(j):
            n, m, s = jobs[j]
            kind, o = groups[n][2], groups[n][3]
            if kind == "tok":
                return zo[:, (j - tok0) % RO, 0:groups[n][1]], groups[n][1]
            t0, tw = SPANS[s]
            if kind == "conv":
                return M[:, o + m, t0:t0 + tw], tw
            a = t0 + (1 if t0 < CTX else 3)
            return z[:, (o + m) % 2, a:a + tw], tw

        def wait_target(eng, j):
            if j >= rw0:
                if tile_of(j) >= 2:
                    eng.wait_ge(*mixed.at(tile_of(j) - 1))
                else:
                    eng.wait_ge(*vard.at(2))
            elif j >= tok0 + RO:
                k = j - tok0
                eng.wait_ge(*st[k % RO].at(16 * (k // RO)))

        with nc.Block() as block:
            @block.sync
            def _(sp):
                for n, (c0, wd, kind, o) in enumerate(groups):
                    if n >= RW:
                        sp.wait_ge(*mm.at(lastjob[n - RW] + 1))
                    sp.dma_start(w[:, n % RW, :, 0:wd], I["w_in"][l].rearrange("(k p) f -> p k f", p=P)[:, :, c0:c0 + wd]) \
                        .then_inc(*w_in[n % RW].up(16))
                    if n == 1:
                        with nc.allow_non_contiguous_dma(reason="vectors into columns"):
                            sp.dma_start(mu[:], col(I["rwkv_mu"][l], 8)).then_inc(*small.up(16))
                            for i in range(3):
                                sp.dma_start(cw[:, i], col(I["conv_w"][l, i], 2)).then_inc(*small.up(16))
                            sp.dma_start(go[:], col(I["g_out_conv"][l], 2)).then_inc(*small.up(16))

            @block.tensor
            def _(pe):
                def squares_sum(s, b):
                    t0, tw = SPANS[s]
                    for i in range(2):
                        ins = nc.tensor.matmul(ps[:, b, 0:tw], g.ones, M[:, 4 + i, t0:t0 + tw], start=(i == 0), stop=(i == 1))
                    ins.then_inc(*csum.up())

                for j, (n, m, s) in enumerate(jobs):
                    if j == 0 or jobs[j - 1][0] != n:
                        pe.wait_ge(*w_in[n % RW].at(16 * (n // RW + 1)))
                    if j >= NB:
                        pe.wait_ge(*ev[j % 2].at((j - NB) // 2 + 1))
                    wd = groups[n][1]
                    for k in range(KT):
                        if s is not None:
                            t0, tw = SPANS[s]
                            ins = nc.tensor.matmul(ps[:, j % NB, 0:tw], w[:, n % RW, k, m * P:(m + 1) * P], hT[:, k, t0:t0 + tw],
                                                   start=(k == 0), stop=(k == KT - 1))
                        else:
                            ins = nc.tensor.matmul(ps[:, j % NB, 0:wd], hT[:, k, m * P:(m + 1) * P], w[:, n % RW, k, 0:wd],
                                                   start=(k == 0), stop=(k == KT - 1))
                    ins.then_inc(*mm.up())
                    if j == tok0 + SUM_AT:
                        pe.wait_ge(*sqd.at(2))
                        squares_sum(0, 6)
                        squares_sum(1, 7)
                    if j == tok0 + SUM2_AT:
                        pe.wait_ge(*vard.at(1))
                        squares_sum(2, 6)

            @block.scalar
            def _(act):
                for j in range(0, len(jobs), 2):
                    act.wait_ge(*mm.at(j + 1))
                    wait_target(act, j)
                    dst, wd = target(j)
                    nc.scalar.copy(dst, ps[:, j % NB, 0:wd]).then_inc(*ev[0].up())
                    if j == tok0 + SQ_AT:
                        for i in range(2):
                            act.wait_ge(*prod.at(i + 1))
                            nc.scalar.activation(M[:, 4 + i], M[:, 2 + i], ACT.Square).then_inc(*sqd.up())
                    if j == tok0 + SUM2_AT + 4:
                        act.wait_ge(*vard.at(2))
                        nc.scalar.activation(M[:, 0], M[:, 0], ACT.Ln).then_inc(*lnd.up())
                        act.wait_ge(*lnd.at(1))
                        nc.scalar.activation(M[:, 0], M[:, 0], ACT.Exp, scale=-0.5).then_inc(*g.rq.up())
                act.wait_ge(*mixed.at(7))
                nc.scalar.activation(M[0:64, 6], M[0:64, 6], ACT.Tanh)
                act.wait_ge(*mixed.at(8))
                nc.scalar.activation(M[:, 7], M[:, 7], ACT.Sigmoid)

            @block.vector
            def _(dve):
                link = linker(dve, chain)

                def conv(n):
                    i, part = divmod(n, 5)
                    u, y = z[:, i], M[:, 2 + i]
                    if part == 0:
                        if i == 0:
                            dve.wait_ge(*ev[0].at(tok0 // 2))
                            dve.wait_ge(*ev[1].at(tok0 // 2))
                            dve.wait_ge(*small.at(80))
                        link(nc.vector.tensor_tensor(u[:, 1:CTX + 1], M[:, 2 + i, 0:CTX], M[:, 4 + i, 0:CTX], ALU.mult))
                        link(nc.vector.tensor_tensor(u[:, CTX + 3:T + 3], M[:, 2 + i, CTX:T], M[:, 4 + i, CTX:T], ALU.mult))
                    elif part < 4:
                        for a, b, o in ((0, CTX, part - 1), (CTX, T, part + 1)):
                            if part == 1:
                                ins = nc.vector.tensor_scalar(y[:, a:b], u[:, a + o:b + o], cw[:, 0, i:i + 1], None, ALU.mult)
                            else:
                                ins = nc.vector.scalar_tensor_tensor(y[:, a:b], u[:, a + o:b + o], cw[:, part - 1, i:i + 1], y[:, a:b],
                                                                     ALU.mult, ALU.add)
                            link(ins)
                    else:
                        nc.vector.tensor_tensor(y, y, M[:, i], ALU.mult).then_inc(*prod.up())

                def variance(spans, b):
                    for s in spans:
                        t0, tw = SPANS[s]
                        dve.wait_ge(*csum.at(s + 1))
                        ins = nc.vector.tensor_scalar(M[:, 0, t0:t0 + tw], ps[:, 6 + s % 2, 0:tw], 1.0 / GW, EPS, ALU.mult, ALU.add)
                    ins.then_inc(*vard.up())

                def mix(i):
                    zz = z[:, i % 2]
                    last = rw0 + 3 * i + 2
                    for j in (last, last - 1):
                        dve.wait_ge(*ev[j % 2].at(j // 2 + 1))
                    link(nc.vector.tensor_tensor(tmp[:], zz[:, 0:T + 2], zz[:, 2:T + 4], ALU.add))
                    link(nc.vector.tensor_scalar(tmp[:], tmp[:], hmu[:, i:i + 1], None, ALU.mult))
                    link(nc.vector.scalar_tensor_tensor(M[:, i, 0:CTX], zz[:, 1:CTX + 1], omu[:, i:i + 1], tmp[:, 0:CTX], ALU.mult, ALU.add))
                    nc.vector.scalar_tensor_tensor(M[:, i, CTX:T], zz[:, CTX + 3:T + 3], omu[:, i:i + 1], tmp[:, CTX + 2:T + 2],
                                                   ALU.mult, ALU.add).then_inc(*mixed.up())
                    dve.wait_ge(*mixed.at(i + 1))

                link(nc.vector.memset(z[:], 0.0))
                for j in range(1, len(jobs), 2):
                    dve.wait_ge(*mm.at(j + 1))
                    wait_target(dve, j)
                    dst, wd = target(j)
                    nc.vector.tensor_copy(dst, ps[:, j % NB, 0:wd]).then_inc(*ev[1].up())
                    k = (j - tok0) // 2
                    if j > tok0 and k < 5:
                        conv(2 * k)
                        conv(2 * k + 1)
                    if j == tok0 + SUM_AT + 1:
                        variance((0, 1), 6)
                    if j == tok0 + SUM2_AT + 1:
                        variance((2,), 6)
                        link(nc.vector.tensor_scalar(hmu[:], mu[:], 0.5, None, ALU.mult))
                        link(nc.vector.tensor_scalar(omu[:], mu[:], -1.0, 1.0, ALU.mult, ALU.add))
                    if j == tok0 + SUM2_AT + 7:
                        dve.wait_ge(*g.rq.at(1))
                        for i in range(2):
                            ins = nc.vector.scalar_tensor_tensor(yT[:, i], M[:, 2 + i], go[:, i:i + 1], M[:, 0], ALU.mult, ALU.mult)
                            link(ins)
                    if j >= rw0 and tile_of(j) >= 1 and (j + 2 >= len(jobs) or tile_of(j + 2) > tile_of(j)):
                        mix(tile_of(j) - 1)
                mix(7)

            @block.gpsimd
            def _(pool):
                for j in range(tok0, rw0):
                    n, t, _ = jobs[j]
                    pool.wait_ge(*ev[j % 2].at(j // 2 + 1))
                    o, wd = groups[n][3], groups[n][1]
                    pool.dma_start(g.zt[t * P:(t + 1) * P, o:o + wd], zo[:, (j - tok0) % RO, 0:wd]).then_inc(*st[(j - tok0) % RO].up(16))
                for s in st:
                    pool.wait_ge(s.sem, s.made)
        sg.settle()


def stage_mla_prep(nc, g, I, l, S):
    sg, ps = g.sg, g.ps
    QT, KTr, V = S["QT"], S["KT"], S["V"]
    with ExitStack() as cx:
        sb = Bufs(nc, cx, f"m{l}")
        z = sb("z", [P, 3, W_MLA])
        rope = sb("rope", [P, SEQ // P, 2, 32])
        wkv = sb("wkv", [P, 512])
        gkv = sb("gkv", [P, 1])
        gqk = sb("gqk", [P, 2, QK])
        junk = sb("junk", [P, P])
        st = sb("st", [P, NT, 2])
        cn = sb("cn", [P, P])
        cT = sb("cT", [P, P])
        qk = sb("qk", [P, 2, 8, QK])
        sq = sb("sq", [P, 8, QK])
        s8 = sb("s8", [P, 8])
        ra = sb("ra", [P, 8, 32])
        rb = sb("rb", [P, 8, 32])
        z_in, small, chain = [sg(f"w_slot{i}") for i in range(3)], sg("small_in"), sg("dve_chain")
        sqd, cnd, ctd, cte, kvd, gath = sg("sq_done"), sg("normed"), sg("mla_ct"), sg("mla_cte"), sg("mm_done"), sg("mla_gath")
        kvr, qkd, tr, ev = sg("mla_kvr"), sg("mla_qk"), sg("transposed"), [sg("evac_a"), sg("mla_ke")]
        ones = sg("mla_ones")

        def n_latent(t):
            return 2 * t if t else 1

        def n_head(t):
            return min(2 * t + 3, 2 * NT)

        with nc.Block() as block:
            @block.sync
            def _(sp):
                sp.dma_start(wkv[:, 0:GW], I["w_uk"][l]).then_inc(*small.up(16))
                sp.dma_start(wkv[:, GW:2 * GW], I["w_uv"][l]).then_inc(*small.up(16))
                with nc.allow_non_contiguous_dma(reason="vectors into columns"):
                    sp.dma_start(gkv[:], col(I["g_kv_norm"][l], 1)).then_inc(*small.up(16))
                sp.dma_start(gqk[:, 0], row(I["g_q_norm"][l])).then_inc(*small.up(16))
                sp.dma_start(gqk[:, 1], row(I["g_k_norm"][l])).then_inc(*small.up(16))
                sp.dma_start(rope[:], g.C["rope_m"].rearrange("(t p) (c f) -> p t c f", p=P, c=2)).then_inc(*small.up(16))
                for t in range(NT):
                    if t >= 3:
                        sp.wait_ge(*gath.at(t - 2))
                    sp.dma_start(z[:, t % 3], g.zt[t * P:(t + 1) * P, 0:W_MLA]).then_inc(*z_in[t % 3].up(16))

            @block.scalar
            def _(act):
                def squares(t):
                    act.wait_ge(*z_in[t % 3].at(16 * (t // 3 + 1)))
                    if t >= 1:
                        act.wait_ge(*sqd.at(t))
                    nc.scalar.activation(junk[:], z[:, t % 3, 384:512], ACT.Square, accum_out=st[:, t, 0:1]).then_inc(*sqd.up())

                def gather(t):
                    zz, q = z[:, t % 3], qk[:, t % 2]
                    if t >= 2:
                        act.wait_ge(*tr.at(2 * (t - 1)))
                    nc.scalar.copy(q[:, 0:4, 0:64], zz[:, 0:256].rearrange("p (h d) -> p h d", h=4))
                    nc.scalar.copy(q[:, 0:4, 64:96], zz[:, 256:384].rearrange("p (h d) -> p h d", h=4))
                    act.wait_ge(*cnd.at(t + 1))
                    nc.scalar.copy(q[:, 4:8, 64:96], zz[:, 512:544].unsqueeze(1).broadcast_to([P, 4, 32])).then_inc(*gath.up())
                    act.wait_ge(*ctd.at(t + 1))
                    nc.scalar.activation(cT[:], ps[:, 0, 0:P], ACT.Copy, scale=gkv[:, 0:1]).then_inc(*cte.up())
                    act.wait_ge(*kvd.at(t + 1))
                    nc.scalar.copy(q[:, 4:8, 0:64], ps[:, 1, 0:256].rearrange("p (h d) -> p h d", h=4))
                    nc.scalar.copy(V[:, t, :, 0:64], ps[:, 1, 256:512].rearrange("p (h d) -> p h d", h=4)).then_inc(*kvr.up())

                def put_out(t):
                    for i, dst in enumerate((QT, KTr)):
                        act.wait_ge(*tr.at(2 * t + 1 + i))
                        nc.scalar.copy(dst[0:QK, :, t * P:(t + 1) * P], ps[0:QK, 2 + i, :].rearrange("p (h d) -> p h d", h=4)) \
                            .then_inc(*ev[i].up())

                act.wait_ge(*small.at(96))
                act.wait_ge(*ones.at(1))
                squares(0)
                for t in range(NT):
                    if t + 1 < NT:
                        squares(t + 1)
                    gather(t)
                    if t >= 1:
                        put_out(t - 1)
                put_out(NT - 1)

            @block.vector
            def _(dve):
                link = linker(dve, chain)
                def latent_variance(t):
                    dve.wait_ge(*sqd.at(t + 1))
                    nc.vector.tensor_scalar(st[:, t, 1:2], st[:, t, 0:1], 1.0 / P, EPS, ALU.mult, ALU.add).then_inc(*g.vr.up())

                def latent(t):
                    dve.wait_ge(*g.rq.at(n_latent(t)))
                    if t >= 1:
                        dve.wait_ge(*ctd.at(t))
                    nc.vector.tensor_scalar(cn[:], z[:, t % 3, 384:512], st[:, t, 1:2], None, ALU.mult).then_inc(*cnd.up())

                def head_variance(t):
                    q = qk[:, t % 2]
                    dve.wait_ge(*kvr.at(t + 1))
                    link(nc.vector.tensor_tensor(sq[:], q, q, ALU.mult))
                    link(nc.vector.tensor_reduce(s8[:], sq[:], AX_X, ALU.add))
                    nc.vector.tensor_scalar(s8[:], s8[:], 1.0 / QK, EPS, ALU.mult, ALU.add).then_inc(*g.vr.up())

                def norm_rotate(t):
                    q = qk[:, t % 2]
                    dve.wait_ge(*g.rq.at(n_head(t)))
                    link(nc.vector.tensor_tensor(q, q, s8[:].unsqueeze(2).broadcast_to([P, 8, QK]), ALU.mult))
                    for i in range(2):
                        ins = nc.vector.tensor_tensor(q[:, 4 * i:4 * i + 4], q[:, 4 * i:4 * i + 4],
                                                      gqk[:, i].unsqueeze(1).broadcast_to([P, 4, QK]), ALU.mult)
                        if i == 0 or t >= NCT:
                            link(ins)
                    if t >= NCT:
                        r = rope[:, t - NCT]
                        link(nc.vector.tensor_tensor(ra[:], q[:, :, 64:96], r[:, 0].unsqueeze(1).broadcast_to([P, 8, 32]), ALU.mult))
                        q5 = q[:, :, 64:96].rearrange("p h (a s f) -> p h a s f", a=2, s=2)
                        b5 = rb[:].rearrange("p h (a s f) -> p h a s f", a=2, s=2)
                        r5 = r[:, 1].rearrange("p (a s f) -> p a s f", a=2, s=2)
                        for s in range(2):
                            link(nc.vector.tensor_tensor(b5[:, :, :, s], q5[:, :, :, 1 - s],
                                                         r5[:, :, s].unsqueeze(1).broadcast_to([P, 8, 2, 8]), ALU.mult))
                        ins = nc.vector.tensor_tensor(q[:, :, 64:96], ra[:], rb[:], ALU.add)
                    ins.then_inc(*qkd.up())

                link(nc.vector.memset(V[:, :, :, 64:65], 1.0))
                nc.vector.memset(KTr[QK:QK + 1], 1.0).then_inc(*ones.up())
                dve.wait_ge(*small.at(96))
                latent_variance(0)
                latent(0)
                for t in range(NT):
                    if t + 1 < NT:
                        latent_variance(t + 1)
                    head_variance(t)
                    if t + 1 < NT:
                        latent(t + 1)
                    norm_rotate(t)

            @block.gpsimd
            def _(pool):
                def latent(t):
                    pool.wait_ge(*g.vr.at(n_latent(t)))
                    nc.gpsimd.tensor_tensor(st[:, t, 1:2], st[:, t, 1:2], g.mhalf[:, 0:1], ALU.pow).then_inc(*g.rq.up())

                latent(0)
                for t in range(NT):
                    if t + 1 < NT:
                        latent(t + 1)
                    pool.wait_ge(*g.vr.at(n_head(t)))
                    nc.gpsimd.tensor_tensor(s8[:], s8[:], g.mhalf[:, 0:8], ALU.pow).then_inc(*g.rq.up())

            @block.tensor
            def _(pe):
                def heads(t):
                    pe.wait_ge(*qkd.at(t + 1))
                    for i in range(2):
                        if t >= 1:
                            pe.wait_ge(*ev[i].at(t))
                        for h in range(4):
                            ins = nc.tensor.transpose(ps[0:QK, 2 + i, h * P:(h + 1) * P], qk[:, t % 2, 4 * i + h], g.ident)
                        ins.then_inc(*tr.up())

                for t in range(NT):
                    pe.wait_ge(*cnd.at(t + 1))
                    if t >= 1:
                        pe.wait_ge(*cte.at(t))
                    nc.tensor.transpose(ps[:, 0, 0:P], cn[:], g.ident).then_inc(*ctd.up())
                    pe.wait_ge(*cte.at(t + 1))
                    if t >= 1:
                        pe.wait_ge(*kvr.at(t))
                    nc.tensor.matmul(ps[:, 1, :], cT[:], wkv[:], start=True, stop=True).then_inc(*kvd.up())
                    if t >= 1:
                        heads(t - 1)
                heads(NT - 1)
        sg.settle()


def stage_mla_attend(nc, g, I, l, S, need_ctx):
    sg, ps, yT = g.sg, g.ps, g.yT
    QT, KTr, V = S["QT"], S["KT"], S["V"]
    SCALE = QK ** -0.5
    groups = ([(0, CTX, NCT)] if need_ctx else []) + [(CTX, 512, NT), (CTX + 512, 512, NT)]
    NP = 3
    with ExitStack() as cx:
        sb = Bufs(nc, cx, f"a{l}")
        mx = sb("mx", [P, 2, H])
        pt = sb("pt", [P, NP, 512])
        ot = sb("ot", [65, H, 512])
        o = sb("o", [P, GW])
        on = sb("on", [P, 2, GW])
        junk = sb("junk", [P, GW])
        rc = sb("rc", [P, H])
        ss = sb("ss", [P, 2])
        go = sb("go", [P, 2])
        small, chain = sg("small_in"), sg("dve_chain")
        sc, mxd, mt, mrow = sg("at_sc"), sg("at_mx"), sg("at_mt"), sg("at_mrow")
        st, ex, pv, ote = sg("at_st"), sg("at_ex"), sg("at_pv"), sg("at_ote")
        otr, od, sqd, ond, ytr, ye = sg("at_otr"), sg("at_od"), sg("sq_done"), sg("normed"), sg("transposed"), sg("evac_a")
        with nc.Block() as block:
            @block.sync
            def _(sp):
                with nc.allow_non_contiguous_dma(reason="vectors into columns"):
                    sp.dma_start(go[:], col(I["g_out_mla"][l], 2)).then_inc(*small.up(16))

            @block.tensor
            def _(pe):
                nsc = nst = nq = nh = 0
                for q0, qw, nk in groups:
                    keys = nk * P
                    if nq:
                        pe.wait_ge(*ye.at(nq))
                    for qt in range(qw // P):
                        qs = slice(q0 + qt * P, q0 + (qt + 1) * P)
                        for h in range(H):
                            if nsc >= 2:
                                pe.wait_ge(*mxd.at(nsc - 1))
                            b = 3 * (nsc % 2)
                            for n in range(0, keys, 512):
                                kw = min(512, keys - n)
                                ins = nc.tensor.matmul(ps[:, b + n // 512, 0:kw], QT[0:QK, h, qs], KTr[0:QK, h, n:n + kw],
                                                       start=True, stop=True)
                            ins.then_inc(*sc.up())
                            nsc += 1
                        pe.wait_ge(*mxd.at(nsc))
                        if nq >= 1:
                            pe.wait_ge(*mrow.at(nq))
                        for h in range(H):
                            ins = nc.tensor.matmul(ps[96:97, 6, h * P:(h + 1) * P], mx[:, nq % 2, h:h + 1], g.ident,
                                                   start=True, stop=True)
                        ins.then_inc(*mt.up())
                        nq += 1
                    pe.wait_ge(*mrow.at(nq))
                    for h in range(H):
                        def scores_t(kt):
                            n = nst + kt
                            if n >= 4:
                                pe.wait_ge(*ex.at(n - 3))
                            nc.tensor.matmul(ps[:, n % 4, 0:qw], KTr[0:QK + 1, h, kt * P:(kt + 1) * P],
                                             QT[0:QK + 1, h, q0:q0 + qw], start=True, stop=True).then_inc(*st.up())
                        for kt in range(min(2, nk)):
                            scores_t(kt)
                        for kt in range(nk):
                            if kt + 2 < nk:
                                scores_t(kt + 2)
                            pe.wait_ge(*ex.at(nst + kt + 1))
                            if kt == 0 and nh >= 2:
                                pe.wait_ge(*ote.at(nh - 1))
                            nc.tensor.matmul(ps[0:65, 4 + nh % 2, 0:qw], V[:, kt, h], pt[:, (nst + kt) % NP, 0:qw],
                                             start=(kt == 0), stop=(kt == nk - 1)).then_inc(*pv.up())
                        nst += nk
                        nh += 1
                    pe.wait_ge(*ote.at(nh))
                    for qt in range(qw // P):
                        n = nq - qw // P + qt
                        if n >= 1:
                            pe.wait_ge(*od.at(n))
                        for h in range(H):
                            ins = nc.tensor.transpose(ps[:, 7, h * 65:(h + 1) * 65], ot[:, h, qt * P:(qt + 1) * P], g.ident[0:65, 0:65])
                        ins.then_inc(*otr.up())
                        pe.wait_ge(*ond.at(n + 1))
                        if n >= 1:
                            pe.wait_ge(*ye.at(n))
                        for i in range(2):
                            ins = nc.tensor.transpose(ps[:, 6, i * P:(i + 1) * P], on[:, n % 2, i * P:(i + 1) * P], g.ident)
                        ins.then_inc(*ytr.up())

            @block.gpsimd
            def _(pool):
                for n in range(sum(qw // P for _, qw, _ in groups)):
                    pool.wait_ge(*g.vr.at(n + 1))
                    nc.gpsimd.tensor_tensor(ss[:, 1:2], ss[:, 1:2], g.mhalf[:, 0:1], ALU.pow).then_inc(*g.rq.up())

            @block.vector
            def _(dve):
                link = linker(dve, chain)
                nsc = nq = 0
                for q0, qw, nk in groups:
                    keys = nk * P
                    for qt in range(qw // P):
                        for h in range(H):
                            dve.wait_ge(*sc.at(nsc + 1))
                            if h == 0 and nq >= 2:
                                dve.wait_ge(*mt.at(nq - 1))
                            b = 3 * (nsc % 2)
                            src = ps[:, b:b + 3, :].rearrange("p b n -> p (b n)")[:, 0:keys]
                            nc.vector.reduce_max(mx[:, nq % 2, h:h + 1], src, AX_X).then_inc(*mxd.up())
                            nsc += 1
                        nq += 1
                    for qt in range(qw // P):
                        n = nq - qw // P + qt
                        dve.wait_ge(*otr.at(n + 1))
                        pss = ps[:, 7, 0:260].rearrange("p (h d) -> p h d", h=H)
                        link(nc.vector.reciprocal(rc[:], pss[:, :, 64]))
                        nc.vector.tensor_tensor(o[:].rearrange("p (h d) -> p h d", h=H), pss[:, :, 0:64],
                                                rc[:].unsqueeze(2).broadcast_to([P, H, 64]), ALU.mult).then_inc(*od.up())
                        dve.wait_ge(*sqd.at(n + 1))
                        nc.vector.tensor_scalar(ss[:, 1:2], ss[:, 0:1], 1.0 / GW, EPS, ALU.mult, ALU.add).then_inc(*g.vr.up())
                        dve.wait_ge(*g.rq.at(n + 1))
                        if n >= 2:
                            dve.wait_ge(*ytr.at(n - 1))
                        nc.vector.tensor_scalar(on[:, n % 2], o[:], ss[:, 1:2], None, ALU.mult).then_inc(*ond.up())

            @block.scalar
            def _(act):
                act.wait_ge(*small.at(16))
                nq = nst = nh = 0
                for q0, qw, nk in groups:
                    for qt in range(qw // P):
                        act.wait_ge(*mt.at(nq + 1))
                        nc.scalar.activation(QT[96:97, :, q0 + qt * P:q0 + (qt + 1) * P],
                                             ps[96:97, 6, :].rearrange("p (h d) -> p h d", h=H), ACT.Copy, scale=-1.0).then_inc(*mrow.up())
                        nq += 1
                    for h in range(H):
                        for kt in range(nk):
                            act.wait_ge(*st.at(nst + 1))
                            if nst >= NP:
                                act.wait_ge(*pv.at(nst - NP + 1))
                            nc.scalar.activation(pt[:, nst % NP, 0:qw], ps[:, nst % 4, 0:qw], ACT.Exp, scale=SCALE).then_inc(*ex.up())
                            nst += 1
                        act.wait_ge(*pv.at(nst))
                        nc.scalar.copy(ot[:, h, 0:qw], ps[0:65, 4 + nh % 2, 0:qw]).then_inc(*ote.up())
                        nh += 1
                    for qt in range(qw // P):
                        n = nq - qw // P + qt
                        act.wait_ge(*od.at(n + 1))
                        if n >= 1:
                            act.wait_ge(*sqd.at(n))
                        nc.scalar.activation(junk[:], o[:], ACT.Square, accum_out=ss[:, 0:1]).then_inc(*sqd.up())
                        act.wait_ge(*ytr.at(n + 1))
                        for i in range(2):
                            ins = nc.scalar.activation(yT[:, 2 + i, q0 + qt * P:q0 + (qt + 1) * P], ps[:, 6, i * P:(i + 1) * P],
                                                       ACT.Copy, scale=go[:, i:i + 1])
                        ins.then_inc(*ye.up())
        sg.settle()


RWKV_LOADS = 8 + 4 + 1


def load_rwkv_params(sp, g, I, l, R, done):
    with g.nc.allow_non_contiguous_dma(reason="vectors into columns"):
        for d in range(2):
            sp.dma_start(R["w0"][:, d], col(I["rwkv_w0"][l, d], 2)).then_inc(*done.up(16))
            sp.dma_start(R["a0"][:, d], col(I["rwkv_a0"][l, d], 2)).then_inc(*done.up(16))
            sp.dma_start(R["wa2"][0:64, d], I["rwkv_w2"][l, d]).then_inc(*done.up(16))
            sp.dma_start(R["wa2"][64:128, d], I["rwkv_a2"][l, d]).then_inc(*done.up(16))
        for name, n in (("rwkv_k_k", "kk"), ("rwkv_k_a", "ka"), ("rwkv_r_k", "rk"), ("g_ln_x", "gln")):
            sp.dma_start(R[n][:], col(I[name][l], 2)).then_inc(*done.up(16))
    sp.dma_start(R["g2"][:], I["rwkv_g2"][l]).then_inc(*done.up(16))
    sp.wait_ge(*done.at(16 * RWKV_LOADS))


def stage_retention(nc, g, I, l, R_rwkv, need_ctx):
    sg, ps, yT = g.sg, g.ps, g.yT
    t_first = 0 if need_ctx else NCT
    with ExitStack() as cx:
        sb = Bufs(nc, cx, f"r{l}")
        z = sb("z", [P, 2, W_RET])
        rope = sb("rope", [P, 2, 2, HD])
        ra = sb("ra", [P, 8, HD])
        rb = sb("rb", [P, 8, HD])
        qk = sb("qk", [P, 2, 8, HD])
        QT = sb("QT", [P, 4, T])
        QX = sb("QX", [P, 2, 2, T])
        kz = sb("kz", [P, 2, GW])
        V = sb("V", [P, NT, GW])
        G = sb("G", [P, NT, GW])
        R = sb("R", [P, NT, 4, P])
        dm = sb("dm", [P, H, P])
        xi = sb("xi", [P, 2, 2, P])
        ze = sb("ze", [P, 2, GW])
        gd = sb("gd", [P, 2])
        pt = sb("pt", [P, 2, H, P])
        o = sb("o", [P, 2, GW])
        sq = sb("sq", [P, GW])
        s4 = sb("s4", [P, 2, H])
        on = sb("on", [P, 2, GW])
        gr = sb("gr", [P, GW])
        z_in, small, chain = [sg(f"w_slot{i}") for i in range(2)], sg("small_in"), sg("dve_chain")
        qkd, tr, ev_a, ev_d, zd, gd_s = sg("normed"), sg("transposed"), sg("evac_a"), sg("evac_d"), sg("rt_zd"), sg("rt_g")
        kzd, rm, rev = sg("rt_kz"), sg("rt_rm"), sg("rt_rev")
        with nc.Block() as block:
            @block.sync
            def _(sp):
                for name, dst in (("dmat", dm), ("xi", xi), ("zeta", ze), ("gdec", gd)):
                    shape = list(dst.shape)
                    sp.dma_start(dst[:], g.C[name].rearrange("p (a b c) -> p a b c", a=2, b=2) if name == "xi" else
                                 g.C[name] if name == "gdec" else
                                 g.C[name].rearrange("p (a b) -> p a b", a=shape[1])).then_inc(*small.up(16))
                sp.dma_start(gr[:], row(I["g_ret_norm"][l])).then_inc(*small.up(16))
                for t in range(NT):
                    if t >= 2:
                        sp.wait_ge(*zd.at(t - 1))
                        sp.wait_ge(*gd_s.at(t - 1))
                    sp.dma_start(z[:, t % 2], g.zt[t * P:(t + 1) * P, W_MLA:W_MLA + W_RET]).then_inc(*z_in[t % 2].up(16))
                    if t >= NCT:
                        sp.dma_start(rope[:, t % 2], g.C["rope_r"].rearrange("(t p) (c f) -> p t c f", p=P, c=2)[:, t - NCT]) \
                            .then_inc(*z_in[t % 2].up(16))

            def z_at(t):
                n = 0
                for u in range(t % 2, t + 1, 2):
                    n += 16 if u < NCT else 32
                return n

            @block.vector
            def _(dve):
                link = linker(dve, chain)
                dve.wait_ge(*small.at(80))
                for t in range(NT):
                    zz, q = z[:, t % 2], qk[:, t % 2]
                    dve.wait_ge(*z_in[t % 2].at(z_at(t)))
                    z8 = zz[:, 0:512].rearrange("p (h d) -> p h d", h=8)
                    if t >= 2:
                        dve.wait_ge(*tr.at(t - 1))
                    if t < NCT:
                        link(nc.vector.tensor_copy(q, z8))
                    else:
                        r = rope[:, t % 2]
                        link(nc.vector.tensor_tensor(ra[:], z8, r[:, 0].unsqueeze(1).broadcast_to([P, 8, HD]), ALU.mult))
                        for s in range(2):
                            a, b = 32 * s, 32 * (1 - s)
                            link(nc.vector.tensor_tensor(rb[:, :, a:a + 32], z8[:, :, b:b + 32],
                                                         r[:, 1, a:a + 32].unsqueeze(1).broadcast_to([P, 8, 32]), ALU.mult))
                        link(nc.vector.tensor_tensor(q, ra[:], rb[:], ALU.add))
                    if t >= 1:
                        dve.wait_ge(*rm.at(t))
                    for d in range(2):
                        link(nc.vector.tensor_tensor(kz[:, d], q[:, 4:8].rearrange("p h d -> p (h d)"), ze[:, d], ALU.mult))
                    nc.vector.tensor_copy(V[:, t], zz[:, 512:768]).then_inc(*zd.up())
                    dve.wait_ge(*zd.at(t + 1))
                    nc.vector.tensor_copy(s4[0:1, 0, 0:1], gr[0:1, 0:1]).then_inc(*qkd.up())
                    dve.wait_ge(*ev_a.at(t + 1))
                    for d in range(2):
                        link(nc.vector.tensor_tensor(QX[:, :, d, t * P:(t + 1) * P],
                                                     ps[:, t % 2, 0:2 * P].rearrange("p (a n) -> p a n", a=2), xi[:, :, d], ALU.mult))
                    nc.vector.tensor_copy(s4[0:1, 0, 0:1], gr[0:1, 0:1]).then_inc(*ev_d.up())
                    dve.wait_ge(*rm.at(t + 1))
                    nc.vector.tensor_tensor(R[:, t], ps[:, 2 + t % 2].rearrange("p (a n) -> p a n", a=4),
                                            g.blk.unsqueeze(1).broadcast_to([P, 4, P]), ALU.mult).then_inc(*rev.up())
                dve.wait_ge(*rev.at(NT))
                link(nc.vector.memset(pt[:, 0], 0.0))
                orders = (list(range(NT)), [1, 0] + list(range(NT - 1, NCT - 1, -1)))
                for n in range(NT):
                    for d in range(2):
                        for p in range(2):
                            ins = nc.vector.scalar_tensor_tensor(pt[:, (n + 1) % 2, 2 * d + p], pt[:, n % 2, 2 * d + p], gd[:, p:p + 1],
                                                                 R[:, orders[d][n], 2 * d + p], ALU.mult, ALU.add)
                    link(ins)
                    for d in range(2):
                        ins = nc.vector.tensor_copy(R[:, orders[d][n], 2 * d:2 * d + 2], pt[:, n % 2, 2 * d:2 * d + 2])
                    link(ins)

            @block.scalar
            def _(act):
                for t in range(NT):
                    act.wait_ge(*z_in[t % 2].at(z_at(t)))
                    nc.scalar.activation(G[:, t], z[:, t % 2, 768:1024], ACT.Silu).then_inc(*gd_s.up())
                    act.wait_ge(*tr.at(t + 1))
                    nc.scalar.copy(QT[:, :, t * P:(t + 1) * P], ps[:, t % 2].rearrange("p (a n) -> p a n", a=4)).then_inc(*ev_a.up())

            @block.tensor
            def _(pe):
                for t in range(NT):
                    pe.wait_ge(*qkd.at(t + 1))
                    if t >= 2:
                        pe.wait_ge(*ev_a.at(t - 1))
                        pe.wait_ge(*ev_d.at(t - 1))
                        pe.wait_ge(*rev.at(t - 1))
                    for a in range(4):
                        ins = nc.tensor.transpose(ps[:, t % 2, a * P:(a + 1) * P],
                                                  qk[:, t % 2, 2 * a:2 * a + 2].rearrange("p h d -> p (h d)"), g.ident)
                    ins.then_inc(*tr.up())
                    for d in range(2):
                        for p in range(2):
                            n = 2 * d + p
                            ins = nc.tensor.matmul(ps[:, 2 + t % 2, n * P:(n + 1) * P], kz[:, d, p * P:(p + 1) * P],
                                                   V[:, t, p * P:(p + 1) * P], start=True, stop=True)
                    ins.then_inc(*rm.up())
        sg.settle()
        sc, ptd, om, oe, od, ytr, ye = sg("at_sc"), sg("at_ex"), sg("at_pv"), sg("at_ote"), sg("normed"), sg("transposed"), sg("evac_a")
        tiles = list(range(t_first, NT))
        SCB = ((0, 3), (4, 5))
        OB, TB = (1, 6), (2, 7)
        N = len(tiles)
        with nc.Block() as block:
            @block.sync
            def _(sp):
                load_rwkv_params(sp, g, I, l, R_rwkv, small)

            @block.tensor
            def _(pe):
                def scores(n):
                    ts = slice(tiles[n] * P, (tiles[n] + 1) * P)
                    if n >= 2:
                        pe.wait_ge(*ptd.at(n - 1))
                    for h in range(H):
                        hp = slice(HD * (h % 2), HD * (h % 2) + HD)
                        b = SCB[n % 2][h % 2]
                        ins = nc.tensor.matmul(ps[:, b, (h // 2) * P:(h // 2 + 1) * P], QT[hp, 2 + h // 2, ts], QT[hp, h // 2, ts],
                                               start=True, stop=True)
                    ins.then_inc(*sc.up())

                def outputs(n):
                    t, b = tiles[n], OB[n % 2]
                    ts = slice(t * P, (t + 1) * P)
                    pe.wait_ge(*ptd.at(n + 1))
                    if n >= 2:
                        pe.wait_ge(*oe.at(n - 1))
                    for p in range(2):
                        for d in range(2):
                            nc.tensor.matmul(ps[:, b, p * P:(p + 1) * P], QX[:, p, d, ts], R[:, t, 2 * d + p], start=(d == 0), stop=False)
                        for h in (2 * p, 2 * p + 1):
                            ins = nc.tensor.matmul(ps[:, b, h * HD:(h + 1) * HD], pt[:, n % 2, h], V[:, t, h * HD:(h + 1) * HD],
                                                   start=False, stop=(h == 2 * p + 1))
                    ins.then_inc(*om.up())

                def turned(n):
                    pe.wait_ge(*od.at(n + 1))
                    if n >= 2:
                        pe.wait_ge(*ye.at(n - 1))
                    for i in range(2):
                        ins = nc.tensor.transpose(ps[:, TB[n % 2], i * P:(i + 1) * P], on[:, n % 2, i * P:(i + 1) * P], g.ident)
                    ins.then_inc(*ytr.up())

                scores(0)
                scores(1)
                for n in range(N):
                    outputs(n)
                    if n + 2 < N:
                        scores(n + 2)
                    if n >= 1:
                        turned(n - 1)
                turned(N - 1)

            @block.vector
            def _(dve):
                link = linker(dve, chain)

                def decayed(n):
                    dve.wait_ge(*sc.at(n + 1))
                    if n >= 2:
                        dve.wait_ge(*om.at(n - 1))
                    for a in range(2):
                        ins = nc.vector.tensor_tensor(pt[:, n % 2, a::2], ps[:, SCB[n % 2][a], 0:2 * P].rearrange("p (h n) -> p h n", h=2),
                                                      dm[:, a::2], ALU.mult)
                    ins.then_inc(*ptd.up())

                decayed(0)
                decayed(1)
                for n, t in enumerate(tiles):
                    on_, o_, s_ = on[:, n % 2], o[:, n % 2], s4[:, n % 2]
                    o4 = o_.rearrange("p (h d) -> p h d", h=H)
                    dve.wait_ge(*oe.at(n + 1))
                    link(nc.vector.tensor_tensor(sq[:], o_, o_, ALU.mult))
                    link(nc.vector.tensor_reduce(s_, sq[:].rearrange("p (h d) -> p h d", h=H), AX_X, ALU.add))
                    nc.vector.tensor_scalar(s_, s_, 1.0 / HD, EPS, ALU.mult, ALU.add).then_inc(*g.vr.up())
                    if n + 2 < N:
                        decayed(n + 2)
                    dve.wait_ge(*g.rq.at(n + 1))
                    link(nc.vector.tensor_tensor(o4, o4, s_.unsqueeze(2).broadcast_to([P, H, HD]), ALU.mult))
                    link(nc.vector.tensor_tensor(o_, o_, gr[:], ALU.mult))
                    if n >= 2:
                        dve.wait_ge(*ytr.at(n - 1))
                    nc.vector.tensor_tensor(on_, o_, G[:, t], ALU.mult).then_inc(*od.up())
                nc.vector.memset(R_rwkv["tiny"][:], 1e-12)
                dve.wait_ge(*small.at(16 * RWKV_LOADS))
                nc.vector.tensor_scalar(R_rwkv["oka"][:], R_rwkv["ka"][:], -1.0, 1.0, ALU.mult, ALU.add)

            @block.gpsimd
            def _(pool):
                for n in range(N):
                    pool.wait_ge(*g.vr.at(n + 1))
                    nc.gpsimd.tensor_tensor(s4[:, n % 2], s4[:, n % 2], g.mhalf[:, 0:H], ALU.pow).then_inc(*g.rq.up())

            @block.scalar
            def _(act):
                def put_out(n):
                    t = tiles[n]
                    act.wait_ge(*ytr.at(n + 1))
                    nc.scalar.copy(yT[:, 6:8, t * P:(t + 1) * P], ps[:, TB[n % 2], 0:2 * P].rearrange("p (a n) -> p a n", a=2)).then_inc(*ye.up())

                for n in range(N):
                    act.wait_ge(*om.at(n + 1))
                    if n >= 2:
                        act.wait_ge(*od.at(n - 1))
                    nc.scalar.copy(o[:, n % 2], ps[:, OB[n % 2], 0:GW]).then_inc(*oe.up())
                    if n >= 1:
                        put_out(n - 1)
                put_out(N - 1)
        sg.settle()


def views(need_ctx):
    return ([(0, CTX, 0)] if need_ctx else []) + [(CTX, SEQ, 1)]


def bank(ps, b, w):
    return ps[:, b:b + (w + 511) // 512, :].rearrange("p b n -> p (b n)")[:, 0:w]


def stage_rwkv_prep(nc, g, I, l, R, p):
    sg, ps, M = g.sg, g.ps, R["M"]
    A, SG, G, GX, E, KK, KS = (R[n] for n in ("A", "SG", "G", "GX", "E", "KK", "KS"))
    KR, BK, ET, tiny = R["KR"], R["BK"], R["ET"], R["tiny"]
    r, k = M[:, p], M[:, 2 + p]
    sqd, wm, am, ssm, acted, gxd, gd, exd, chain = (sg(n) for n in ("sq_done", "rw_wm", "rw_am", "rw_ssm", "evac_a", "rw_gx",
                                                                    "rw_g", "rw_ex", "dve_chain"))
    ed, kkd, kad, masks_in = sg("rw_e"), sg("rw_kk"), sg("rw_ka"), sg("rw_masks_in")
    allv, lnd, small = views(True), sg("ln_done"), sg("small_in")
    with nc.Block() as block:
        @block.sync
        def _(sp):
            sp.dma_start(R["reset"][:], g.C["reset"]).then_inc(*small.up(16))
            if p == 0:
                sp.dma_start(R["masks"][:], g.C["masks"].rearrange("p (d a n) -> p d a n", d=2, a=4)).then_inc(*masks_in.up(16))
                sp.dma_start(R["nlev"][:], g.C["nlev"].rearrange("p (d a n) -> p d a n", d=2, a=LEVELS)).then_inc(*masks_in.up(16))
                sp.wait_ge(*masks_in.at(32))
            sp.wait_ge(*small.at(16))

        @block.tensor
        def _(pe):
            def products(b, lhsT, rhs, done):
                for s, (t0, tw) in enumerate(SPANS):
                    ins = nc.tensor.matmul(ps[:, b + s, 0:tw], lhsT, rhs[:, t0:t0 + tw], start=True, stop=True)
                ins.then_inc(*done.up())
            pp = slice(p * P, (p + 1) * P)
            products(0, R["wa2"][0:64, 0, pp], M[0:64, 6], wm)
            products(3, R["wa2"][64:128, 0, pp], M[64:128, 6], am)
            pe.wait_ge(*acted.at(1))
            products(0, R["wa2"][0:64, 1, pp], M[0:64, 6], wm)
            pe.wait_ge(*acted.at(2))
            pe.wait_ge(*sqd.at(1))
            products(3, g.blk, KK, ssm)
            pe.wait_ge(*acted.at(3))
            products(0, R["wa2"][64:128, 1, pp], M[64:128, 6], am)

        @block.scalar
        def _(act):
            for d in range(2):
                act.wait_ge(*wm.at(d + 1))
                for t0, tw, b in allv:
                    ins = nc.scalar.activation(SG[d][:, t0:t0 + tw], bank(ps, b, tw), ACT.Sigmoid, bias=R["w0"][:, d, p:p + 1])
                ins.then_inc(*acted.up())
                if d == 0:
                    nc.scalar.activation(KK[:], k, ACT.Square, scale=R["kk"][:, p:p + 1]).then_inc(*sqd.up())
                act.wait_ge(*am.at(d + 1))
                for t0, tw, b in allv:
                    ins = nc.scalar.activation(A[d][:, t0:t0 + tw], bank(ps, 3 * (1 - d) + b, tw), ACT.Sigmoid, bias=R["a0"][:, d, p:p + 1])
                ins.then_inc(*acted.up())
            act.wait_ge(*ssm.at(1))
            for t0, tw, b in allv:
                ins = nc.scalar.activation(KS[:, t0:t0 + tw], bank(ps, 3 + b, tw), ACT.Ln, bias=tiny[:, 0:1])
            ins.then_inc(*lnd.up())
            act.wait_ge(*lnd.at(1))
            nc.scalar.activation(KS[:], KS[:], ACT.Exp, scale=-0.5).then_inc(*g.rq.up())
            for d in range(2):
                act.wait_ge(*gxd.at(d + 1))
                nc.scalar.activation(KR[d][:, 0], GX[d][:], ACT.Exp, scale=LWC).then_inc(*exd.up())
                act.wait_ge(*gd.at(d + 1))
                nc.scalar.activation(KR[d][:, 1], G[d][:], ACT.Exp, scale=LWC).then_inc(*exd.up())
                nc.scalar.activation(BK[d][:, 0], G[d][:], ACT.Exp, scale=-LWC).then_inc(*exd.up())
                nc.scalar.activation(ET[d][:, 1], ET[d][:, 0], ACT.Exp, scale=LWC)

        @block.vector
        def _(dve):
            link = linker(dve, chain)
            dve.wait_ge(*small.at(16))
            for d in range(2):
                dve.wait_ge(*acted.at(2 * d + 1))
                scan = nc.vector.tensor_tensor_scan(G[d][:], R["reset"][:], SG[d][:], 0.0, ALU.mult, ALU.add)
                if d == 0:
                    scan.then_inc(*gd.up())
                    dve.wait_ge(*gd.at(1))
                else:
                    link(scan)
                link(nc.vector.tensor_copy(ET[d][:, 0], G[d][:, CH - 1::CH]))
                if d == 0:
                    nc.vector.tensor_tensor(GX[d][:], G[d][:], SG[d][:], ALU.subtract).then_inc(*gxd.up())
                else:
                    g3 = G[d][:].rearrange("p (c n) -> p c n", n=CH)
                    nc.vector.tensor_tensor(GX[d][:].rearrange("p (c n) -> p c n", n=CH), ET[d][:, 0].unsqueeze(2).broadcast_to([P, T // CH, CH]),
                                            g3, ALU.subtract).then_inc(*gxd.up())
                    dve.wait_ge(*gxd.at(2))
                    nc.vector.tensor_tensor(G[d][:], GX[d][:], SG[d][:], ALU.add).then_inc(*gd.up())
                dve.wait_ge(*acted.at(2 * d + 2))
                link(nc.vector.tensor_scalar(E[d][:], A[d][:], R["ka"][:, p:p + 1], R["oka"][:, p:p + 1], ALU.mult, ALU.add))
                nc.vector.tensor_tensor(E[d][:], E[d][:], k, ALU.mult).then_inc(*ed.up())
            dve.wait_ge(*g.rq.at(1))
            nc.vector.scalar_tensor_tensor(KK[:], k, R["kk"][:, p:p + 1], KS[:], ALU.mult, ALU.mult).then_inc(*kkd.up())
            dve.wait_ge(*kkd.at(1))
            dve.wait_ge(*ed.at(2))
            for d in range(2):
                dve.wait_ge(*exd.at(3 * d + 3))
                nc.vector.tensor_tensor(KR[d][:, 0], KR[d][:, 0], KK[:], ALU.mult)
                nc.vector.tensor_tensor(KR[d][:, 1], KR[d][:, 1], r, ALU.mult)
                link(nc.vector.tensor_tensor(BK[d][:, 1], E[d][:], BK[d][:, 0], ALU.mult))
                dve.wait_ge(*kad.at(d + 1))
                nc.vector.tensor_tensor(BK[d][:, 0], BK[d][:, 0], A[d][:], ALU.mult)

        @block.gpsimd
        def _(pool):
            for d in range(2):
                pool.wait_ge(*kkd.at(1))
                pool.wait_ge(*ed.at(d + 1))
                nc.gpsimd.tensor_tensor(A[d][:], A[d][:], KK[:], ALU.mult).then_inc(*kad.up())
            pool.wait_ge(*ed.at(2))
            nc.gpsimd.tensor_tensor(KS[:], E[0][:], E[1][:], ALU.add)
    sg.settle()


def stage_rwkv_scan(nc, g, I, l, R, p, need_ctx):
    sg, ps, M, yT = g.sg, g.ps, R["M"], g.yT
    KR, BK, ET = R["KR"], R["BK"], R["ET"]
    order = [list(range(NT)), [1, 0] + list(range(NT - 1, NCT - 1, -1))]
    chunks = [[0, 1], [1, 0]]
    DD = (0, 1)
    with ExitStack() as cx:
        sb = Bufs(nc, cx, f"s{l}{p}")
        UM = [sb(f"UM{d}", [P, 2, 2, 4, P]) for d in DD]
        TM = [sb(f"TM{d}", [P, 3, 4, P]) for d in DD]
        NL = [sb(f"NL{d}", [P, LEVELS, 2, P]) for d in DD]
        TS = [sb(f"TS{d}", [P, 2, 2, P]) for d in DD]
        X = [sb(f"X{d}", [P, 2, P]) for d in DD]
        W1 = [sb(f"W1{d}", [P, P]) for d in DD]
        W2 = [sb(f"W2{d}", [P, P]) for d in DD]
        MV = [sb(f"MV{d}", [P, P]) for d in DD]
        U = [sb(f"U{d}", [P, P]) for d in DD]
        S = [sb(f"S{d}", [P, 3, P]) for d in DD]
        Se = [sb(f"Se{d}", [P, P]) for d in DD]
        bX, bT, bS, bR = ([4 * d + n for d in DD] for n in range(4))

        def sig(name):
            return [sg(f"rw_{name}{d}") for d in DD]
        p1, tr, um, tme, nl, ts = sig("p1"), sig("tr"), sig("um"), sig("tme"), sig("nl"), sig("ts")
        xm, xe, tm, wm, we, mv, mve = sig("xm"), sig("xe"), sig("tm"), sig("wm"), sig("we"), sig("mv"), sig("mve")
        umm, ue, smm, su, ym, ye, chain = sig("umm"), sig("ue"), sig("smm"), sig("su"), sig("ym"), sig("ye"), sg("dve_chain")
        NLV = LEVELS - 1
        AHEAD = LEVELS - 2

        SLOTS, LAG = LEVELS, (0, 3)

        def slots():
            for q in range(SLOTS * (NT + 1) + LAG[1]):
                yield [(d, *divmod(q - LAG[d], SLOTS)) for d in DD if 0 <= q - LAG[d] < SLOTS * (NT + 1)]

        def n_y(d, s):
            return sum(need_ctx or t >= NCT for t in order[d][:s])

        with nc.Block() as block:
            @block.tensor
            def _(pe):
                def carry(d, s, piece):
                    t = order[d][s]
                    b = ps[:, bS[d]]
                    if piece < 4:
                        n = 2 * s + piece // 2
                        c = chunks[d][piece // 2]
                        cs = slice(CH * c, CH * c + CH)
                        if piece % 2 == 0:
                            pe.wait_ge(*su[d].at(n + 1))
                            if piece == 0:
                                pe.wait_ge(*we[d].at(2 * (s + 1)))
                                pe.wait_ge(*ye[d].at(n_y(d, s)) if n_y(d, s) else su[d].at(n + 1))
                            nc.tensor.matmul(b[cs, 0:P], W1[d][:, cs], S[d][:, n % 3], start=True, stop=True).then_inc(*umm[d].up())
                        else:
                            pe.wait_ge(*ue[d].at(n + 1))
                            nc.tensor.matmul(b[:, P:2 * P], TM[d][cs, s % 3, 1], U[d][cs], start=True, stop=False)
                            nc.tensor.matmul(b[:, P:2 * P], TM[d][cs, s % 3, 2], TM[d][cs, s % 3, 3], start=False, stop=True) \
                                .then_inc(*smm[d].up())
                    elif need_ctx or t >= NCT:
                        pe.wait_ge(*su[d].at(2 * s + 3))
                        o = b[:, 2 * P:3 * P]
                        for q, c in enumerate(chunks[d]):
                            cs = slice(CH * c, CH * c + CH)
                            nc.tensor.matmul(o[:, cs], S[d][:, (2 * s + q) % 3], KR[d][:, 1, t * P + CH * c:t * P + CH * c + CH],
                                             start=(q == 0), stop=False, skip_group_check=True)
                        for h in range(2):
                            hp = slice(HD * h, HD * h + HD)
                            nc.tensor.matmul(o[hp], U[d][:, hp], UM[d][:, s % 2, h, 1], start=False, stop=False, skip_group_check=True)
                            ins = nc.tensor.matmul(o[hp], TM[d][:, s % 3, 3, hp], UM[d][:, s % 2, h, 3], start=False, stop=True,
                                                   skip_group_check=True)
                        ins.then_inc(*ym[d].up())

                def transposes(d, s):
                    tt = slice(order[d][s] * P, order[d][s] * P + P)
                    if s:
                        pe.wait_ge(*mve[d].at(s))
                    for a, src in enumerate((KR[d][:, 0, tt], BK[d][:, 0, tt], BK[d][:, 1, tt], M[:, 4 + p, tt])):
                        ins = nc.tensor.transpose(ps[:, bR[d], a * P:(a + 1) * P], src, g.ident)
                    ins.then_inc(*tr[d].up())

                def products(d, s):
                    tt = slice(order[d][s] * P, order[d][s] * P + P)
                    if s:
                        pe.wait_ge(*we[d].at(2 * s))
                    for h in range(2):
                        hp = slice(HD * h, HD * h + HD)
                        o = ps[:, (bX, bT)[h][d]]
                        nc.tensor.matmul(o[:, 0:256], BK[d][hp, 0, tt], KR[d][hp, :, tt], start=True, stop=True)
                        nc.tensor.matmul(o[:, 256:512], BK[d][hp, 1, tt], KR[d][hp, :, tt], start=True, stop=True).then_inc(*p1[d].up())

                def level_x(d, s, v):
                    pe.wait_ge(*um[d].at(2 * s + 2))
                    pe.wait_ge(*nl[d].at(s * NLV + v))
                    pe.wait_ge(*ts[d].at(s * LEVELS + v))
                    for h in range(2):
                        ins = nc.tensor.matmul(ps[:, bX[d], h * P:(h + 1) * P], NL[d][:, v, h], TS[d][:, 0, h], start=True, stop=True)
                    ins.then_inc(*xm[d].up())

                def level_t(d, s, v):
                    pe.wait_ge(*xe[d].at(s * NLV + v))
                    if v < LEVELS - 1:
                        for h in range(2):
                            nc.tensor.matmul(ps[:, bT[d], h * P:(h + 1) * P], TS[d][:, 1, h], X[d][:, h], start=True, stop=True)
                    for h in range(2):
                        ins = nc.tensor.matmul(ps[:, bT[d], (2 + h) * P:(3 + h) * P], X[d][:, h], TS[d][:, 1, h], start=True, stop=True)
                    ins.then_inc(*tm[d].up())

                def m_v(d, s):
                    pe.wait_ge(*um[d].at(2 * s + 2))
                    pe.wait_ge(*tme[d].at(s + 1))
                    for h in range(2):
                        hp = slice(HD * h, HD * h + HD)
                        ins = nc.tensor.matmul(ps[:, bR[d], hp], UM[d][:, s % 2, h, 2], TM[d][:, s % 3, 3, hp], start=True, stop=True)
                    ins.then_inc(*mv[d].up())

                def w1_w2(d, s):
                    pe.wait_ge(*ts[d].at((s + 1) * LEVELS))
                    pe.wait_ge(*mve[d].at(s + 1))
                    for h in range(2):
                        hp = slice(HD * h, HD * h + HD)
                        nc.tensor.matmul(ps[hp, bX[d], 0:P], TM[d][:, s % 3, 0, hp], TS[d][:, 1, h], start=True, stop=True)
                        ins = nc.tensor.matmul(ps[:, bT[d], hp], TS[d][:, 1, h], MV[d][:, hp], start=True, stop=True)
                    ins.then_inc(*wm[d].up())

                for now in slots():
                    for d, s, i in now:
                        if i == 0 and s:
                            w1_w2(d, s - 1)
                        if i >= 2 and s < NT:
                            level_x(d, s, i)
                    for d, s, i in now:
                        if i and s:
                            carry(d, s - 1, i - 1)
                    for d, s, i in now:
                        if i == AHEAD and s + 1 < NT:
                            transposes(d, s + 1)
                    for d, s, i in now:
                        if i == 1 and s < NT:
                            m_v(d, s)
                            level_x(d, s, 1)
                    for d, s, i in now:
                        if i == 0 and s == 0:
                            transposes(d, 0)
                        if i == 0 and s < NT:
                            products(d, s)
                        if i and s < NT:
                            level_t(d, s, i)

            @block.vector
            def _(dve):
                link = linker(dve, chain)

                def carry(d, s, piece):
                    t = order[d][s]
                    b = ps[:, bS[d]]
                    n = 2 * s + piece // 2
                    if piece < 4:
                        c = chunks[d][piece // 2]
                        cs = slice(CH * c, CH * c + CH)
                        e = ET[d][:, 1, 2 * t + c:2 * t + c + 1]
                        if piece % 2 == 0:
                            dve.wait_ge(*su[d].at(n + 1))
                            link(nc.vector.tensor_scalar(Se[d][:], S[d][:, n % 3], e, None, ALU.mult))
                            dve.wait_ge(*umm[d].at(n + 1))
                            dve.wait_ge(*we[d].at(2 * (s + 1)))
                            nc.vector.scalar_tensor_tensor(U[d][cs], b[cs, 0:P], -1.0, W2[d][cs], ALU.mult, ALU.subtract).then_inc(*ue[d].up())
                        else:
                            dve.wait_ge(*smm[d].at(n + 1))
                            for h in range(2):
                                hp = slice(HD * h, HD * h + HD)
                                ins = nc.vector.scalar_tensor_tensor(S[d][hp, (n + 1) % 3, hp], b[hp, P + HD * h:P + HD * h + HD], e[hp],
                                                                     Se[d][hp, hp], ALU.mult, ALU.add)
                            ins.then_inc(*su[d].up())
                    elif need_ctx or t >= NCT:
                        dve.wait_ge(*ym[d].at(n_y(d, s) + 1))
                        y = yT[:, 4 + p, t * P:(t + 1) * P]
                        o = b[:, 2 * P:3 * P]
                        if s < order[1 - d].index(t):
                            nc.vector.tensor_copy(y, o).then_inc(*ye[d].up())
                        else:
                            dve.wait_ge(ye[1 - d].sem, ye[1 - d].made)
                            nc.vector.tensor_tensor(y, y, o, ALU.add).then_inc(*ye[d].up())

                for d in DD:
                    nc.vector.memset(S[d][:], 0.0).then_inc(*su[d].up())
                def masked(d, s):
                    for h in range(2):
                        dve.wait_ge(*p1[d].at(2 * s + h + 1))
                        nc.vector.tensor_tensor(UM[d][:, s % 2, h], ps[:, (bX, bT)[h][d]].rearrange("p (a n) -> p a n", a=4),
                                                R["masks"][:, d], ALU.mult).then_inc(*um[d].up())

                def level_0(d, s):
                    dve.wait_ge(*um[d].at(2 * s + 2))
                    if s:
                        dve.wait_ge(*wm[d].at(s))
                    link(nc.vector.tensor_tensor(TS[d][:, 1], UM[d][:, s % 2, :, 0], R["nlev"][:, d, 0].unsqueeze(1).broadcast_to([P, 2, P]),
                                                 ALU.mult))
                    link(nc.vector.tensor_tensor(TS[d][:, 1], TS[d][:, 1], g.ident.unsqueeze(1).broadcast_to([P, 2, P]), ALU.add))
                    nc.vector.transpose(TS[d][:, 0].rearrange("p u n -> p (u n)"), TS[d][:, 1].rearrange("p u n -> p (u n)")) \
                        .then_inc(*ts[d].up())

                for now in slots():
                    for d, s, i in now:
                        if i == 1 and s < NT:
                            level_0(d, s)
                    for d, s, i in now:
                        if i and s:
                            carry(d, s - 1, i - 1)
                    for d, s, i in now:
                        if i == 0 and s < NT:
                            masked(d, s)
                        if i and s < NT:
                            v = i
                            dve.wait_ge(*tm[d].at(s * NLV + v))
                            dve.wait_ge(*ts[d].at(s * LEVELS + v))
                            a = 0 if v < LEVELS - 1 else 1
                            T2 = TS[d][:, a:2].rearrange("p a u n -> p (a u n)")
                            nc.vector.tensor_tensor(T2, T2, ps[:, bT[d], 2 * P * a:4 * P], ALU.add).then_inc(*ts[d].up())

            @block.gpsimd
            def _(pool):
                for now in slots():
                    for d, s, i in now:
                        if i == 0 and s < NT:
                            pool.wait_ge(*um[d].at(2 * (s + 1)))
                            if s:
                                pool.wait_ge(*tm[d].at(s * NLV))
                            for v in range(1, LEVELS):
                                nc.gpsimd.tensor_tensor(NL[d][:, v], UM[d][:, s % 2, :, 0],
                                                        R["nlev"][:, d, v].unsqueeze(1).broadcast_to([P, 2, P]), ALU.mult).then_inc(*nl[d].up())

            @block.scalar
            def _(act):
                def by_token(d, s):
                    act.wait_ge(*tr[d].at(s + 1))
                    nc.scalar.copy(TM[d][:, s % 3], ps[:, bR[d]].rearrange("p (a n) -> p a n", a=4)).then_inc(*tme[d].up())

                def x_out(d, s, v):
                    act.wait_ge(*xm[d].at(s * NLV + v))
                    nc.scalar.copy(X[d][:].rearrange("p u n -> p (u n)"), ps[:, bX[d], 0:2 * P]).then_inc(*xe[d].up())

                for now in slots():
                    for d, s, i in now:
                        if i == 0 and s:
                            act.wait_ge(*wm[d].at(s))
                            nc.scalar.copy(W1[d][:], ps[:, bX[d], 0:P]).then_inc(*we[d].up())
                            nc.scalar.copy(W2[d][:], ps[:, bT[d], 0:P]).then_inc(*we[d].up())
                        if i >= 2 and s < NT:
                            x_out(d, s, i)
                    for d, s, i in now:
                        if i == AHEAD and s + 1 < NT:
                            by_token(d, s + 1)
                    for d, s, i in now:
                        if i == 1 and s < NT:
                            act.wait_ge(*mv[d].at(s + 1))
                            nc.scalar.copy(MV[d][:], ps[:, bR[d], 0:P]).then_inc(*mve[d].up())
                            x_out(d, s, 1)
                    for d, s, i in now:
                        if i == 0 and s == 0:
                            by_token(d, 0)
        sg.settle()


def stage_rwkv_out(nc, g, I, l, R, p, need_ctx):
    sg, ps, M = g.sg, g.ps, R["M"]
    y, r, v = g.yT[:, 4 + p], M[:, p], M[:, 4 + p]
    YC, SQ, RS, RK = R["KR"][0][:, 0], R["KR"][0][:, 1], R["BK"][0][:, 0], R["BK"][0][:, 1]
    vw = views(need_ctx)
    spans = [(s, t0, tw) for s, (t0, tw) in enumerate(SPANS) if need_ctx or s > 0]
    lnd = sg("ln_done")
    mm, ycd, sqd, rkd, rsd, bon, chain = (sg(n) for n in ("mm_done", "normed", "sq_done", "coef", "evac_d", "rw_g", "dve_chain"))
    with nc.Block() as block:
        @block.tensor
        def _(pe):
            def grp(b, lhsT, rhs):
                for s, t0, tw in spans:
                    ins = nc.tensor.matmul(ps[:, b + s, 0:tw], lhsT, rhs[:, t0:t0 + tw], start=True, stop=True)
                ins.then_inc(*mm.up())
            grp(0, g.blk, y)
            pe.wait_ge(*sqd.at(1))
            grp(3, g.blk, SQ)
            pe.wait_ge(*rkd.at(1))
            grp(0, g.blk, RK)
            pe.wait_ge(*rsd.at(1))
            grp(3, R["g2"][:, p * P:(p + 1) * P], M[:, 7])

        @block.scalar
        def _(act):
            act.wait_ge(*ycd.at(1))
            for t0, tw, b in vw:
                ins = nc.scalar.activation(SQ[:, t0:t0 + tw], YC[:, t0:t0 + tw], ACT.Square)
            ins.then_inc(*sqd.up())
            act.wait_ge(*rsd.at(1))
            al = slice(vw[0][0], T)
            nc.scalar.activation(RS[:, al], RS[:, al], ACT.Ln).then_inc(*lnd.up())
            act.wait_ge(*lnd.at(1))
            nc.scalar.activation(RS[:, al], RS[:, al], ACT.Exp, scale=-0.5).then_inc(*g.rq.up())

        @block.vector
        def _(dve):
            link = linker(dve, chain)
            dve.wait_ge(*mm.at(1))
            for t0, tw, b in vw:
                t = slice(t0, t0 + tw)
                ins = nc.vector.scalar_tensor_tensor(YC[:, t], bank(ps, b, tw), -1.0 / HD, y[:, t], ALU.mult, ALU.add)
            ins.then_inc(*ycd.up())
            t0 = vw[0][0]
            al = slice(t0, T)
            nc.vector.scalar_tensor_tensor(RK[:, al], r[:, al], R["rk"][:, p:p + 1], R["KS"][:, al], ALU.mult, ALU.mult).then_inc(*rkd.up())
            dve.wait_ge(*mm.at(2))
            for t0, tw, b in vw:
                ins = nc.vector.tensor_scalar(RS[:, t0:t0 + tw], bank(ps, 3 + b, tw), 1.0 / HD, GN_EPS, ALU.mult, ALU.add)
            ins.then_inc(*rsd.up())
            dve.wait_ge(*rsd.at(1))
            dve.wait_ge(*g.rq.at(1))
            link(nc.vector.scalar_tensor_tensor(YC[:, al], YC[:, al], R["gln"][:, p:p + 1], RS[:, al], ALU.mult, ALU.mult))
            dve.wait_ge(*mm.at(3))
            for t0, tw, b in vw:
                t = slice(t0, t0 + tw)
                link(nc.vector.tensor_tensor(RS[:, t], bank(ps, b, tw), v[:, t], ALU.mult))
            link(nc.vector.tensor_tensor(YC[:, al], YC[:, al], RS[:, al], ALU.add))
            dve.wait_ge(*mm.at(4))
            for t0, tw, b in vw:
                t = slice(t0, t0 + tw)
                nc.vector.tensor_tensor(y[:, t], YC[:, t], bank(ps, 3 + b, tw), ALU.mult)
    sg.settle()


def stage_out(nc, g, I, l, need_ctx):
    sg, ps, yT = g.sg, g.ps, g.yT
    tiles = list(range(0 if need_ctx else NCT, NT))
    with ExitStack() as cx:
        sb = Bufs(nc, cx, f"o{l}")
        w = sb("w", [P, KT, D])
        rows = sb("rows", [P, 2, 3, D])
        gn = sb("gn", [P, D])
        wr = sb("wr", [P, KT, NE])
        br = sb("br", [P, NE])
        xi_ = sb("xi", [P, 2, D])
        xo = sb("xo", [P, 2, D])
        h2 = sb("h2", [P, 2, D])
        hT2 = sb("hT2", [P, KT, P])
        junk = sb("junk", [P, D])
        st = sb("st", [P, 4])
        lg = sb("lg", [P, NE])
        ex = sb("ex", [P, NE])
        WQ = 4
        w_in, small, x_in, chain = [sg(f"w_slot{2 + q}") for q in range(WQ)], sg("small_in"), [sg(f"w_slot{i}") for i in range(2)], sg("dve_chain")
        om, xd, sqd, hd, tr, te = sg("mm_done"), sg("coef"), sg("sq_done"), sg("normed"), sg("transposed"), sg("evac_a")
        lm, lgd, exd, afd, at, ae = sg("ro_lm"), sg("ro_lg"), sg("ro_ex"), sg("ro_aff"), sg("ro_at"), sg("ro_ae")
        xs, hs = [sg(f"out_slot{i}") for i in range(2)], [sg(f"out_slot{2 + i}") for i in range(2)]
        with nc.Block() as block:
            @block.sync
            def _(sp):
                for q in range(WQ):
                    kq = slice(q * KT // WQ, (q + 1) * KT // WQ)
                    sp.dma_start(w[:, kq], I["w_out"][l].rearrange("(k p) f -> p k f", p=P)[:, kq]).then_inc(*w_in[q].up(16))
                for s in range(2):
                    for n, c in enumerate((2, 3, 4)):
                        sp.dma_start(rows[:, s, n], row(g.mod[l, s, c * D:(c + 1) * D])).then_inc(*small.up(16))
                sp.dma_start(gn[:], row(I["g_norm2"][l])).then_inc(*small.up(16))
                sp.dma_start(wr[:], I["w_router"][l].rearrange("(k p) e -> p k e", p=P)).then_inc(*small.up(16))
                sp.dma_start(br[:], row(I["b_router"][l])).then_inc(*small.up(16))
                for n, t in enumerate(tiles):
                    if n >= 2:
                        sp.wait_ge(*xd.at(n - 1))
                    sp.dma_start(xi_[:, n % 2], g.x_rows(I, l, t)).then_inc(*x_in[n % 2].up(16))

            @block.gpsimd
            def _(pool):
                for n, t in enumerate(tiles):
                    ts = slice(t * P, (t + 1) * P)
                    pool.wait_ge(*xd.at(n + 1))
                    pool.dma_start(g.x[ts], xo[:, n % 2]).then_inc(*xs[n % 2].up(16))
                    pool.wait_ge(*g.vr.at(n + 1))
                    nc.gpsimd.tensor_tensor(st[:, 1:2], st[:, 1:2], g.mhalf[:, 0:1], ALU.pow).then_inc(*g.rq.up())
                    pool.wait_ge(*hd.at(n + 1))
                    pool.dma_start(g.h2[ts], h2[:, n % 2]).then_inc(*hs[n % 2].up(16))
                for s in xs + hs:
                    pool.wait_ge(s.sem, s.made)

            @block.tensor
            def _(pe):

                def proj(n):
                    t = tiles[n]
                    if n >= 2:
                        pe.wait_ge(*xd.at(n - 1))
                    for k in range(KT):
                        if n == 0 and k % (KT // WQ) == 0:
                            pe.wait_ge(*w_in[k // (KT // WQ)].at(16))
                        for half in range(2):
                            ins = nc.tensor.matmul(ps[:, 2 * (n % 2) + half, :], yT[:, k, t * P:(t + 1) * P], w[:, k, half * 512:(half + 1) * 512],
                                                   start=(k == 0), stop=(k == KT - 1))
                    ins.then_inc(*om.up())
                proj(0)
                pe.wait_ge(*small.at(144))
                for n, t in enumerate(tiles):
                    if n + 1 < len(tiles):
                        proj(n + 1)
                    pe.wait_ge(*hd.at(n + 1))
                    if n >= 1:
                        pe.wait_ge(*te.at(n))
                    for k in range(KT):
                        ins = nc.tensor.transpose(ps[:, 4 + k // 4, (k % 4) * P:(k % 4 + 1) * P], h2[:, n % 2, k * P:(k + 1) * P], g.ident)
                    ins.then_inc(*tr.up())
                    pe.wait_ge(*te.at(n + 1))
                    if n >= 1:
                        pe.wait_ge(*lgd.at(n))
                    for k in range(KT):
                        ins = nc.tensor.matmul(ps[:, 6, 0:NE], hT2[:, k], wr[:, k], start=(k == 0), stop=(k == KT - 1))
                    ins.then_inc(*lm.up())
                    pe.wait_ge(*afd.at(n + 1))
                    if n >= 1:
                        pe.wait_ge(*ae.at(n))
                    nc.tensor.transpose(ps[0:NE, 7, 0:P], ex[:], g.ident).then_inc(*at.up())

            @block.vector
            def _(dve):
                link = linker(dve, chain)
                dve.wait_ge(*small.at(144))
                for s in range(2):
                    link(nc.vector.scalar_tensor_tensor(rows[:, s, 2], rows[:, s, 2], 1.0, gn[:], ALU.add, ALU.mult))
                for n, t in enumerate(tiles):
                    s = 1 if t < NCT else 0
                    dve.wait_ge(*om.at(n + 1))
                    dve.wait_ge(*x_in[n % 2].at(16 * (n // 2 + 1)))
                    if n >= 2:
                        dve.wait_ge(*xs[n % 2].at(16 * (n // 2)))
                    link(nc.vector.tensor_tensor(xo[:, n % 2], bank(ps, 2 * (n % 2), D), rows[:, s, 0], ALU.mult))
                    nc.vector.tensor_tensor(xo[:, n % 2], xo[:, n % 2], xi_[:, n % 2], ALU.add).then_inc(*xd.up())
                    dve.wait_ge(*sqd.at(n + 1))
                    nc.vector.tensor_scalar(st[:, 1:2], st[:, 0:1], 1.0 / D, EPS, ALU.mult, ALU.add).then_inc(*g.vr.up())
                    dve.wait_ge(*g.rq.at(n + 1))
                    if n >= 2:
                        dve.wait_ge(*hs[n % 2].at(16 * (n // 2)))
                    link(nc.vector.scalar_tensor_tensor(h2[:, n % 2], xo[:, n % 2], st[:, 1:2], rows[:, s, 2], ALU.mult, ALU.mult))
                    nc.vector.tensor_tensor(h2[:, n % 2], h2[:, n % 2], rows[:, s, 1], ALU.add).then_inc(*hd.up())
                    dve.wait_ge(*lm.at(n + 1))
                    link(nc.vector.tensor_tensor(lg[:], ps[:, 6, 0:NE], br[:], ALU.add))
                    link(nc.vector.reduce_max(st[:, 2:3], lg[:], AX_X))
                    nc.vector.tensor_scalar(lg[:], lg[:], st[:, 2:3], None, ALU.subtract).then_inc(*lgd.up())
                    dve.wait_ge(*exd.at(n + 1))
                    link(nc.vector.reciprocal(st[:, 3:4], st[:, 3:4]))
                    nc.vector.tensor_scalar(ex[:], ex[:], st[:, 3:4], None, ALU.mult).then_inc(*afd.up())
                    dve.wait_ge(*at.at(n + 1))
                    nc.vector.tensor_copy(g.aff[:, t * P:(t + 1) * P], ps[0:NE, 7, 0:P]).then_inc(*ae.up())

            @block.scalar
            def _(act):
                for n, t in enumerate(tiles):
                    act.wait_ge(*xd.at(n + 1))
                    if n >= 1:
                        act.wait_ge(*sqd.at(n))
                    nc.scalar.activation(junk[:], xo[:, n % 2], ACT.Square, accum_out=st[:, 0:1]).then_inc(*sqd.up())
                    act.wait_ge(*tr.at(n + 1))
                    nc.scalar.copy(hT2[:].rearrange("p k n -> p (k n)"), bank(ps, 4, D)).then_inc(*te.up())
                    act.wait_ge(*lgd.at(n + 1))
                    nc.scalar.activation(ex[:], lg[:], ACT.Exp, accum_out=st[:, 3:4]).then_inc(*exd.up())
        sg.settle()


MOE_RW = 8
MOE_PARTS = [(e, m, half) for e in range(NE) for m in range(3) for half in range(2)]


def load_expert_part(sp, g, I, l, j):
    e, m, half = MOE_PARTS[j]
    src = I[("w_gate", "w_up", "w_down")[m]][l, e].rearrange("(k p) f -> p k f", p=P)[:, 4 * half:4 * half + 4]
    sp.dma_start(g.moe_w[:, j % MOE_RW], src).then_inc(*g.sg(f"w_slot{j % MOE_RW}").up(16))


def stage_topk(nc, g, I, l, need_ctx):
    sg, ps = g.sg, g.ps
    sets = [("x", CTX, SEQ, CAPX)] + ([("c", 0, CTX, CAPC)] if need_ctx else [])
    with ExitStack() as cx:
        sb = Bufs(nc, cx, f"k{l}")
        val = sb("val", [NE, 2, P])
        idx = sb("idx", [NE, 2, P], U32)
        idf = sb("idf", [NE, 2, P])
        zero = sb("zero", [P, D])
        zd, zs, found, tr, chain = sg("coef"), sg("zeroed"), sg("normed"), sg("transposed"), sg("dve_chain")
        with nc.Block() as block:
            @block.sync
            def _(sp):
                for j in range(MOE_RW):
                    load_expert_part(sp, g, I, l, j)

            @block.vector
            def _(dve):
                link = linker(dve, chain)
                nc.vector.memset(zero[:], 0.0).then_inc(*zd.up())
                for n, (_, t0, tw, cap) in enumerate(sets):
                    a = g.aff[:, t0:t0 + tw]
                    for r in range(cap // 8):
                        v8 = val[:, n, 8 * r:8 * r + 8]
                        link(nc.vector.max(v8, a))
                        link(nc.vector.max_index(idx[:, n, 8 * r:8 * r + 8], v8, a))
                        link(nc.vector.match_replace(a, v8, a, -1.0))
                    link(nc.vector.tensor_copy(idf[:, n, 0:cap], idx[:, n, 0:cap]))
                    nc.vector.tensor_scalar(idf[:, n, 0:cap], idf[:, n, 0:cap], float(t0), None, ALU.add).then_inc(*found.up())
                for n, (_, t0, tw, cap) in enumerate(sets):
                    dve.wait_ge(*tr.at(n + 1))
                    nc.vector.tensor_copy(g.tok[0:cap, n], ps[0:cap, n, 0:NE])
                    nc.vector.tensor_copy(g.gate[0:cap, n], ps[0:cap, n, NE:2 * NE])

            @block.gpsimd
            def _(pool):
                pool.wait_ge(*zd.at(1))
                for t in range(0 if need_ctx else NCT, NT):
                    pool.dma_start(g.acc[t * P:(t + 1) * P], zero[:]).then_inc(*zs.up(16))
                pool.wait_ge(zs.sem, zs.made)

            @block.tensor
            def _(pe):
                for n, (_, t0, tw, cap) in enumerate(sets):
                    pe.wait_ge(*found.at(n + 1))
                    nc.tensor.transpose(ps[0:cap, n, 0:NE], idf[:, n, 0:cap], g.ident[0:NE, 0:NE])
                    nc.tensor.transpose(ps[0:cap, n, NE:2 * NE], val[:, n, 0:cap], g.ident[0:NE, 0:NE]).then_inc(*tr.up())
        sg.settle()


def stage_moe(nc, g, I, l, need_ctx):
    sg, ps = g.sg, g.ps
    sets = [(0, CAPX)] + ([(1, CAPC)] if need_ctx else [])
    passes = [(e, n, cap) for e in range(NE) for n, cap in sets]
    NP, RW, w = len(passes), MOE_RW, g.moe_w
    with ExitStack() as cx:
        sb = Bufs(nc, cx, f"e{l}")
        xe = sb("xe", [P, 3, D])
        xT = sb("xT", [P, KT, P])
        hid = sb("hid", [P, FF])
        hT2 = sb("hT2", [P, KT, P])
        ye = sb("ye", [P, 2, D])
        pg = sb("pg", [P, FF])
        pu = sb("pu", [P, FF])
        gs = sb("gs", [P, KT, CAPC])
        w_in = [sg(f"w_slot{i}") for i in range(RW)]
        ga = [sg(f"moe_gather{b}") for b in range(3)]
        sc, gm, um, dm = sg("moe_scatter"), sg("moe_gm"), sg("moe_um"), sg("moe_dm")
        xtr, xte, si, hd, htr, hte, yd = (sg(n) for n in ("moe_xtr", "moe_xte", "moe_silu", "moe_hid", "moe_htr", "moe_hte", "moe_ye"))
        gsd, dpm, pdd = sg("moe_gs"), sg("moe_dp"), sg("moe_pd")
        with nc.Block() as block:
            @block.sync
            def _(sp):
                for j in range(RW, len(MOE_PARTS)):
                    eo, mo, _ = MOE_PARTS[j - RW]
                    last = (eo + 1) * len(sets)
                    sp.wait_ge(*(gm, um, dm)[mo].at(last if mo == 2 else 2 * last))
                    load_expert_part(sp, g, I, l, j)

            @block.gpsimd
            def _(pool):
                def gather(i):
                    e, n, cap = passes[i]
                    if i >= 3:
                        pool.wait_ge(*xtr.at(i - 2))
                    pool.indirect_dma_start(xe[0:cap, i % 3], None, g.h2, bass.IndirectOffsetOnAxis(ap=g.tok[0:cap, n, e:e + 1], axis=0)) \
                        .then_inc(*ga[i % 3].up(16))
                gather(0)
                gather(1)
                for i, (e, n, cap) in enumerate(passes):
                    if i + 2 < NP:
                        gather(i + 2)
                    pool.wait_ge(*yd.at(i + 1))
                    if i:
                        pool.wait_ge(*sc.at(16 * i))
                    pool.indirect_dma_start(g.acc, bass.IndirectOffsetOnAxis(ap=g.tok[0:cap, n, e:e + 1], axis=0), ye[0:cap, i % 2], None,
                                            compute_op=ALU.add).then_inc(*sc.up(16))
                pool.wait_ge(*sc.at(16 * NP))

            @block.tensor
            def _(pe):
                def slot(e, m, half):
                    j = 6 * e + 2 * m + half
                    return j % RW, 16 * (j // RW)

                def product(n, cap, half, k, b, xs, rhs):
                    kk = 4 * half + k
                    if n == 1:
                        return nc.tensor.matmul(ps[32 * k:32 * k + 32, b, :], xs[:, kk, 0:cap], rhs, start=(half == 0), stop=(half == 1))
                    return nc.tensor.matmul(ps[0:cap, b, :], xs[:, kk, 0:cap], rhs, start=(kk == 0), stop=(kk == KT - 1))

                def x_transposes(i):
                    e, n, cap = passes[i]
                    pe.wait_ge(*ga[i % 3].at(16 * (i // 3 + 1)))
                    if i >= 2:
                        pe.wait_ge(*yd.at(i - 1))
                    for k in range(KT):
                        ins = nc.tensor.transpose(ps[:, 6 + k // 4, (k % 4) * P:(k % 4) * P + cap], xe[0:cap, i % 3, k * P:(k + 1) * P],
                                                  g.ident[0:cap, 0:cap])
                    ins.then_inc(*xtr.up())
                x_transposes(0)
                for i, (e, n, cap) in enumerate(passes):
                    pe.wait_ge(*xte.at(i + 1))
                    if i >= 1:
                        pe.wait_ge(*hd.at(2 * i))
                    for c in range(2):
                        for m in range(2):
                            for half in range(2):
                                s, v = slot(e, m, half)
                                pe.wait_ge(*w_in[s].at(v))
                                for k in range(4):
                                    ins = product(n, cap, half, k, 2 * m + c, xT, w[:, s, k, c * 512:(c + 1) * 512])
                            ins.then_inc(*(gm, um)[m].up())
                    if i + 1 < NP:
                        x_transposes(i + 1)
                    if n == 1:
                        pe.wait_ge(*hd.at(2 * i + 2))
                        for src, b in ((pg, 4), (pu, 5)):
                            for k in range(KT):
                                ins = nc.tensor.matmul(ps[:, b, k * CAPC:(k + 1) * CAPC], src[:, k * P:(k + 1) * P], g.sel[:],
                                                       start=True, stop=True)
                    for k in range(KT if n == 0 else 0):
                        if k % 4 == 0:
                            pe.wait_ge(*hd.at(2 * i + 1 + k // 4))
                        ins = nc.tensor.transpose(ps[:, 4 + k // 4, (k % 4) * P:(k % 4) * P + cap], hid[0:cap, k * P:(k + 1) * P],
                                                  g.ident[0:cap, 0:cap])
                    ins.then_inc(*htr.up())
                    pe.wait_ge(*hte.at(i + 1))
                    if i + 1 < NP:
                        pe.wait_ge(*xte.at(i + 2))
                    for half in range(2):
                        s, v = slot(e, 2, half)
                        pe.wait_ge(*w_in[s].at(v))
                        for c in range(2):
                            for k in range(4):
                                ins = product(n, cap, half, k, 6 + c, hT2, w[:, s, k, c * 512:(c + 1) * 512])
                    if n == 1:
                        ins.then_inc(*dpm.up())
                        pe.wait_ge(*pdd.at(e + 1))
                        for c in range(2):
                            ins = nc.tensor.matmul(ps[0:CAPC, 6 + c, :], g.sel[:], pg[:, c * 512:(c + 1) * 512], start=True, stop=True)
                    ins.then_inc(*dm.up())

            def x_copy(act, i):
                cap = passes[i][2]
                act.wait_ge(*xtr.at(i + 1))
                if i:
                    act.wait_ge(*um.at(2 * i))
                nc.scalar.copy(xT[:, :, 0:cap], bank(ps, 6, D).rearrange("p (k n) -> p k n", k=KT)[:, :, 0:cap]).then_inc(*xte.up())

            @block.scalar
            def _(act):
                for i, (e, n, cap) in enumerate(passes):
                    if i == 0:
                        x_copy(act, 0)
                    if i >= 1:
                        act.wait_ge(*htr.at(i))
                    for c in range(2):
                        act.wait_ge(*gm.at(2 * i + c + 1))
                        dst, fn = ((hid, ACT.Silu), (pg, ACT.Copy))[n]
                        nc.scalar.activation(dst[:, c * 512:(c + 1) * 512], ps[:, c], fn).then_inc(*si.up())
                    if i + 1 < NP:
                        x_copy(act, i + 1)
                    if n == 0:
                        act.wait_ge(*htr.at(i + 1))
                        nc.scalar.copy(hT2[:, :, 0:cap], bank(ps, 4, D).rearrange("p (k n) -> p k n", k=KT)[:, :, 0:cap]).then_inc(*hte.up())
                    else:
                        act.wait_ge(*htr.at(i + 1))
                        nc.scalar.activation(gs[:].rearrange("p k n -> p (k n)"), ps[:, 4, 0:KT * CAPC], ACT.Silu).then_inc(*gsd.up())
                    if n == 1:
                        act.wait_ge(*dpm.at(e + 1))
                        nc.scalar.copy(pg[:], bank(ps, 6, D)).then_inc(*pdd.up())

            @block.vector
            def _(dve):
                for i, (e, n, cap) in enumerate(passes):
                    for c in range(2):
                        dve.wait_ge(*um.at(2 * i + c + 1))
                        dve.wait_ge(*si.at(2 * i + c + 1))
                        h = slice(c * 512, (c + 1) * 512)
                        if n == 0:
                            nc.vector.tensor_tensor(hid[:, h], hid[:, h], ps[:, 2 + c], ALU.mult).then_inc(*hd.up())
                        else:
                            nc.vector.tensor_copy(pu[:, h], ps[:, 2 + c]).then_inc(*hd.up())
                    if n == 1:
                        dve.wait_ge(*gsd.at(e + 1))
                        nc.vector.tensor_tensor(hT2[:, :, 0:CAPC], gs[:], ps[:, 5, 0:KT * CAPC].rearrange("p (k n) -> p k n", k=KT),
                                                ALU.mult).then_inc(*hte.up())
                    dve.wait_ge(*dm.at(i + 1))
                    if i >= 2:
                        dve.wait_ge(*sc.at(16 * (i - 1)))
                    nc.vector.tensor_scalar(ye[0:cap, i % 2], bank(ps, 6, D)[0:cap], g.gate[0:cap, n, e:e + 1], None, ALU.mult).then_inc(*yd.up())
        sg.settle()


def stage_residual(nc, g, I):
    sg, l = g.sg, DEPTH - 1
    tiles = list(range(NCT, NT))
    with ExitStack() as cx:
        sb = Bufs(nc, cx, f"f{l}")
        rows = sb("rows", [P, D])
        xb = sb("xb", [P, 3, D])
        ab = sb("ab", [P, 3, D])
        small, x_in, done, st, chain = sg("small_in"), [sg(f"w_slot{i}") for i in range(3)], sg("normed"), [sg(f"out_slot{i}") for i in range(3)], sg("dve_chain")
        with nc.Block() as block:
            @block.sync
            def _(sp):
                sp.dma_start(rows[:], row(g.mod[l, 0, 5 * D:6 * D])).then_inc(*small.up(16))
                for n, t in enumerate(tiles):
                    ts = slice(t * P, (t + 1) * P)
                    if n >= 3:
                        sp.wait_ge(*st[n % 3].at(16 * (n // 3)))
                    sp.dma_start(xb[:, n % 3], g.x[ts]).then_inc(*x_in[n % 3].up(16))
                    sp.dma_start(ab[:, n % 3], g.acc[ts]).then_inc(*x_in[n % 3].up(16))

            @block.vector
            def _(dve):
                link = linker(dve, chain)
                dve.wait_ge(*small.at(16))
                for n, t in enumerate(tiles):
                    dve.wait_ge(*x_in[n % 3].at(32 * (n // 3 + 1)))
                    link(nc.vector.tensor_tensor(ab[:, n % 3], ab[:, n % 3], rows[:], ALU.mult))
                    nc.vector.tensor_tensor(ab[:, n % 3], ab[:, n % 3], xb[:, n % 3], ALU.add).then_inc(*done.up())

            @block.gpsimd
            def _(pool):
                for n, t in enumerate(tiles):
                    pool.wait_ge(*done.at(n + 1))
                    pool.dma_start(g.out[0, (t - NCT) * P:(t - NCT + 1) * P], ab[:, n % 3]).then_inc(*st[n % 3].up(16))
                for s in st:
                    pool.wait_ge(s.sem, s.made)
        sg.settle()


class Core:
    pass


def build(nc, I, C, out, dbg=None):
    g = Core()
    g.nc = nc
    kind = "Internal"
    def dram(name, shape):
        if dbg is not None and name in dbg:
            return nc.dram_tensor("out_dbg_" + name, shape, F32, kind="ExternalOutput").ap()
        return nc.dram_tensor(name, shape, F32, kind=kind).ap()
    g.mod = dram("mod_rows", [DEPTH, 2, 6 * D])
    g.x = dram("x_rows", [T, D])
    g.h2 = dram("h2_rows", [T, D])
    g.acc = dram("acc_rows", [T, D])
    g.zt = dram("z_rows", [T, W_MLA + W_RET])
    g.C, g.out = C, out

    def x_rows(I, l, t):
        if l == 0:
            return I["ctx"][0, t * P:(t + 1) * P] if t < NCT else I["x"][0, (t - NCT) * P:(t - NCT + 1) * P]
        return g.x[t * P:(t + 1) * P]
    g.x_rows = x_rows
    with ExitStack() as ctx:
        g.sg = Signals(ctx, nc)
        fixed = Bufs(nc, ctx, "all")
        g.ps = ctx.enter_context(nc.psum_tensor("ps", [P, 8, 512], F32))
        tabs = fixed("tabs", [P, 3, P])
        g.ident, g.ones, g.blk = tabs[:, 0], tabs[:, 1], tabs[:, 2]
        g.aff = fixed("aff", [NE, T])
        g.tok = fixed("tok", [P, 2, NE], I32)
        g.gate = fixed("gate", [P, 2, NE])
        g.mhalf = fixed("mhalf", [P, 8])
        g.sel = fixed("sel", [P, 32])
        g.vr, g.rq = g.sg("var_ready"), g.sg("rsqrt_done")
        small = g.sg("small_in")
        with nc.Block() as block:
            @block.vector
            def _(dve):
                nc.vector.memset(g.mhalf[:], -0.5)

            @block.sync
            def _(sp):
                for n, name in enumerate(("ident", "ones", "blk")):
                    sp.dma_start(tabs[:, n], C[name]).then_inc(*small.up(16))
                sp.dma_start(g.sel[:], C["sel"]).then_inc(*small.up(16))
                sp.wait_ge(*small.at(64))
        g.sg.settle()
        stage_modulation(nc, g, I)
        for l in range(DEPTH):
            need_ctx = l < DEPTH - 1
            with ExitStack() as lay:
                g.yT = lay.enter_context(nc.sbuf_tensor(f"yT{l}", [P, KT, T], F32))
                with ExitStack() as mix:
                    M = mix.enter_context(nc.sbuf_tensor(f"M{l}", [P, 8, T], F32))
                    with ExitStack() as norm:
                        g.hT = norm.enter_context(nc.sbuf_tensor(f"hT{l}", [P, KT, T], F32))
                        stage_norm1(nc, g, I, l)
                        stage_project(nc, g, I, l, M)
                    with ExitStack() as mla:
                        sb = Bufs(nc, mla, f"mla{l}")
                        S = dict(QT=sb("QT", [P, H, T]), KT=sb("KT", [P, H, T]), V=sb("V", [P, NT, H, 65]))
                        stage_mla_prep(nc, g, I, l, S)
                        stage_mla_attend(nc, g, I, l, S, need_ctx)
                    sb = Bufs(nc, mix, f"rw{l}")
                    R = dict(M=M, w0=sb("w0", [P, 2, 2]), a0=sb("a0", [P, 2, 2]), wa2=sb("wa2", [P, 2, GW]),
                             kk=sb("kk", [P, 2]), ka=sb("ka", [P, 2]), oka=sb("oka", [P, 2]), rk=sb("rk", [P, 2]), gln=sb("gln", [P, 2]),
                             g2=sb("g2", [P, GW]),
                             tiny=sb("tiny", [P, 1]))
                    stage_retention(nc, g, I, l, R, need_ctx)
                    R.update(masks=sb("masks", [P, 2, 4, P]), nlev=sb("nlev", [P, 2, LEVELS, P]), KR=[sb(f"KR{d}", [P, 2, T]) for d in range(2)], BK=[sb(f"BK{d}", [P, 2, T]) for d in range(2)],
                             ET=[sb(f"ET{d}", [P, 2, T // CH]) for d in range(2)], KS=sb("KS", [P, T]))
                    for p in range(2):
                        with ExitStack() as pr:
                            tb = Bufs(nc, pr, f"rp{l}{p}")
                            R.update((n, tb(n, [P, T])) for n in ("KK", "reset"))
                            R.update((n, [tb(f"{n}{d}", [P, T]) for d in range(2)]) for n in ("A", "SG", "G", "GX", "E"))
                            stage_rwkv_prep(nc, g, I, l, R, p)
                        stage_rwkv_scan(nc, g, I, l, R, p, need_ctx)
                        stage_rwkv_out(nc, g, I, l, R, p, need_ctx)
                stage_out(nc, g, I, l, need_ctx)
            with nc.sbuf_tensor(f"moe_w{l}", [P, MOE_RW, 4, 1024], F32) as g.moe_w:
                stage_topk(nc, g, I, l, need_ctx)
                stage_moe(nc, g, I, l, need_ctx)
        stage_residual(nc, g, I)


_INS = ['x', 'c', 'ctx', 'c_ctx', 'w_ada', 'b_ada', 'g_norm1', 'g_norm2', 'w_in', 'w_out', 'conv_w', 'g_out_conv', 'g_kv_norm',
        'w_uk', 'w_uv', 'g_q_norm', 'g_k_norm', 'g_out_mla', 'rwkv_mu', 'rwkv_w0', 'rwkv_w2', 'rwkv_a0', 'rwkv_a2', 'rwkv_g2',
        'rwkv_k_k', 'rwkv_k_a', 'rwkv_r_k', 'g_ln_x', 'g_ret_norm', 'w_router', 'b_router', 'w_gate', 'w_up', 'w_down']


def kernel(**inputs):
    import numpy as _np
    import concourse.bacc as _bacc
    from concourse import mybir as _mybir
    from concourse.bass_utils import run_bass_kernel_spmd as _run

    nc = _bacc.Bacc("TRN2", target_bir_lowering=False, num_devices=1)
    arrays, I, C = {}, {}, {}
    for name in _INS:
        a = _np.ascontiguousarray(inputs[name])
        arrays[f"in_{name}_dram"] = a
        I[name] = nc.dram_tensor(f"in_{name}_dram", a.shape, _mybir.dt.from_np(a.dtype), kind="ExternalInput").ap()
    for name, a in constants().items():
        arrays[f"const_{name}_dram"] = a
        C[name] = nc.dram_tensor(f"const_{name}_dram", a.shape, _mybir.dt.from_np(a.dtype), kind="ExternalInput").ap()
    out = nc.dram_tensor("out_0_dram", (1, SEQ, D), F32, kind="ExternalOutput").ap()
    build(nc, I, C, out)
    r = _run(nc, [arrays], core_ids=[0])
    return r.results[0]["out_0_dram"]
```
